# Optimizing a Trainium2 kernel written in Bass

```python
import math
import jax
import jax.numpy as jnp
from jax import lax
import numpy as np

D_MODEL = 1024
BATCH = 1
SEQ = 256
DEPTH = 2

N_MIXERS = 2
N_EVEN_LAYERS = (DEPTH + 1) // 2
N_ODD_LAYERS = DEPTH // 2

MLSTM_HEADS = 4
MLSTM_DV = D_MODEL // MLSTM_HEADS
MLSTM_DQK = MLSTM_DV // 2
MLSTM_QK_WIDTH = 2 * MLSTM_HEADS * MLSTM_DQK
MLSTM_V_WIDTH = MLSTM_HEADS * MLSTM_DV
MLSTM_PROJ = MLSTM_QK_WIDTH + 2 * MLSTM_V_WIDTH + 2 * MLSTM_HEADS
MLSTM_CHUNK = 64
CONV_WIDTH = 4
FGATE_BIAS_LO = 3.0
FGATE_BIAS_HI = 6.0

DIFF_HEADS = 8
DIFF_HEAD_DIM = D_MODEL // (2 * DIFF_HEADS)
DIFF_V_DIM = 2 * DIFF_HEAD_DIM
DIFF_QK_WIDTH = 2 * DIFF_HEADS * DIFF_HEAD_DIM
DIFF_PROJ = 2 * DIFF_QK_WIDTH + DIFF_HEADS * DIFF_V_DIM
Q_BLOCK = 128

NUM_BUCKETS = 32
REL_MAX_DISTANCE = 128

D_FF = 3584
N_EXPERTS = 8
TOP_K = 2
MOE_BLOCK = 256

NORM_EPS = 1e-6
SUBLN_EPS = 1e-5

kernel_name = 'mlstm_diffattn_moe_hybrid'

def rms_norm(x, w, eps=NORM_EPS):
    xf = x.astype(jnp.float32)
    y = xf * lax.rsqrt(jnp.mean(xf * xf, axis=-1, keepdims=True) + eps)
    return (y * w.astype(jnp.float32)).astype(x.dtype)

def swiglu(h, w_gate, w_up, w_down):
    return (jax.nn.silu(h @ w_gate) * (h @ w_up)) @ w_down

def causal_depthwise_conv(x, w, b):
    c = x.shape[-1]
    y = lax.conv_general_dilated(
        x, w.reshape(CONV_WIDTH, 1, c).astype(x.dtype), window_strides=(1,),
        padding=[(CONV_WIDTH - 1, 0)], dimension_numbers=('NWC', 'WIO', 'NWC'),
        feature_group_count=c)
    return y + b.astype(x.dtype)

def _mlstm_chunk_step(carry, inp):
    c_mem, n_mem, m_prev = carry
    q, k, v, log_i, log_f = inp
    L = q.shape[2]
    b = jnp.cumsum(log_f, axis=-1)
    causal = jnp.tril(jnp.ones((L, L), dtype=bool))
    log_d = jnp.where(causal, b[..., :, None] - b[..., None, :] + log_i[..., None, :], -jnp.inf)
    log_inter = b + m_prev[..., None]
    m_t = jnp.maximum(log_inter, jnp.max(log_d, axis=-1))
    s = jnp.einsum('bhtd,bhsd->bhts', q, k) * jnp.exp(log_d - m_t[..., None])
    inter = jnp.exp(log_inter - m_t)
    num = jnp.einsum('bhts,bhsv->bhtv', s, v) + inter[..., None] * jnp.einsum('bhtd,bhdv->bhtv', q, c_mem)
    den = jnp.sum(s, axis=-1) + inter * jnp.einsum('bhtd,bhd->bht', q, n_mem)
    h = num / jnp.maximum(jnp.abs(den), jnp.exp(-m_t))[..., None]
    g = b[..., -1]
    log_w = g[..., None] - b + log_i
    m_new = jnp.maximum(g + m_prev, jnp.max(log_w, axis=-1))
    kw = k * jnp.exp(log_w - m_new[..., None])[..., None]
    decay = jnp.exp(g + m_prev - m_new)
    c_new = decay[..., None, None] * c_mem + jnp.einsum('bhsd,bhsv->bhdv', kw, v)
    n_new = decay[..., None] * n_mem + jnp.sum(kw, axis=2)
    return (c_new, n_new, m_new), h

def mlstm_chunkwise(q, k, v, log_i, log_f):
    B, S, H, DK = q.shape
    DV = v.shape[-1]
    L = MLSTM_CHUNK
    nc = S // L

    def to_chunks(t):
        return t.reshape(B, nc, L, H, t.shape[-1]).transpose(1, 0, 3, 2, 4)

    def gate_chunks(t):
        return t.reshape(B, nc, L, H).transpose(1, 0, 3, 2)

    init = (jnp.zeros((B, H, DK, DV), jnp.float32), jnp.zeros((B, H, DK), jnp.float32),
            jnp.zeros((B, H), jnp.float32))
    _, hs = lax.scan(_mlstm_chunk_step, init,
                     (to_chunks(q), to_chunks(k), to_chunks(v), gate_chunks(log_i), gate_chunks(log_f)))
    return hs.transpose(1, 0, 3, 2, 4).reshape(B, S, H, DV)

def mlstm_mixer(h, w_in, conv_w, conv_b, b_igate, b_fgate, head_norm, w_out):
    B, S, _ = h.shape
    proj = h @ w_in
    o1 = MLSTM_QK_WIDTH
    o2 = o1 + MLSTM_V_WIDTH
    o3 = o2 + MLSTM_V_WIDTH
    o4 = o3 + MLSTM_HEADS
    qk = jax.nn.silu(causal_depthwise_conv(proj[..., :o1], conv_w, conv_b))
    q = qk[..., :o1 // 2].reshape(B, S, MLSTM_HEADS, MLSTM_DQK).astype(jnp.float32)
    k = qk[..., o1 // 2:].reshape(B, S, MLSTM_HEADS, MLSTM_DQK).astype(jnp.float32) * (MLSTM_DQK ** -0.5)
    v = proj[..., o1:o2].reshape(B, S, MLSTM_HEADS, MLSTM_DV).astype(jnp.float32)
    o_gate = jax.nn.sigmoid(proj[..., o2:o3])
    log_i = (proj[..., o3:o4] + b_igate).astype(jnp.float32)
    log_f = jax.nn.log_sigmoid((proj[..., o4:] + b_fgate).astype(jnp.float32))
    hh = mlstm_chunkwise(q, k, v, log_i, log_f)
    hh = rms_norm(hh, head_norm.reshape(MLSTM_HEADS, MLSTM_DV)).astype(h.dtype)
    return (o_gate * hh.reshape(B, S, MLSTM_V_WIDTH)) @ w_out

def t5_causal_bucket(rel):
    n = jnp.maximum(rel, 0)
    max_exact = NUM_BUCKETS // 2
    nf = jnp.maximum(n, 1).astype(jnp.float32)
    large = max_exact + (jnp.log(nf / max_exact) / math.log(REL_MAX_DISTANCE / max_exact)
                         * (NUM_BUCKETS - max_exact)).astype(jnp.int32)
    large = jnp.minimum(large, NUM_BUCKETS - 1)
    return jnp.where(n < max_exact, n, large)

def diff_attention(h, w_in, lam_q1, lam_k1, lam_q2, lam_k2, subln, w_out, rel_table, layer_idx):
    B, S, _ = h.shape
    proj = h @ w_in
    q = proj[..., :DIFF_QK_WIDTH].reshape(B, S, 2 * DIFF_HEADS, DIFF_HEAD_DIM).transpose(0, 2, 1, 3)
    k = proj[..., DIFF_QK_WIDTH:2 * DIFF_QK_WIDTH].reshape(B, S, 2 * DIFF_HEADS, DIFF_HEAD_DIM).transpose(0, 2, 1, 3)
    v = proj[..., 2 * DIFF_QK_WIDTH:].reshape(B, S, DIFF_HEADS, DIFF_V_DIM).transpose(0, 2, 1, 3)
    lam_init = 0.8 - 0.6 * math.exp(-0.3 * layer_idx)
    lam = (jnp.exp(jnp.sum(lam_q1.astype(jnp.float32) * lam_k1.astype(jnp.float32)))
           - jnp.exp(jnp.sum(lam_q2.astype(jnp.float32) * lam_k2.astype(jnp.float32))) + lam_init)
    scale = DIFF_HEAD_DIM ** -0.5
    outs = []
    for j in range(S // Q_BLOCK):
        q0 = j * Q_BLOCK
        kv_len = q0 + Q_BLOCK
        qpos = q0 + jnp.arange(Q_BLOCK, dtype=jnp.int32)
        kpos = jnp.arange(kv_len, dtype=jnp.int32)
        rel = qpos[:, None] - kpos[None, :]
        bias = rel_table[t5_causal_bucket(rel)].astype(jnp.float32).transpose(2, 0, 1)
        logits = jnp.einsum('bmqd,bmkd->bmqk', q[:, :, q0:kv_len], k[:, :, :kv_len]).astype(jnp.float32) * scale + bias
        logits = jnp.where(rel[None, None] >= 0, logits, -jnp.inf)
        p = jax.nn.softmax(logits, axis=-1).reshape(B, DIFF_HEADS, 2, Q_BLOCK, kv_len)
        a = p[:, :, 0] - lam * p[:, :, 1]
        outs.append(jnp.einsum('bhqk,bhkv->bhqv', a.astype(v.dtype), v[:, :, :kv_len]))
    o = jnp.concatenate(outs, axis=2)
    o = rms_norm(o, subln, SUBLN_EPS) * (1.0 - lam_init)
    return o.transpose(0, 2, 1, 3).reshape(B, S, DIFF_HEADS * DIFF_V_DIM) @ w_out

def moe_swiglu(h, w_router, b_router, w_gate, w_up, w_down):
    B, S, D = h.shape
    xt = h.reshape(B * S, D)
    n_assign = B * S * TOP_K
    logits = (xt @ w_router).astype(jnp.float32) + b_router.astype(jnp.float32)
    top_logit, top_expert = lax.top_k(logits, TOP_K)
    gates = jax.nn.softmax(top_logit, axis=-1)
    expert_flat = top_expert.reshape(-1).astype(jnp.int32)
    gate_flat = gates.reshape(-1)
    order = jnp.argsort(expert_flat * n_assign + jnp.arange(n_assign, dtype=jnp.int32))
    expert_sorted = expert_flat[order]
    token_sorted = (order // TOP_K).astype(jnp.int32)
    counts = jnp.bincount(expert_flat, length=N_EXPERTS)
    padded = (counts + MOE_BLOCK - 1) // MOE_BLOCK * MOE_BLOCK
    pad_end = jnp.cumsum(padded)
    pad_start = pad_end - padded
    raw_start = jnp.cumsum(counts) - counts
    slot = pad_start[expert_sorted] + jnp.arange(n_assign, dtype=jnp.int32) - raw_start[expert_sorted]
    n_blocks = -(-n_assign // MOE_BLOCK) + N_EXPERTS
    n_slots = n_blocks * MOE_BLOCK
    slot_token = jnp.zeros((n_slots,), jnp.int32).at[slot].set(token_sorted)
    slot_gate = jnp.zeros((n_slots,), jnp.float32).at[slot].set(gate_flat[order])
    block_expert = jnp.minimum(
        jnp.searchsorted(pad_end, jnp.arange(n_blocks, dtype=pad_end.dtype) * MOE_BLOCK, side='right'),
        N_EXPERTS - 1)
    xs = xt[slot_token].reshape(n_blocks, MOE_BLOCK, D)

    def expert_block(args):
        xb, e = args
        return swiglu(xb, w_gate[e], w_up[e], w_down[e])

    ys = lax.map(expert_block, (xs, block_expert)).reshape(n_slots, D)
    out = jnp.zeros_like(xt).at[slot_token].add(ys * slot_gate[:, None].astype(ys.dtype))
    return out.reshape(B, S, D)

def setup_inputs(seed: int = 0) -> dict:
    key = jax.random.key(seed)
    ks = iter(jax.random.split(key, 48))

    def nrm(shape, scale):
        return jax.random.normal(next(ks), shape, jnp.float32) * scale

    na, nb, d = N_EVEN_LAYERS, N_ODD_LAYERS, D_MODEL
    return {
        'x': nrm((BATCH, SEQ, d), 1.0),
        'rel_bias_table': nrm((NUM_BUCKETS, 2 * DIFF_HEADS), 0.5),
        'mlstm_norm': 1.0 + nrm((na, d), 0.05),
        'mlstm_w_in': nrm((na, d, MLSTM_PROJ), d ** -0.5),
        'mlstm_conv_w': nrm((na, CONV_WIDTH, MLSTM_QK_WIDTH), CONV_WIDTH ** -0.5),
        'mlstm_conv_b': nrm((na, MLSTM_QK_WIDTH), 0.02),
        'mlstm_b_igate': nrm((na, MLSTM_HEADS), 0.1),
        'mlstm_b_fgate': jnp.linspace(FGATE_BIAS_LO, FGATE_BIAS_HI, MLSTM_HEADS)[None, :] + nrm((na, MLSTM_HEADS), 0.1),
        'mlstm_head_norm': 1.0 + nrm((na, MLSTM_V_WIDTH), 0.05),
        'mlstm_w_out': nrm((na, MLSTM_V_WIDTH, d), MLSTM_V_WIDTH ** -0.5),
        'diff_norm': 1.0 + nrm((nb, d), 0.05),
        'diff_w_in': nrm((nb, d, DIFF_PROJ), d ** -0.5),
        'diff_lambda_q1': nrm((nb, DIFF_HEAD_DIM), 0.1),
        'diff_lambda_k1': nrm((nb, DIFF_HEAD_DIM), 0.1),
        'diff_lambda_q2': nrm((nb, DIFF_HEAD_DIM), 0.1),
        'diff_lambda_k2': nrm((nb, DIFF_HEAD_DIM), 0.1),
        'diff_subln': 1.0 + nrm((nb, DIFF_V_DIM), 0.05),
        'diff_w_out': nrm((nb, DIFF_HEADS * DIFF_V_DIM, d), (DIFF_HEADS * DIFF_V_DIM) ** -0.5),
        'ffn_norm': 1.0 + nrm((na, d), 0.05),
        'ffn_w_gate': nrm((na, d, D_FF), d ** -0.5),
        'ffn_w_up': nrm((na, d, D_FF), d ** -0.5),
        'ffn_w_down': nrm((na, D_FF, d), D_FF ** -0.5),
        'moe_norm': 1.0 + nrm((nb, d), 0.05),
        'moe_w_router': nrm((nb, d, N_EXPERTS), d ** -0.5),
        'moe_b_router': nrm((nb, N_EXPERTS), 0.01),
        'moe_w_gate': nrm((nb, N_EXPERTS, d, D_FF), d ** -0.5),
        'moe_w_up': nrm((nb, N_EXPERTS, d, D_FF), d ** -0.5),
        'moe_w_down': nrm((nb, N_EXPERTS, D_FF, d), D_FF ** -0.5),
        'final_norm': 1.0 + nrm((d,), 0.05),
    }

def reference(x, rel_bias_table,
              mlstm_norm, mlstm_w_in, mlstm_conv_w, mlstm_conv_b, mlstm_b_igate, mlstm_b_fgate,
              mlstm_head_norm, mlstm_w_out,
              diff_norm, diff_w_in, diff_lambda_q1, diff_lambda_k1, diff_lambda_q2, diff_lambda_k2,
              diff_subln, diff_w_out,
              ffn_norm, ffn_w_gate, ffn_w_up, ffn_w_down,
              moe_norm, moe_w_router, moe_b_router, moe_w_gate, moe_w_up, moe_w_down,
              final_norm):
    for i in range(DEPTH):
        s = i // 2
        if i % N_MIXERS == 0:
            x = x + mlstm_mixer(rms_norm(x, mlstm_norm[s]), mlstm_w_in[s], mlstm_conv_w[s], mlstm_conv_b[s],
                                mlstm_b_igate[s], mlstm_b_fgate[s], mlstm_head_norm[s], mlstm_w_out[s])
            x = x + swiglu(rms_norm(x, ffn_norm[s]), ffn_w_gate[s], ffn_w_up[s], ffn_w_down[s])
        else:
            x = x + diff_attention(rms_norm(x, diff_norm[s]), diff_w_in[s], diff_lambda_q1[s], diff_lambda_k1[s],
                                   diff_lambda_q2[s], diff_lambda_k2[s], diff_subln[s], diff_w_out[s],
                                   rel_bias_table, i)
            x = x + moe_swiglu(rms_norm(x, moe_norm[s]), moe_w_router[s], moe_b_router[s],
                               moe_w_gate[s], moe_w_up[s], moe_w_down[s])
    return rms_norm(x, final_norm)


_drawn_inputs = setup_inputs


def setup_inputs(seed=0):
    import zlib

    import numpy as np

    out = dict(_drawn_inputs(seed))
    spreads = {}
    factors = {'mlstm_b_igate': 64.0,
     'diff_lambda_q2': 8.829,
     'mlstm_conv_b': 3.043,
     'moe_b_router': 3.511}
    for name, (base, spread) in spreads.items():
        noise = np.random.default_rng([zlib.crc32(name.encode()), seed]).standard_normal(out[name].shape)
        drawn = base * np.exp(spread * noise) if base else spread * noise
        out[name] = jnp.asarray(drawn.astype(out[name].dtype))
    for name, factor in factors.items():
        out[name] = (out[name] * factor).astype(out[name].dtype)
    return out
```

```python
import math
from contextlib import ExitStack

import concourse.bass as bass
from concourse import mybir

F32 = mybir.dt.float32
F32R = mybir.dt.float32r
I32 = mybir.dt.int32
U32 = mybir.dt.uint32
ALU = mybir.AluOpType
ACT = mybir.ActivationFunctionType
AX_X = mybir.AxisListType.X

P = 128
T = 256
NT = T // P
D = 1024
KC = D // P
NW = 512
F_FF = 3584
GROUPS = F_FF // NW
NE = 8
HALF = 2048
RAW_SLOTS = 6
SPLIT_SLOTS = 3
OVERFLOW_PASSES = 3
PASSES = NE + OVERFLOW_PASSES

ML_H, ML_DK, ML_DV = 4, 128, 256
ML_DVX = ML_DV + 1
ML_SCALE = ML_DK ** -0.5
CONV_W = 4
ROW = 384

DH, DHD, DDV = 8, 64, 128
DMAPS = 2 * DH
DSCALE = DHD ** -0.5
LAYER = 1
LAM_INIT = 0.8 - 0.6 * math.exp(-0.3 * LAYER)
BUCKETS, MAX_DIST = 32, 128
BIAS_W = 384
NEG = -1.0e30

EPS, SUB_EPS = 1e-6, 1e-5

HALF_Q, HALF_K, HALF_V, HALF_O, HALF_MOUT = 0, 2, 4, 8, 12
HALF_FFN = 16
HALF_DQ = HALF_FFN + 6 * GROUPS
HALF_DK, HALF_DVV, HALF_DOUT = HALF_DQ + 4, HALF_DQ + 8, HALF_DQ + 12
HALF_MOE = HALF_DQ + 16

C_MNORM, C_HNORM, C_FNORM, C_DNORM, C_CONVB, C_CONVW, C_SUB = 0, 8, 16, 24, 32, 40, 72
PRM = 73

S_RSTD, S_MS, S_SQ = 0, 2, 4


def bucket_of(n):
    half = BUCKETS // 2
    if n < half:
        return n
    return min(half + int(math.log(n / half) / math.log(MAX_DIST / half) * (BUCKETS - half) + 1e-9), BUCKETS - 1)


def bucket_hot():
    rows = [[0.0] * BIAS_W for _ in range(BUCKETS + 1)]
    for c in range(BIAS_W):
        n = T - 1 - c
        rows[bucket_of(n) if n >= 0 else BUCKETS][c] = 1.0
    return rows


def bass_hybrid(nc, A, out):
    ctx = ExitStack()
    with ctx:
        scope = [ctx]

        def sb(name, shape, dt=F32):
            return scope[-1].enter_context(nc.sbuf_tensor(name, shape, dt))

        def sem(name):
            return ctx.enter_context(nc.semaphore(name))

        x = sb("x", [P, NT, D])
        xs = sb("xs", [P, NT, D])
        xt_hi = sb("xt_hi", [P, KC, T], F32R)
        xt_lo = sb("xt_lo", [P, KC, T], F32R)
        raw = sb("raw", [P, RAW_SLOTS, HALF])
        w_hi = sb("w_hi", [P, SPLIT_SLOTS, HALF], F32R)
        w_lo = sb("w_lo", [P, SPLIT_SLOTS, HALF], F32R)
        gate_act = sb("gate_act", [P, NT, NW])
        hid = sb("hid", [P, NT, NW])
        hid_t_hi = sb("hid_t_hi", [P, 4, T], F32R)
        hid_t_lo = sb("hid_t_lo", [P, 4, T], F32R)
        ident = sb("ident", [P, P])
        ones = sb("ones", [P, P])
        prm = sb("prm", [PRM, P])
        col = sb("col", [P, PRM])
        small = sb("small", [P, 8])
        w8 = sb("w8", [P, 2, KC, 8])
        w8_hi = sb("w8_hi", [P, 2, KC, 8], F32R)
        w8_lo = sb("w8_lo", [P, 2, KC, 8], F32R)
        b8 = sb("b8", [P, 2, 8])
        lamv = sb("lamv", [P, 4, DHD])
        lamp = sb("lamp", [P, 2, DHD])
        lam = sb("lam", [P, 8])
        sub_w = sb("sub_w", [P, 1])
        anti = sb("anti", [P, P])

        scope.append(ExitStack())
        qk = sb("qk", [P, 2 * ML_H, T])
        vx = sb("vx", [P, NT, ML_H, ML_DVX])
        sig_o = sb("sig_o", [P, NT, D])
        dec = sb("dec", [P, ML_H, ROW])
        prob = sb("prob", [P, ML_H, ROW])
        gtok = sb("gtok", [P, NT, 8])
        grow = sb("grow", [ML_H, 2 * T])
        g_abs = sb("g_abs", [ML_H, T])
        g_exp = sb("g_exp", [ML_H, T])
        g_ln = sb("g_ln", [ML_H, T])
        g_logf = sb("g_logf", [ML_H, T])
        g_cum = sb("g_cum", [ML_H, T])
        g_a = sb("g_a", [ML_H, T])
        g_max = sb("g_max", [ML_H, T])
        g_m = sb("g_m", [ML_H, T])
        g_em = sb("g_em", [ML_H, T])
        zrow = sb("zrow", [ML_H, T])
        headsel = sb("headsel", [ML_H, ML_H, P])
        acol = sb("acol", [P, NT, ML_H])
        em = sb("em", [P, ML_H * NT])
        mn = sb("mn", [P, 8, 8])
        scope.pop().close()

        scope.append(ExitStack())
        qz = sb("qz", [P, DH, 2, T])
        kt = sb("kt", [P, DH, T])
        vv = sb("vv", [P, NT, D])
        bias = sb("bias", [P, DMAPS, T])
        ex = gate_act[:, :, :].rearrange("p i (m k) -> p i m k", m=2)
        aw = sb("aw", [P, 2, T])
        awt = sb("awt", [P, 2, T])
        nmx = sb("nmx", [P, 3, 2])
        sm = sb("sm", [P, 2, 8])
        osq = [gate_act[:, 0, :], gate_act[:, 1, :], hid[:, 0, :], hid[:, 1, :]]
        oms = sb("oms", [P, 4, 2 * DH])
        scope.pop().close()

        scope.append(ExitStack())
        xn_hi = sb("xn_hi", [P, NT, D], F32R)
        xn_lo = sb("xn_lo", [P, NT, D], F32R)
        moe_w = sb("moe_w", [P, D])
        fin_w = sb("fin_w", [P, D])
        y_hi = sb("y_hi", [P, D], F32R)
        y_lo = sb("y_lo", [P, D], F32R)
        pick = sb("pick", [P, NT, P], F32R)
        pick_t = sb("pick_t", [P, T], F32R)
        slots_i = sb("slots_i", [P, P], I32)
        slots = sb("slots", [P, P])
        before = sb("before", [P, P])
        lg = sb("lg", [P, NT, NE])
        top = sb("top", [P, NT, 8])
        topi = sb("topi", [P, NT, 8], U32)
        topf = sb("topf", [P, NT, 8])
        m12 = sb("m12", [P, NT, 2, NE])
        gsc = sb("gsc", [P, NT, 8])
        rt = sb("rt", [P, 2, NT, NE])
        pos = sb("pos", [P, NT, NE])
        ovf = sb("ovf", [P, 8, NE])
        ovs = sb("ovs", [P, 16])
        plan = sb("plan", [P, PASSES, 6])
        cur = sb("cur", [P, 6])
        gslot = sb("gslot", [P, 1])
        route = sb("route", [1, 4], I32)
        scope.pop().close()

        hot = gate_act[0:BUCKETS + 1, 0, 0:BIAS_W]
        tab = gate_act[0:BUCKETS + 1, 1, 0:DMAPS]
        brow = hid[0:DMAPS, 0, 0:BIAS_W]

        ps = ctx.enter_context(nc.psum_tensor("ps", [P, 8, NW], F32))
        skew = nc.dram_tensor("skew", (DMAPS, BIAS_W), F32, kind="Internal").ap()

        x_landed = [sem(f"x_landed{t}") for t in range(NT)]
        prm_landed = sem("prm_landed")
        w8_landed = sem("w8_landed")
        lam_landed = sem("lam_landed")
        rows_landed = sem("rows_landed")
        tab_landed = sem("tab_landed")
        brow_stored = sem("brow_stored")
        bias_landed = sem("bias_landed")
        out_stored = sem("out_stored")
        raw_landed = [sem(f"raw_landed{s}") for s in range(RAW_SLOTS)]
        hi_ready = sem("hi_ready")
        lo_ready = sem("lo_ready")
        half_used = sem("half_used")
        const_step = sem("const_step")
        act_self = sem("act_self")
        dve_self = sem("dve_self")
        col_t = sem("col_t")
        col_ready = sem("col_ready")
        brow_done = sem("brow_done")
        brow_ready = sem("brow_ready")
        ss_ready = sem("ss_ready")
        ms_ready = sem("ms_ready")
        root_ready = sem("root_ready")
        xs_ready = sem("xs_ready")
        t_done = sem("t_done")
        t_hi = sem("t_hi")
        xt_ready = sem("xt_ready")
        w8h_ready = sem("w8h_ready")
        w8_ready = sem("w8_ready")
        conv_ready = sem("conv_ready")
        qk_ready = sem("qk_ready")
        g8_done = sem("g8_done")
        gtok_ready = sem("gtok_ready")
        grow_done = sem("grow_done")
        gabs_ready = sem("gabs_ready")
        gln_ready = sem("gln_ready")
        gm_ready = sem("gm_ready")
        gem_ready = sem("gem_ready")
        gbc_done = sem("gbc_done")
        acol_ready = sem("acol_ready")
        v_ready = sem("v_ready")
        o_ready = sem("o_ready")
        z_ready = sem("z_ready")
        e_ready = sem("e_ready")
        mask_ready = sem("mask_ready")
        st_done = sem("st_done")
        prob_ready = sem("prob_ready")
        pv_done = sem("pv_done")
        den_read = sem("den_read")
        x_added = sem("x_added")
        silu_ready = sem("silu_ready")
        hid_ready = sem("hid_ready")
        hid_t_done = sem("hid_t_done")
        hid_t_h = sem("hid_t_h")
        hid_t_ready = sem("hid_t_ready")
        dq_ready = sem("dq_ready")
        dkv_ready = sem("dkv_ready")
        qz_zeroed = sem("qz_zeroed")
        logit_done = sem("logit_done")
        max_ready = sem("max_ready")
        exp_ready = sem("exp_ready")
        a_ready = sem("a_ready")
        at_done = sem("at_done")
        at_ready = sem("at_ready")
        opv_done = sem("opv_done")
        osq_ready = sem("osq_ready")
        oms_ready = sem("oms_ready")
        oroot_ready = sem("oroot_ready")
        lam_dot = sem("lam_dot")
        lam_exp = sem("lam_exp")
        xn_h = sem("xn_h")
        xn_ready = sem("xn_ready")
        router_done = sem("router_done")
        gap_ready = sem("gap_ready")
        gexp_ready = sem("gexp_ready")
        chosen_ready = sem("chosen_ready")
        pos_done = sem("pos_done")
        route_ready = sem("route_ready")
        cur_ready = sem("cur_ready")
        pick_ready = sem("pick_ready")
        gather_done = sem("gather_done")
        xe_hi = sem("xe_hi")
        xe_ready = sem("xe_ready")
        pick_t_done = sem("pick_t_done")
        pick_t_ready = sem("pick_t_ready")
        y_h = sem("y_h")
        y_ready = sem("y_ready")
        combine_done = sem("combine_done")
        x_combined = sem("x_combined")
        fin_ready = sem("fin_ready")

        block = ctx.enter_context(nc.Block())

        def at(s, q=0):
            return q * RAW_SLOTS + s

        combine_bank = [[2, 3], [5, 7]]

        def known(v):
            return isinstance(v, int)

        def wait_from(eng, s, v):
            if not (known(v) and v <= 0):
                eng.wait_ge(s, v)

        x_in = A["x"].rearrange("a (t p) d -> (a p) t d", p=P)
        out_v = out.rearrange("a (t p) d -> (a p) t d", p=P)

        @block.sync
        def _(sp):
            def load(s, q, src):
                wait_from(sp, lo_ready, at(s, q) - RAW_SLOTS + 1)
                slot = s % RAW_SLOTS
                n = src.shape[1]
                sp.dma_start(raw[:, slot, :].rearrange("p (k n) -> p k n", k=n), src)\
                  .then_inc(raw_landed[slot], 16)

            def wide(w, k0, n0):
                return w.rearrange("(k p) n -> p k n", p=P)[:, k0:k0 + 4, n0:n0 + NW]

            def slabs(s, w, n_slabs):
                for n in range(n_slabs):
                    for hh in range(2):
                        load(s + 2 * n + hh, 0, wide(w, 4 * hh, n * NW))

            def swiglu(s, q, wg, wu, wd):
                def gate_up(s, q, f):
                    for w in (wg, wu):
                        for hh in range(2):
                            load(s, q, w[:, 4 * hh:4 * hh + 4, bass.ds(f * NW, NW)])
                            s += 1
                    return s

                def down(s, q, f):
                    for hh in range(2):
                        load(s + hh, q, wd[:, bass.ds(f * 4 + 2 * hh, 2), :])

                gate_up(s, q, 0)
                with sp.Fori(1, GROUPS) as f:
                    nxt = gate_up(s + 4, q + (f - 1), f)
                    down(nxt, q + (f - 1), f - 1)
                down(s + 4 + 6 * (GROUPS - 1), q, GROUPS - 1)

            for t in range(NT):
                sp.dma_start(x[:, t, :], x_in[:, t, :]).then_inc(x_landed[t], 16)
            slabs(HALF_Q, A["mlstm_w_in"][0], 6)
            slabs(HALF_MOUT, A["mlstm_w_out"][0], 2)
            swiglu(HALF_FFN, 0, A["ffn_w_gate"][0].rearrange("(k p) f -> p k f", p=P),
                   A["ffn_w_up"][0].rearrange("(k p) f -> p k f", p=P),
                   A["ffn_w_down"][0].rearrange("(c p) d -> p c d", p=P))
            slabs(HALF_DQ, A["diff_w_in"][0], 6)
            slabs(HALF_DOUT, A["diff_w_out"][0], 2)

            mg = A["moe_w_gate"][0].rearrange("e (k p) f -> e p k f", p=P)
            mu = A["moe_w_up"][0].rearrange("e (k p) f -> e p k f", p=P)
            md = A["moe_w_down"][0].rearrange("e (c p) d -> e p c d", p=P)

            def expert(n, e):
                swiglu(HALF_MOE, n * GROUPS, mg[e, :, :, :], mu[e, :, :, :], md[e, :, :, :])

            with sp.Fori(0, NE) as n:
                expert(n, n)
            sp.wait_ge(route_ready, 1)
            over = sp.value_load(route[0:1, 0:1], min_val=0, max_val=OVERFLOW_PASSES)
            with sp.Fori(0, OVERFLOW_PASSES) as j:
                with sp.If(over > j):
                    e = sp.value_load(route[0:1, bass.ds(j + 1, 1)], min_val=0, max_val=NE - 1)
                    expert(j + NE, e)
                sp.nop()
            for t in range(NT):
                sp.wait_ge(fin_ready, t + 1)
                sp.dma_start(out_v[:, t, :], xs[:, t, :]).then_inc(out_stored, 16)
            sp.wait_ge(out_stored, 16 * NT)

        @block.gpsimd
        def _(pool):
            pool.memset(ident[:, :], 0.0).then_inc(const_step, 1)
            pool.memset(anti[:, :], 0.0).then_inc(const_step, 1)
            pool.memset(ones[:, :], 1.0).then_inc(const_step, 1)
            pool.memset(tab, NEG).then_inc(const_step, 1)
            pool.wait_ge(const_step, 1)
            pool.affine_select(out=ident[:, :], in_=ident[:, :], compare_op=ALU.not_equal, fill=1.0, base=0,
                               pattern=[[-1, P]], channel_multiplier=1).then_inc(const_step, 1)
            pool.wait_ge(const_step, 4)
            pool.affine_select(out=anti[:, :], in_=anti[:, :], compare_op=ALU.not_equal, fill=1.0,
                               base=-(P - 1), pattern=[[1, P]], channel_multiplier=1).then_inc(const_step, 1)
            pool.dma_start(hot, A["bucket_hot"]).then_inc(tab_landed, 16)
            pool.dma_start(tab[0:BUCKETS, :], A["rel_bias_table"]).then_inc(tab_landed, 16)
            for i, name in enumerate(("diff_lambda_q1", "diff_lambda_k1", "diff_lambda_q2", "diff_lambda_k2")):
                pool.dma_start(lamv[:, i, :], A[name][0].partition_broadcast(P)).then_inc(lam_landed, 16)
            pool.memset(vx[:, :, :, ML_DV:ML_DVX], 1.0).then_inc(const_step, 1)
            pool.memset(headsel[:, :, :], 0.0).then_inc(const_step, 1)
            pool.memset(zrow[:, :], 0.0).then_inc(const_step, 1)
            pool.wait_ge(const_step, 8)
            pool.affine_select(out=headsel[:, :, :], in_=headsel[:, :, :], compare_op=ALU.not_equal, fill=1.0,
                               base=0, pattern=[[-1, ML_H], [0, P]], channel_multiplier=1)\
                .then_inc(const_step, 1)
            pool.wait_ge(brow_ready, 1)
            pool.dma_start(skew, brow).then_inc(brow_stored, 16)
            pool.wait_ge(e_ready, ML_H)
            for c0 in (0, T):
                d = dec[:, :, c0:c0 + P]
                pool.affine_select(out=d, in_=d, compare_op=ALU.is_ge, fill=0.0, base=0,
                                   pattern=[[0, ML_H], [1, P]], channel_multiplier=-1).then_inc(mask_ready, 1)
            pool.wait_ge(xs_ready, 2 + 2)
            pool.memset(qz[:, :, :, :], 0.0).then_inc(qz_zeroed, 1)
            pool.wait_ge(brow_stored, 16)
            pool.dma_start(bias[:, :, :], bass.AP(skew.tensor, 0, [[1, P], [BIAS_W, DMAPS], [1, T]]))\
                .then_inc(bias_landed, 16)
            pool.wait_ge(xs_ready, 2 * 5)
            pool.dma_start(moe_w[:, :], A["moe_norm"][0].partition_broadcast(P)).then_inc(rows_landed, 16)
            pool.dma_start(fin_w[:, :], A["final_norm"].partition_broadcast(P)).then_inc(rows_landed, 16)
            pool.iota(slots_i[:, :], pattern=[[1, P]], base=0, channel_multiplier=0).then_inc(const_step, 1)
            pool.memset(before[:, :], 1.0).then_inc(const_step, 1)
            pool.wait_ge(const_step, 12)
            pool.affine_select(out=before[:, :], in_=before[:, :], compare_op=ALU.is_gt, fill=0.0, base=0,
                               pattern=[[1, P]], channel_multiplier=-1).then_inc(const_step, 1)
            pool.tensor_copy(slots[:, :], slots_i[:, :]).then_inc(const_step, 1)

        @block.tensor
        def _(pe):
            def three(out_ap, s_hi, s_lo, m_hi, m_lo, start, stop):
                pe.matmul(out_ap, s_hi, m_hi, start=start, stop=False)
                pe.matmul(out_ap, s_hi, m_lo, start=False, stop=False)
                return pe.matmul(out_ap, s_lo, m_hi, start=False, stop=stop)

            def half(s, q, k):
                pe.wait_ge(lo_ready, at(s, q) + 1)
                slot = s % SPLIT_SLOTS
                return [w[:, slot, :].rearrange("p (k n) -> p k n", k=k) for w in (w_hi, w_lo)]

            def tokens_by_columns(s, q, banks, ready=None):
                for hh in range(2):
                    if ready:
                        ready(hh)
                    wh, wl = half(s + hh, q, 4)
                    for k in range(4):
                        kk = 4 * hh + k
                        for t, b in enumerate(banks):
                            mm = three(ps[:, b, :], xt_hi[:, kk, t * P:(t + 1) * P], xt_lo[:, kk, t * P:(t + 1) * P],
                                       wh[:, k, :], wl[:, k, :], kk == 0, kk == KC - 1)
                    mm.then_inc(half_used, 1)

            def columns_by_tokens(s, banks, ready=None):
                for hh in range(2):
                    if ready:
                        ready(hh)
                    wh, wl = half(s + hh, 0, 4)
                    for k in range(4):
                        kk = 4 * hh + k
                        for c, b in enumerate(banks):
                            mm = three(ps[:, b, 0:T], wh[:, k, c * P:(c + 1) * P], wl[:, k, c * P:(c + 1) * P],
                                       xt_hi[:, kk, :], xt_lo[:, kk, :], kk == 0, kk == KC - 1)
                    mm.then_inc(half_used, 1)

            def transpose_xs(n):
                pe.wait_ge(xs_ready, 2 * n + 2)
                for b in range(4):
                    for c in (2 * b, 2 * b + 1):
                        for t in range(NT):
                            o = (c % 2) * T + t * P
                            mm = pe.transpose(ps[:, b, o:o + P], xs[:, t, c * P:(c + 1) * P], ident[:, :])
                    mm.then_inc(t_done, 1)

            def xt_wait(n):
                return lambda hh: pe.wait_ge(xt_ready, 4 * n + 2 * hh + 2)

            def narrow(which, bank):
                for t in range(NT):
                    for k in range(KC):
                        mm = three(ps[:, bank, t * 8:t * 8 + 8], xt_hi[:, k, t * P:(t + 1) * P],
                                   xt_lo[:, k, t * P:(t + 1) * P], w8_hi[:, which, k, :], w8_lo[:, which, k, :],
                                   k == 0, k == KC - 1)
                return mm

            def swiglu(s, q, tiles, tb, after_up=None, before_last=None):
                def down(s, q, first, last):
                    for hh in range(2):
                        wh, wl = half(s + hh, q, 2)
                        for c in range(2):
                            cc = 2 * hh + c
                            for t in range(tiles):
                                for n in range(2):
                                    mm = three(ps[:, 2 * t + n, :], hid_t_hi[:, cc, t * P:(t + 1) * P],
                                               hid_t_lo[:, cc, t * P:(t + 1) * P],
                                               wh[:, c, n * NW:(n + 1) * NW], wl[:, c, n * NW:(n + 1) * NW],
                                               first and cc == 0, last and cc == 3)
                        mm.then_inc(half_used, 1)

                def turn(f):
                    for t in range(tiles):
                        pe.wait_ge(hid_ready, tb + f * tiles + t + 1)
                        for c in range(4):
                            mm = pe.transpose(ps[:, 6 + t, c * P:(c + 1) * P], hid[:, t, c * P:(c + 1) * P],
                                              ident[:, :])
                        mm.then_inc(hid_t_done, 1)

                gate_banks, up_banks = list(range(4, 4 + tiles)), list(range(6, 6 + tiles))

                def group(s, q, f, first):
                    tokens_by_columns(s, q, gate_banks)
                    pe.wait_ge(hid_t_ready, tb + f * tiles)
                    tokens_by_columns(s + 2, q, up_banks)
                    down(s + 4, q, first, False)
                    turn(f)

                tokens_by_columns(s + 2, q, up_banks)
                if after_up:
                    after_up()
                turn(0)
                group(s + 4, q, 1, True)
                with pe.Fori(2, GROUPS) as f:
                    group(s + 4, q + (f - 1), f, False)
                if before_last:
                    before_last()
                pe.wait_ge(hid_t_ready, tb + GROUPS * tiles)
                down(s + 4 + 6 * (GROUPS - 1), q, False, True)

            pe.wait_ge(const_step, 6)
            pe.wait_ge(prm_landed, 16 * 7)
            pe.transpose(ps[:, 7, 0:PRM], prm[:, :], ident[0:PRM, 0:PRM]).then_inc(col_t, 1)
            pe.wait_ge(tab_landed, 32)
            pe.matmul(ps[0:DMAPS, 6, 0:BIAS_W], tab, hot, start=True, stop=True).then_inc(brow_done, 1)

            transpose_xs(0)
            pe.wait_ge(col_ready, 1)
            pe.wait_ge(brow_ready, 1)
            columns_by_tokens(HALF_Q, [4, 5, 6, 7], xt_wait(0))
            columns_by_tokens(HALF_K, [0, 1, 2, 3])
            pe.wait_ge(w8_ready, 1)
            pe.wait_ge(conv_ready, 1)
            narrow(0, 4).then_inc(g8_done, 1)
            pe.wait_ge(conv_ready, 3)
            tokens_by_columns(HALF_V, 0, [5, 6])
            pe.wait_ge(gtok_ready, 1)
            for g in range(2):
                for t in range(NT):
                    o = g * T + t * P
                    mm = pe.transpose(ps[0:ML_H, 4, o:o + P], gtok[:, t, g * ML_H:(g + 1) * ML_H], ident[:, :])
            mm.then_inc(grow_done, 1)
            pe.wait_ge(conv_ready, 5)
            tokens_by_columns(HALF_V + 2, 0, [7, 0])
            pe.wait_ge(v_ready, 1)
            tokens_by_columns(HALF_O, 0, [5, 6])
            pe.wait_ge(conv_ready, 8)
            pe.wait_ge(const_step, 10)
            pe.wait_ge(gm_ready, 1)
            for h in range(ML_H):
                pe.matmul(ps[:, 1 + h // 2, (h % 2) * T:(h % 2 + 1) * T], headsel[:, h, :], g_max[:, :],
                          start=True, stop=True)
            pe.wait_ge(gem_ready, 1)
            for i, g in enumerate((g_a, g_em)):
                for t in range(NT):
                    o = i * 8 + t * ML_H
                    mm = pe.transpose(ps[:, 3, o:o + ML_H], g[:, t * P:(t + 1) * P], ident[0:ML_H, 0:ML_H])
            mm.then_inc(gbc_done, 1)
            pe.wait_ge(v_ready, 2)
            tokens_by_columns(HALF_O + 2, 0, [7, 0])
            pe.wait_ge(qk_ready, 8)
            pe.wait_ge(z_ready, ML_H)
            st_bank = [4, 3, 1, 2]
            for h in range(ML_H):
                b = st_bank[h]
                pe.matmul(ps[:, b, 0:T], qk[:, ML_H + h, 0:P], qk[:, h, :], start=True, stop=True)
                pe.matmul(ps[:, b, T:ROW], qk[:, ML_H + h, P:T], qk[:, h, P:T], start=True, stop=True)\
                  .then_inc(st_done, 1)
            for h in range(ML_H):
                pe.wait_ge(prob_ready, ML_H if h >= 2 else h + 1)
                if h < 2:
                    pe.wait_ge(o_ready, h + 1)
                b0, b1 = (5 + 2 * h) % 8, (6 + 2 * h) % 8
                pe.matmul(ps[:, b0, 0:ML_DVX], prob[:, h, 0:P], vx[:, 0, h, :], start=True, stop=True)
                pe.matmul(ps[:, b1, 0:ML_DVX], prob[:, h, P:T], vx[:, 0, h, :], start=True, stop=False)
                mm = pe.matmul(ps[:, b1, 0:ML_DVX], prob[:, h, T:ROW], vx[:, 1, h, :], start=False, stop=True)
            mm.then_inc(pv_done, 1)
            transpose_xs(1)
            tokens_by_columns(HALF_MOUT, 0, [4, 5], xt_wait(1))
            tokens_by_columns(HALF_MOUT + 2, 0, [6, 7])

            transpose_xs(2)
            tokens_by_columns(HALF_FFN, 0, [4, 5], xt_wait(2))
            swiglu(HALF_FFN, 0, NT, 0)

            transpose_xs(3)
            columns_by_tokens(HALF_DQ, [4, 5, 6, 7], xt_wait(3))
            columns_by_tokens(HALF_DQ + 2, [0, 1, 2, 3])
            pe.wait_ge(dq_ready, 1)
            columns_by_tokens(HALF_DK, [4, 5, 6, 7])
            pe.wait_ge(dq_ready, 2)
            columns_by_tokens(HALF_DK + 2, [0, 1, 2, 3])
            pe.wait_ge(dkv_ready, 1)
            tokens_by_columns(HALF_DVV, 0, [4, 5])
            tokens_by_columns(HALF_DVV + 2, 0, [6, 7])
            pe.wait_ge(dkv_ready, 2)
            pe.wait_ge(bias_landed, 16)
            units = [(h, t) for h in range(DH) for t in range(NT)]

            def logits(i):
                h, t = units[i]
                pe.wait_ge(dkv_ready, 3)
                if i == 2:
                    pe.wait_ge(dkv_ready, 4)
                if i >= 3:
                    pe.wait_ge(exp_ready, i - 2)
                for m in range(2):
                    o = ps[:, 4 + i % 3, m * T:m * T + (t + 1) * P]
                    pe.matmul(o, anti[:, :], bias[:, 2 * h + m, (1 - t) * P:T], start=True, stop=False)
                    mm = pe.matmul(o, qz[:, h, m, t * P:(t + 1) * P], kt[:, h, 0:(t + 1) * P],
                                   start=False, stop=True)
                mm.then_inc(logit_done, 1)

            def turn_a(i):
                h, t = units[i]
                pe.wait_ge(a_ready, i + 1)
                if i >= 1:
                    pe.wait_ge(at_ready, i)
                for b in range(t + 1):
                    mm = pe.transpose(ps[:, 7, b * P:(b + 1) * P], aw[:, i % 2, b * P:(b + 1) * P],
                                      ident[:, :])
                mm.then_inc(at_done, 1)

            def values(i):
                h, t = units[i]
                pe.wait_ge(at_ready, i + 1)
                c = (h % 4) * P
                for b in range(t + 1):
                    mm = pe.matmul(ps[:, 2 * t + h // 4, c:c + P], awt[:, i % 2, b * P:(b + 1) * P],
                                   vv[:, b, h * DDV:(h + 1) * DDV], start=(b == 0), stop=(b == t))
                mm.then_inc(opv_done, 1)

            logits(0)
            logits(1)
            for i in range(len(units)):
                if i + 2 < len(units):
                    logits(i + 2)
                turn_a(i)
                if i >= 1:
                    values(i - 1)
            values(len(units) - 1)
            transpose_xs(4)
            tokens_by_columns(HALF_DOUT, 0, [4, 5], xt_wait(4))
            tokens_by_columns(HALF_DOUT + 2, 0, [6, 7])

            transpose_xs(5)
            pe.wait_ge(xt_ready, 4 * 6)
            narrow(1, 4).then_inc(router_done, 1)
            pe.wait_ge(chosen_ready, 1)
            pe.wait_ge(const_step, 14)
            pe.matmul(ps[:, 5, 0:8], before[:, :], rt[:, 0, 0, :], start=True, stop=True)
            pe.matmul(ps[:, 5, 8:16], before[:, :], rt[:, 0, 1, :], start=True, stop=False)
            pe.matmul(ps[:, 5, 8:16], ones[:, :], rt[:, 0, 0, :], start=False, stop=True)
            pe.matmul(ps[:, 5, 16:24], ones[:, :], rt[:, 0, 0, :], start=True, stop=False)
            pe.matmul(ps[:, 5, 16:24], ones[:, :], rt[:, 0, 1, :], start=False, stop=True).then_inc(pos_done, 1)
            pe.wait_ge(xn_ready, NT)

            def gather(n):
                pe.wait_ge(pick_ready, n + 1)
                for b in range(2):
                    for c in range(4):
                        f0 = (4 * b + c) * P
                        for i, (xn, t) in enumerate([(xn, t) for xn in (xn_hi, xn_lo) for t in range(NT)]):
                            mm = pe.matmul(ps[:, 2 + b, c * P:(c + 1) * P], xn[:, t, f0:f0 + P], pick[:, t, :],
                                           start=(i == 0), stop=(i == 3))
                    mm.then_inc(gather_done, 1)

            def first_gate(n, s, q):
                tokens_by_columns(s, q, [4], lambda hh: pe.wait_ge(xe_ready, n * 2 + hh + 1))

            def transpose_pick(n):
                pe.wait_ge(x_combined, n * 4 + 1)
                for t in range(NT):
                    pe.transpose(ps[:, 7, t * P:(t + 1) * P], pick[:, t, :].bitcast(F32), ident[:, :])
                for t in range(NT):
                    mm = pe.matmul(ps[:, 7, T:T + 1], pick[:, t, :].bitcast(F32), cur[:, 4 + t:5 + t],
                                   start=(t == 0), stop=(t == NT - 1))
                mm.then_inc(pick_t_done, 1)

            def combine(n):
                pe.wait_ge(pick_t_ready, n + 1)
                for nh in range(2):
                    pe.wait_ge(y_ready, n * 2 + nh + 1)
                    for t in range(NT):
                        for y in (y_hi, y_lo):
                            mm = pe.matmul(ps[:, combine_bank[nh][t], :], pick_t[:, t * P:(t + 1) * P],
                                           y[:, nh * NW:(nh + 1) * NW], start=(y is y_hi), stop=(y is y_lo))
                        mm.then_inc(combine_done, 1)

            def expert(n, follows):
                swiglu(HALF_MOE, n * GROUPS, 1, NT * GROUPS + n * GROUPS,
                       after_up=lambda: transpose_pick(n),
                       before_last=(lambda: gather(n + 1)) if follows else None)
                if follows:
                    first_gate(n + 1, HALF_MOE + 6 * GROUPS, n * GROUPS)
                combine(n)

            gather(0)
            first_gate(0, HALF_MOE, 0)
            with pe.Fori(0, NE - 1) as n:
                expert(n, True)
            expert(NE - 1, False)
            pe.wait_ge(route_ready, 1)
            over = pe.value_load(route[0:1, 0:1], min_val=0, max_val=OVERFLOW_PASSES)
            with pe.Fori(0, OVERFLOW_PASSES) as j:
                with pe.If(over > j):
                    gather(j + NE)
                    first_gate(j + NE, HALF_MOE, (j + NE) * GROUPS)
                    expert(j + NE, False)
                pe.nop()

        @block.scalar
        def _(act):
            self_n = [0]

            def mine(ins):
                ins.then_inc(act_self, 1)
                self_n[0] += 1
                act.wait_ge(act_self, self_n[0])

            def hi(s, q=0):
                slot = s % RAW_SLOTS
                act.wait_ge(raw_landed[slot], (q + (s // RAW_SLOTS + 1)) * 16)
                wait_from(act, half_used, at(s, q) - SPLIT_SLOTS + 1)
                act.activation(w_hi[:, s % SPLIT_SLOTS, :], raw[:, slot, :], ACT.Copy).then_inc(hi_ready, 1)

            def squares(n, wait):
                for t in range(NT):
                    wait(t)
                    act.activation(xs[:, t, :], x[:, t, :], ACT.Square, accum_out=small[:, S_SQ + t:S_SQ + t + 1])\
                       .then_inc(ss_ready, 1)

            def root(n):
                act.wait_ge(ms_ready, n + 1)
                act.activation(small[:, S_SQ:S_SQ + 2], small[:, S_MS:S_MS + 2], ACT.Sqrt).then_inc(root_ready, 1)

            def evac_xt(n, c0, banks=range(4), scale=None):
                for b in banks:
                    act.wait_ge(t_done, 4 * n + b + 1)
                    if c0 is None and scale is None:
                        ins = act.activation(xt_hi[:, 2 * b:2 * b + 2, :],
                                             ps[:, b, :].rearrange("p (c t) -> p c t", c=2), ACT.Copy)
                    else:
                        for i in range(2):
                            c = 2 * b + i
                            w = scale if scale is not None else col[:, c0 + c:c0 + c + 1]
                            ins = act.activation(xt_hi[:, c, :], ps[:, b, i * T:(i + 1) * T], ACT.Copy, scale=w)
                    ins.then_inc(t_hi, 1)

            def swiglu(s, q, tiles, tb, after_gate=None):
                def evac(f):
                    for t in range(tiles):
                        act.wait_ge(hid_t_done, tb + tiles * f + t + 1)
                        act.activation(hid_t_hi[:, :, t * P:(t + 1) * P],
                                       ps[:, 6 + t, :].rearrange("p (c t) -> p c t", c=4), ACT.Copy)\
                           .then_inc(hid_t_h, 1)

                def gate(s, q):
                    act.wait_ge(half_used, at(s, q) + 2)
                    for t in range(tiles):
                        act.activation(gate_act[:, t, :], ps[:, 4 + t, :], ACT.Silu).then_inc(silu_ready, 1)

                gate(s, q)
                for i in (4, 5):
                    hi(s + i, q)
                if after_gate:
                    after_gate()
                with act.Fori(1, GROUPS) as f:
                    q1, s1 = q + (f - 1), s + 4
                    evac(f - 1)
                    for i in (2, 3):
                        hi(s1 + i, q1)
                    gate(s1, q1)
                    for i in (4, 5, 6, 7):
                        hi(s1 + i, q1)
                evac(GROUPS - 1)

            prm_rows = [("mlstm_norm", C_MNORM), ("mlstm_head_norm", C_HNORM), ("ffn_norm", C_FNORM),
                        ("diff_norm", C_DNORM), ("mlstm_conv_b", C_CONVB)]
            for name, r in prm_rows:
                act.dma_start(prm[r:r + 8, :], A[name][0].rearrange("(c p) -> c p", p=P)).then_inc(prm_landed, 16)
            act.dma_start(prm[C_CONVW:C_CONVW + 32, :], A["mlstm_conv_w"][0].rearrange("w (c p) -> (w c) p", p=P))\
               .then_inc(prm_landed, 16)
            act.dma_start(prm[C_SUB:C_SUB + 1, :], A["diff_subln"]).then_inc(prm_landed, 16)
            act.dma_start(w8[:, 0, :, :], A["mlstm_w_in"][0].rearrange("(k p) n -> p k n", p=P)[:, :, 3 * D:3 * D + 8])\
               .then_inc(w8_landed, 16)
            act.dma_start(w8[:, 1, :, :], A["moe_w_router"][0].rearrange("(k p) n -> p k n", p=P))\
               .then_inc(w8_landed, 16)
            act.dma_start(b8[:, 0, 0:4], A["mlstm_b_igate"][0].partition_broadcast(P)).then_inc(w8_landed, 16)
            act.dma_start(b8[:, 0, 4:8], A["mlstm_b_fgate"][0].partition_broadcast(P)).then_inc(w8_landed, 16)
            act.dma_start(b8[:, 1, :], A["moe_b_router"][0].partition_broadcast(P)).then_inc(w8_landed, 16)

            squares(0, lambda t: act.wait_ge(x_landed[t], 16))
            root(0)
            act.wait_ge(w8_landed, 16 * 5)
            act.activation(w8_hi[:, :, :, :], w8[:, :, :, :], ACT.Copy).then_inc(w8h_ready, 1)
            act.wait_ge(col_ready, 1)
            hi(0)
            evac_xt(0, C_MNORM, (0, 1))
            hi(1)
            evac_xt(0, C_MNORM, (2, 3))
            hi(2)
            hi(3)

            def silu_qk(c):
                act.wait_ge(conv_ready, c + 1)
                act.activation(qk[:, c, :], qk[:, c, :], ACT.Silu).then_inc(qk_ready, 1)

            for c in (0, 1):
                silu_qk(c)
            hi(4)
            for c in (2, 3):
                silu_qk(c)
            hi(5)
            hi(6)
            for c in (4, 5):
                silu_qk(c)
            hi(7)
            for c in (6, 7):
                silu_qk(c)
            hi(8)

            def evac_v(n, banks):
                act.wait_ge(half_used, HALF_V + 2 * n + 2)
                for t, b in enumerate(banks):
                    ins = act.activation(vx[:, t, 2 * n:2 * n + 2, 0:ML_DV],
                                         ps[:, b, :].rearrange("p (h v) -> p h v", h=2), ACT.Copy)
                ins.then_inc(v_ready, 1)

            def evac_o(n, banks):
                act.wait_ge(half_used, HALF_O + 2 * n + 2)
                for t, b in enumerate(banks):
                    ins = act.activation(sig_o[:, t, n * NW:(n + 1) * NW], ps[:, b, :], ACT.Sigmoid)
                ins.then_inc(o_ready, 1)

            evac_v(0, (5, 6))
            hi(9)
            act.wait_ge(gabs_ready, 1)
            mine(act.activation(g_exp[:, :], g_abs[:, :], ACT.Exp, scale=-1.0))
            act.activation(g_ln[:, :], g_exp[:, :], ACT.Ln, bias=1.0).then_inc(gln_ready, 1)
            hi(10)
            evac_v(1, (7, 0))
            act.wait_ge(gm_ready, 2)
            act.activation(g_em[:, :], g_m[:, :], ACT.Exp, scale=-1.0).then_inc(gem_ready, 1)
            hi(11)
            hi(12)
            evac_o(0, (5, 6))
            for h in range(ML_H):
                act.wait_ge(z_ready, h + 1)
                act.activation(dec[:, h, :], dec[:, h, :], ACT.Exp, scale=-1.0).then_inc(e_ready, 1)
            hi(13)
            evac_o(1, (7, 0))
            act.wait_ge(den_read, 1)
            for r in range(2 * ML_H):
                ins = act.activation(xs[:, r // 4, (r % 4) * ML_DV:(r % 4 + 1) * ML_DV], ps[:, (5 + r) % 8, 0:ML_DV], ACT.Square, accum_out=mn[:, 0, r:r + 1])
            ins.then_inc(ss_ready, 1)
            act.wait_ge(ms_ready, 2)
            act.activation(mn[:, 2, :], mn[:, 1, :], ACT.Sqrt).then_inc(root_ready, 1)
            evac_xt(1, C_HNORM)
            for i in range(HALF_MOUT + 2, HALF_MOUT + 6):
                hi(i)

            squares(2, lambda t: act.wait_ge(x_added, 4))
            root(2)
            evac_xt(2, C_FNORM)
            hi(HALF_FFN + 2)
            hi(HALF_FFN + 3)
            swiglu(HALF_FFN, 0, NT, 0)
            hi(HALF_DQ)
            hi(HALF_DQ + 1)

            squares(3, lambda t: act.wait_ge(x_added, 8))
            root(3)
            evac_xt(3, C_DNORM)
            act.wait_ge(qz_zeroed, 1)
            for n in range(2):
                hi(HALF_DQ + 2 * n + 2)
                hi(HALF_DQ + 2 * n + 3)
                act.wait_ge(half_used, HALF_DQ + 2 * n + 2)
                for c in range(4):
                    b = 4 * (1 - n) + c
                    for m in range(2):
                        r = slice(m * DHD, (m + 1) * DHD)
                        ins = act.activation(qz[r, 4 * n + c, m, :], ps[r, b, 0:T], ACT.Copy, scale=-DSCALE)
                ins.then_inc(dq_ready, 1)
            act.wait_ge(lam_dot, 1)
            act.activation(lam[:, 2:4], lam[:, 0:2], ACT.Exp).then_inc(lam_exp, 1)
            for i in range(HALF_DK + 2, HALF_DOUT + 2):
                hi(i)
            for i in range(2 * DH):
                klen = (i % 2 + 1) * P
                act.wait_ge(max_ready, i + 1)
                if i >= 2:
                    act.wait_ge(a_ready, i - 1)
                for m in range(2):
                    ins = act.activation(ex[:, i % 2, m, 0:klen], ps[:, 4 + i % 3, m * T:m * T + klen], ACT.Exp,
                                         scale=-1.0, bias=nmx[:, i % 3, m:m + 1], accum_out=sm[:, i % 2, m:m + 1])
                ins.then_inc(exp_ready, 1)

                def evac_a(i):
                    klen = (i % 2 + 1) * P
                    act.wait_ge(at_done, i + 1)
                    if i >= 2:
                        act.wait_ge(opv_done, i - 1)
                    act.activation(awt[:, i % 2, 0:klen], ps[:, 7, 0:klen], ACT.Copy).then_inc(at_ready, 1)

                if i >= 1:
                    evac_a(i - 1)
            evac_a(2 * DH - 1)
            act.wait_ge(opv_done, 2 * DH)
            for b in range(4):
                act.activation(osq[b], ps[:, b, :], ACT.Square)\
                   .then_inc(osq_ready, 1)
            act.wait_ge(oms_ready, 1)
            act.activation(oms[:, 2, :], oms[:, 1, :], ACT.Sqrt).then_inc(oroot_ready, 1)
            evac_xt(4, None, scale=sub_w[:, 0:1])
            for i in range(HALF_DOUT + 2, HALF_DOUT + 6):
                hi(i)

            squares(4, lambda t: act.wait_ge(x_added, 12))
            root(4)
            for t in range(NT):
                act.wait_ge(xs_ready, 2 * 5 + t + 1)
                act.activation(xn_hi[:, t, :], xs[:, t, :], ACT.Copy).then_inc(xn_h, 1)
            evac_xt(5, None)
            act.wait_ge(gap_ready, 1)
            act.activation(gsc[:, :, 1:2], gsc[:, :, 0:1], ACT.Exp).then_inc(gexp_ready, 1)

            def gathered(n):
                for b in range(2):
                    act.wait_ge(gather_done, n * 2 + b + 1)
                    act.activation(xt_hi[:, 4 * b:4 * b + 4, 0:P], ps[:, 2 + b, :].rearrange("p (c t) -> p c t", c=4),
                                   ACT.Copy).then_inc(xe_hi, 1)

            def picked(n):
                act.wait_ge(pick_t_done, n + 1)
                act.activation(pick_t[:, :], ps[:, 7, 0:T], ACT.Copy)
                act.activation(gslot[:, :], ps[:, 7, T:T + 1], ACT.Copy).then_inc(pick_t_ready, 1)

            def expert(n, follows):
                q, nxt = n * GROUPS, HALF_MOE + 6 * GROUPS
                swiglu(HALF_MOE, q, 1, NT * GROUPS + n * GROUPS, lambda: picked(n))
                if follows:
                    gathered(n + 1)
                    hi(nxt, q)
                    hi(nxt + 1, q)
                act.wait_ge(half_used, n * (6 * GROUPS) + (HALF_MOE + 6 * GROUPS))
                act.wait_ge(pick_t_ready, n + 1)
                for nh in range(2):
                    act.activation(y_hi[:, nh * NW:(nh + 1) * NW], ps[:, nh, :], ACT.Copy, scale=gslot[:, 0:1])\
                       .then_inc(y_h, 1)
                if follows:
                    hi(nxt + 2, q)
                    hi(nxt + 3, q)

            gathered(0)
            hi(HALF_MOE + 2)
            hi(HALF_MOE + 3)
            with act.Fori(0, NE - 1) as n:
                expert(n, True)
            expert(NE - 1, False)
            act.wait_ge(route_ready, 1)
            over = act.value_load(route[0:1, 0:1], min_val=0, max_val=OVERFLOW_PASSES)
            with act.Fori(0, OVERFLOW_PASSES) as j:
                with act.If(over > j):
                    hi(HALF_MOE, (j + NE) * GROUPS)
                    hi(HALF_MOE + 1, (j + NE) * GROUPS)
                    gathered(j + NE)
                    hi(HALF_MOE + 2, (j + NE) * GROUPS)
                    hi(HALF_MOE + 3, (j + NE) * GROUPS)
                    expert(j + NE, False)
                act.nop()
            squares(5, lambda t: act.wait_ge(x_combined, over * 4 + (4 * NE + 1)))
            root(5)

        @block.vector
        def _(dve):
            self_n = [0]

            def own(ins):
                ins.then_inc(dve_self, 1)
                self_n[0] += 1
                dve.wait_ge(dve_self, self_n[0])

            def lo(s, q=0):
                slot, ring = s % RAW_SLOTS, s % SPLIT_SLOTS
                dve.wait_ge(hi_ready, at(s, q) + 1)
                dve.tensor_tensor(w_lo[:, ring, :], raw[:, slot, :], w_hi[:, ring, :].bitcast(F32), ALU.subtract)\
                   .then_inc(lo_ready, 1)

            def mean(n, d, eps):
                dve.wait_ge(ss_ready, n)
                dve.tensor_scalar(small[:, S_MS:S_MS + 2], small[:, S_SQ:S_SQ + 2], 1.0 / d, eps, ALU.mult, ALU.add)\
                   .then_inc(ms_ready, 1)

            def normed(n, row=None, out_t=None):
                dve.wait_ge(root_ready, n)
                own(dve.reciprocal(small[:, S_RSTD:S_RSTD + 2], small[:, S_SQ:S_SQ + 2]))
                for t in range(NT):
                    r = small[:, S_RSTD + t:S_RSTD + t + 1]
                    if row is None:
                        ins = dve.tensor_scalar(xs[:, t, :], x[:, t, :], r, None, ALU.mult)
                    else:
                        ins = dve.scalar_tensor_tensor(out=xs[:, t, :], in0=x[:, t, :], scalar=r, in1=row,
                                                       op0=ALU.mult, op1=ALU.mult)
                    ins.then_inc(out_t or xs_ready, 1)

            def evac_xt(n, c0, banks=range(4), scale=None):
                for b in banks:
                    dve.wait_ge(t_hi, 4 * n + b + 1)
                    if c0 is None and scale is None:
                        ins = dve.tensor_tensor(xt_lo[:, 2 * b:2 * b + 2, :],
                                                ps[:, b, :].rearrange("p (c t) -> p c t", c=2),
                                                xt_hi[:, 2 * b:2 * b + 2, :].bitcast(F32), ALU.subtract)
                    else:
                        for i in range(2):
                            c = 2 * b + i
                            w = scale if scale is not None else col[:, c0 + c:c0 + c + 1]
                            ins = dve.scalar_tensor_tensor(out=xt_lo[:, c, :], in0=ps[:, b, i * T:(i + 1) * T],
                                                           scalar=w, in1=xt_hi[:, c, :].bitcast(F32),
                                                           op0=ALU.mult, op1=ALU.subtract)
                    ins.then_inc(xt_ready, 1)

            def add_x(banks, n, done):
                dve.wait_ge(half_used, done)
                for t, b in enumerate(banks):
                    xv = x[:, t, n * NW:(n + 1) * NW]
                    dve.tensor_tensor(xv, ps[:, b, :], xv, ALU.add).then_inc(x_added, 1)

            def swiglu(s, q, tiles, tb, after_hidden=None):
                def evac(f):
                    for t in range(tiles):
                        dve.wait_ge(hid_t_h, tb + tiles * f + t + 1)
                        dve.tensor_tensor(hid_t_lo[:, :, t * P:(t + 1) * P],
                                          ps[:, 6 + t, :].rearrange("p (c t) -> p c t", c=4),
                                          hid_t_hi[:, :, t * P:(t + 1) * P].bitcast(F32), ALU.subtract)\
                           .then_inc(hid_t_ready, 1)

                def hidden(s, q, f):
                    dve.wait_ge(half_used, at(s, q) + 4)
                    for t in range(tiles):
                        dve.wait_ge(silu_ready, tb + tiles * f + t + 1)
                        dve.tensor_tensor(hid[:, t, :], ps[:, 6 + t, :], gate_act[:, t, :], ALU.mult)\
                           .then_inc(hid_ready, 1)

                lo(s + 4, q)
                lo(s + 5, q)
                hidden(s, q, 0)
                if after_hidden:
                    after_hidden()
                with dve.Fori(1, GROUPS) as f:
                    q1, s1 = q + (f - 1), s + 4
                    evac(f - 1)
                    for i in (2, 3, 4, 5):
                        lo(s1 + i, q1)
                    hidden(s1, q1, f)
                    for i in (6, 7):
                        lo(s1 + i, q1)
                evac(GROUPS - 1)

            dve.wait_ge(col_t, 1)
            dve.tensor_copy(col[:, :], ps[:, 7, 0:PRM]).then_inc(col_ready, 1)
            mean(2, D, EPS)
            normed(1)
            dve.wait_ge(w8h_ready, 1)
            dve.tensor_tensor(w8_lo[:, :, :, :], w8[:, :, :, :], w8_hi[:, :, :, :].bitcast(F32), ALU.subtract)\
               .then_inc(w8_ready, 1)
            dve.wait_ge(brow_done, 1)
            dve.tensor_scalar(brow, ps[0:DMAPS, 6, 0:BIAS_W], -1.0, None, ALU.mult).then_inc(brow_ready, 1)
            lo(0)
            evac_xt(0, C_MNORM, (0, 1))
            lo(1)
            evac_xt(0, C_MNORM, (2, 3))
            lo(2)
            lo(3)

            def conv_pair(c0):
                dve.wait_ge(half_used, 2 if c0 < 4 else 4)
                for d in range(CONV_W):
                    for c in (c0, c0 + 1):
                        b = 4 + c if c < 4 else c - 4
                        w = col[:, C_CONVW + (CONV_W - 1 - d) * 8 + c:C_CONVW + (CONV_W - 1 - d) * 8 + c + 1]
                        if d == 0:
                            ins = dve.tensor_scalar(qk[:, c, :], ps[:, b, 0:T], w, col[:, C_CONVB + c:C_CONVB + c + 1],
                                                    ALU.mult, ALU.add)
                        else:
                            ins = dve.scalar_tensor_tensor(out=qk[:, c, d:T], in0=ps[:, b, 0:T - d], scalar=w,
                                                           in1=qk[:, c, d:T], op0=ALU.mult, op1=ALU.add)
                        if d == CONV_W - 1:
                            ins.then_inc(conv_ready, 1)
                        elif c == c0:
                            ins.then_inc(dve_self, 1)
                            self_n[0] += 1
                        else:
                            own(ins)

            conv_pair(0)
            lo(4)
            conv_pair(2)
            lo(5)
            lo(6)
            dve.wait_ge(g8_done, 1)
            dve.wait_ge(w8_landed, 16 * 5)
            for t in range(NT):
                ins = dve.tensor_tensor(gtok[:, t, :], ps[:, 4, t * 8:t * 8 + 8], b8[:, 0, :], ALU.add)
            ins.then_inc(gtok_ready, 1)
            conv_pair(4)
            lo(7)
            conv_pair(6)
            lo(8)
            dve.wait_ge(grow_done, 1)
            own(dve.tensor_copy(grow[:, :], ps[0:ML_H, 4, :]))
            dve.scalar_tensor_tensor(out=g_abs[:, :], in0=grow[:, T:2 * T], scalar=-1.0, in1=grow[:, T:2 * T],
                                     op0=ALU.mult, op1=ALU.max).then_inc(gabs_ready, 1)
            dve.wait_ge(gln_ready, 1)
            own(dve.scalar_tensor_tensor(out=g_logf[:, :], in0=grow[:, T:2 * T], scalar=0.0, in1=g_ln[:, :],
                                         op0=ALU.min, op1=ALU.subtract))
            dve.wait_ge(const_step, 9)
            own(dve.tensor_tensor_scan(g_cum[:, :], g_logf[:, :], zrow[:, :], 0.0, ALU.add, ALU.add))
            own(dve.tensor_tensor(g_a[:, :], grow[:, 0:T], g_cum[:, :], ALU.subtract))
            dve.tensor_tensor_scan(g_max[:, :], g_a[:, :], g_a[:, :], 0.0, ALU.max, ALU.max).then_inc(gm_ready, 1)
            dve.wait_ge(gm_ready, 1)
            dve.tensor_tensor(g_m[:, :], g_cum[:, :], g_max[:, :], ALU.add).then_inc(gm_ready, 1)
            for i in (9, 10, 11, 12):
                lo(i)
            dve.wait_ge(gbc_done, 1)
            own(dve.tensor_copy(acol[:, :, :], ps[:, 3, 0:8].rearrange("p (t h) -> p t h", t=NT)))
            dve.tensor_copy(em[:, :].rearrange("p (h t) -> p t h", t=NT),
                            ps[:, 3, 8:16].rearrange("p (t h) -> p t h", t=NT)).then_inc(acol_ready, 1)
            for h in range(ML_H):
                mb = ps[:, 1 + h // 2, (h % 2) * T:(h % 2 + 1) * T]
                dve.tensor_scalar(dec[:, h, 0:T], mb, acol[:, 0, h:h + 1], 0.0, ALU.subtract, ALU.max)
                dve.tensor_scalar(dec[:, h, T:ROW], mb[:, P:T], acol[:, 1, h:h + 1], 0.0, ALU.subtract, ALU.max)\
                   .then_inc(z_ready, 1)
            lo(13)
            dve.wait_ge(mask_ready, 2)
            for h, b in enumerate([4, 3, 1, 2]):
                dve.wait_ge(st_done, h + 1)
                dve.scalar_tensor_tensor(out=prob[:, h, :], in0=ps[:, b, 0:ROW], scalar=ML_SCALE, in1=dec[:, h, :],
                                         op0=ALU.mult, op1=ALU.mult).then_inc(prob_ready, 1)
            dve.wait_ge(pv_done, 1)
            dve.tensor_copy(mn[:, 3, 0:3], ps[:, 5:8, ML_DV])
            dve.tensor_copy(mn[:, 3, 3:8], ps[:, 0:5, ML_DV]).then_inc(den_read, 1)
            dve.wait_ge(den_read, 1)
            own(dve.scalar_tensor_tensor(out=mn[:, 4, :], in0=mn[:, 3, :], scalar=-1.0, in1=mn[:, 3, :],
                                         op0=ALU.mult, op1=ALU.max))
            dve.wait_ge(acol_ready, 1)
            own(dve.tensor_tensor(mn[:, 6, :], mn[:, 4, :], em[:, :], ALU.max))
            own(dve.reciprocal(mn[:, 5, :], mn[:, 6, :]))
            own(dve.tensor_tensor(mn[:, 6, :], mn[:, 5, :], mn[:, 5, :], ALU.mult))
            dve.wait_ge(ss_ready, 3)
            own(dve.tensor_tensor(mn[:, 7, :], mn[:, 0, :], mn[:, 6, :], ALU.mult))
            dve.tensor_scalar(mn[:, 1, :], mn[:, 7, :], 1.0 / ML_DV, EPS, ALU.mult, ALU.add).then_inc(ms_ready, 1)
            dve.wait_ge(root_ready, 2)
            own(dve.reciprocal(mn[:, 3, :], mn[:, 2, :]))
            own(dve.tensor_tensor(mn[:, 6, :], mn[:, 3, :], mn[:, 5, :], ALU.mult))
            dve.wait_ge(o_ready, 2)
            for r in range(2 * ML_H):
                h, t = divmod(r, 2)
                c = slice(h * ML_DV, (h + 1) * ML_DV)
                ins = dve.scalar_tensor_tensor(out=xs[:, t, c], in0=ps[:, (5 + r) % 8, 0:ML_DV], scalar=mn[:, 6, r:r + 1],
                                               in1=sig_o[:, t, c], op0=ALU.mult, op1=ALU.mult)
                if r >= 2 * ML_H - 2:
                    ins.then_inc(xs_ready, 1)
            evac_xt(1, C_HNORM)
            lo(HALF_MOUT + 2)
            lo(HALF_MOUT + 3)
            add_x((4, 5), 0, HALF_MOUT + 2)
            lo(HALF_MOUT + 4)
            lo(HALF_MOUT + 5)
            add_x((6, 7), 1, HALF_MOUT + 4)

            mean(5, D, EPS)
            normed(3)
            evac_xt(2, C_FNORM)
            dve.wait_ge(brow_stored, 16)
            lo(HALF_FFN + 2)
            lo(HALF_FFN + 3)
            swiglu(HALF_FFN, 0, NT, 0)
            lo(HALF_DQ)
            lo(HALF_DQ + 1)
            dve.wait_ge(half_used, HALF_DQ)
            for t in range(NT):
                for n in range(2):
                    xv = x[:, t, n * NW:(n + 1) * NW]
                    dve.tensor_tensor(xv, ps[:, 2 * t + n, :], xv, ALU.add).then_inc(x_added, 1)

            mean(7, D, EPS)
            normed(4)
            dve.wait_ge(lam_landed, 64)
            own(dve.tensor_tensor(lamp[:, :, :], lamv[:, 0:4:2, :], lamv[:, 1:4:2, :], ALU.mult))
            dve.tensor_reduce(lam[:, 0:2], lamp[:, :, :], AX_X, ALU.add).then_inc(lam_dot, 1)
            own(dve.tensor_scalar(sub_w[:, :], col[:, C_SUB:C_SUB + 1], 1.0 - LAM_INIT, None, ALU.mult))
            evac_xt(3, C_DNORM)
            for i in range(HALF_DQ + 2, HALF_DK + 2):
                lo(i)

            def copy_k(n):
                lo(HALF_DK + 2 * n + 2)
                lo(HALF_DK + 2 * n + 3)
                dve.wait_ge(half_used, HALF_DK + 2 * n + 2)
                if n == 0:
                    dve.wait_ge(xs_ready, 4)
                for c in range(4):
                    ins = dve.tensor_copy(kt[:, 4 * n + c, :], ps[:, 4 * (1 - n) + c, 0:T])
                ins.then_inc(dkv_ready, 1)

            def copy_v(n):
                lo(HALF_DVV + 2 * n + 2)
                lo(HALF_DVV + 2 * n + 3)
                dve.wait_ge(half_used, HALF_DVV + 2 * n + 2)
                for t in range(NT):
                    ins = dve.tensor_copy(vv[:, t, n * NW:(n + 1) * NW], ps[:, 4 + 2 * n + t, :])
                ins.then_inc(dkv_ready, 1)

            for n in range(2):
                copy_k(n)
            for n in range(2):
                copy_v(n)
            dve.wait_ge(lam_exp, 1)
            own(dve.tensor_tensor(lam[:, 4:5], lam[:, 3:4], lam[:, 2:3], ALU.subtract))
            own(dve.tensor_scalar(lam[:, 5:6], lam[:, 4:5], -LAM_INIT, None, ALU.add))

            def row_max(i):
                klen = (i % 2 + 1) * P
                dve.wait_ge(logit_done, i + 1)
                if i >= 3:
                    dve.wait_ge(exp_ready, i - 2)
                lg2 = ps[:, 4 + i % 3, :].rearrange("p (m k) -> p m k", m=2)[:, :, 0:klen]
                dve.tensor_reduce(nmx[:, i % 3, :], lg2, AX_X, ALU.min).then_inc(max_ready, 1)

            def mix(i):
                klen = (i % 2 + 1) * P
                j = i % 2
                dve.wait_ge(exp_ready, i + 1)
                own(dve.reciprocal(sm[:, j, 2:4], sm[:, j, 0:2]))
                own(dve.tensor_tensor(sm[:, j, 4:5], sm[:, j, 3:4], lam[:, 5:6], ALU.mult))
                if i >= 2:
                    dve.wait_ge(at_done, i - 1)
                own(dve.tensor_scalar(aw[:, j, 0:klen], ex[:, j, 0, 0:klen], sm[:, j, 2:3], None, ALU.mult))
                dve.scalar_tensor_tensor(out=aw[:, j, 0:klen], in0=ex[:, j, 1, 0:klen], scalar=sm[:, j, 4:5],
                                         in1=aw[:, j, 0:klen], op0=ALU.mult, op1=ALU.add).then_inc(a_ready, 1)

            row_max(0)
            row_max(1)
            for i in range(2 * DH):
                mix(i)
                if i + 2 < 2 * DH:
                    row_max(i + 2)
            for b in range(4):
                dve.wait_ge(osq_ready, b + 1)
                ins = dve.tensor_reduce(oms[:, 0, 4 * b:4 * b + 4],
                                        osq[b].rearrange("p (h v) -> p h v", h=4),
                                        AX_X, ALU.add)
            own(ins)
            dve.tensor_scalar(oms[:, 1, :], oms[:, 0, :], 1.0 / DDV, SUB_EPS, ALU.mult, ALU.add).then_inc(oms_ready, 1)
            dve.wait_ge(oroot_ready, 1)
            own(dve.reciprocal(oms[:, 3, :], oms[:, 2, :]))
            for b in range(4):
                r = oms[:, 3, 4 * b:4 * b + 4].unsqueeze(2).to_broadcast([P, 4, DDV])
                ins = dve.tensor_tensor(
                    xs[:, b // 2, (b % 2) * NW:(b % 2 + 1) * NW].rearrange("p (h v) -> p h v", h=4),
                    ps[:, b, :].rearrange("p (h v) -> p h v", h=4), r, ALU.mult)
                if b >= 2:
                    ins.then_inc(xs_ready, 1)
            evac_xt(4, None, scale=sub_w[:, 0:1])
            lo(HALF_DOUT + 2)
            lo(HALF_DOUT + 3)
            add_x((4, 5), 0, HALF_DOUT + 2)
            lo(HALF_DOUT + 4)
            lo(HALF_DOUT + 5)
            add_x((6, 7), 1, HALF_DOUT + 4)

            mean(9, D, EPS)
            dve.wait_ge(rows_landed, 32)
            normed(5, row=moe_w[:, :])
            for t in range(NT):
                dve.wait_ge(xn_h, t + 1)
                dve.tensor_tensor(xn_lo[:, t, :], xs[:, t, :], xn_hi[:, t, :].bitcast(F32), ALU.subtract)\
                   .then_inc(xn_ready, 1)
            evac_xt(5, None)
            dve.wait_ge(router_done, 1)
            for t in range(NT):
                ins = dve.tensor_tensor(lg[:, t, :], ps[:, 4, t * 8:t * 8 + 8], b8[:, 1, :], ALU.add)
            own(ins)
            for t in range(NT):
                ins = dve.max(top[:, t, :], lg[:, t, :])
            own(ins)
            for t in range(NT):
                ins = dve.max_index(topi[:, t, :], top[:, t, :], lg[:, t, :])
            own(ins)
            dve.tensor_tensor(gsc[:, :, 0:1], top[:, :, 1:2], top[:, :, 0:1], ALU.subtract).then_inc(gap_ready, 1)
            own(dve.tensor_copy(topf[:, :, :], topi[:, :, :]))
            dve.wait_ge(const_step, 14)
            for t in range(NT):
                for i in range(2):
                    ins = dve.tensor_scalar(m12[:, t, i, :], slots[:, 0:NE], topf[:, t, i:i + 1], None, ALU.is_equal)
            own(ins)
            for t in range(NT):
                ins = dve.tensor_tensor(rt[:, 0, t, :], m12[:, t, 0, :], m12[:, t, 1, :], ALU.add)
            ins.then_inc(chosen_ready, 1)
            dve.wait_ge(gexp_ready, 1)
            own(dve.tensor_scalar(gsc[:, :, 2:3], gsc[:, :, 1:2], 1.0, None, ALU.add))
            own(dve.reciprocal(gsc[:, :, 3:4], gsc[:, :, 2:3]))
            own(dve.tensor_tensor(gsc[:, :, 4:5], gsc[:, :, 3:4], gsc[:, :, 1:2], ALU.mult))
            for t in range(NT):
                ins = dve.tensor_scalar(rt[:, 1, t, :], m12[:, t, 0, :], gsc[:, t, 3:4], None, ALU.mult)
            own(ins)
            for t in range(NT):
                ins = dve.scalar_tensor_tensor(out=rt[:, 1, t, :], in0=m12[:, t, 1, :], scalar=gsc[:, t, 4:5],
                                               in1=rt[:, 1, t, :], op0=ALU.mult, op1=ALU.add)
            own(ins)
            dve.wait_ge(pos_done, 1)
            dve.tensor_copy(pos[:, :, :], ps[:, 5, 0:16].rearrange("p (t e) -> p t e", t=NT))
            own(dve.tensor_scalar(ovf[:, 0, :], ps[:, 5, 16:24], float(P), None, ALU.is_gt))
            for t in range(NT):
                dve.tensor_copy(plan[:, 0:NE, t], pos[:, t, :])
                dve.tensor_copy(plan[:, 0:NE, 2 + t], rt[:, 0, t, :])
                dve.tensor_copy(plan[:, 0:NE, 4 + t], rt[:, 1, t, :])
            own(dve.tensor_copy(ovf[:, 1, :], ovf[:, 0, :]))
            for step in (1, 2, 4):
                src, dst = (1, 2) if step != 2 else (2, 1)
                dve.tensor_copy(ovf[:, dst, 0:step], ovf[:, src, 0:step])
                own(dve.tensor_tensor(ovf[:, dst, step:NE], ovf[:, src, step:NE], ovf[:, src, 0:NE - step], ALU.add))
            for j in range(OVERFLOW_PASSES):
                own(dve.scalar_tensor_tensor(out=ovf[:, 3 + j, :], in0=ovf[:, 2, :], scalar=float(j + 1),
                                             in1=ovf[:, 0, :], op0=ALU.is_equal, op1=ALU.mult))
            for j in range(OVERFLOW_PASSES):
                sel = ovf[:, 3 + j, :]
                for i, (src, shift) in enumerate([(pos[:, 0, :], -float(P)), (pos[:, 1, :], -float(P)),
                                                  (rt[:, 0, 0, :], 0.0), (rt[:, 0, 1, :], 0.0),
                                                  (rt[:, 1, 0, :], 0.0), (rt[:, 1, 1, :], 0.0),
                                                  (slots[:, 0:NE], 0.0)]):
                    dst = plan[:, NE + j, i:i + 1] if i < 6 else ovs[:, 1 + j:2 + j]
                    own(dve.tensor_tensor_reduce(ovf[:, 6, :], sel, src, 1.0, shift, ALU.mult, ALU.add, dst))
            dve.tensor_copy(ovs[:, 0:1], ovf[:, 2, NE - 1:NE]).then_inc(x_combined, 1)
            dve.wait_ge(x_combined, 1)
            dve.tensor_copy(route[0:1, :], ovs[0:1, 0:4]).then_inc(route_ready, 1)

            def choose(n):
                if not (known(n) and n == 0):
                    dve.wait_ge(pick_t_done, n)
                dve.tensor_copy(cur[:, :], plan[:, bass.ds(n, 1), :].rearrange("p a c -> p (a c)")).then_inc(cur_ready, 1)
                dve.wait_ge(cur_ready, n + 1)
                for t in range(NT):
                    ins = dve.tensor_scalar(pick[:, t, :], slots[:, :], cur[:, t:t + 1], cur[:, 2 + t:3 + t],
                                            ALU.is_equal, ALU.mult)
                ins.then_inc(pick_ready, 1)

            def gathered(n):
                for b in range(2):
                    dve.wait_ge(xe_hi, n * 2 + b + 1)
                    dve.tensor_tensor(xt_lo[:, 4 * b:4 * b + 4, 0:P], ps[:, 2 + b, :].rearrange("p (c t) -> p c t", c=4),
                                      xt_hi[:, 4 * b:4 * b + 4, 0:P].bitcast(F32), ALU.subtract).then_inc(xe_ready, 1)

            def expert(n, follows):
                q, nxt = n * GROUPS, HALF_MOE + 6 * GROUPS
                swiglu(HALF_MOE, q, 1, NT * GROUPS + n * GROUPS, (lambda: choose(n + 1)) if follows else None)
                if follows:
                    gathered(n + 1)
                    lo(nxt, q)
                    lo(nxt + 1, q)
                for nh in range(2):
                    c = slice(nh * NW, (nh + 1) * NW)
                    dve.wait_ge(y_h, n * 2 + nh + 1)
                    dve.scalar_tensor_tensor(out=y_lo[:, c], in0=ps[:, nh, :], scalar=gslot[:, 0:1],
                                             in1=y_hi[:, c].bitcast(F32), op0=ALU.mult, op1=ALU.subtract)\
                       .then_inc(y_ready, 1)
                if follows:
                    lo(nxt + 2, q)
                    lo(nxt + 3, q)
                for i, (nh, t) in enumerate([(nh, t) for nh in range(2) for t in range(NT)]):
                    xv = x[:, t, nh * NW:(nh + 1) * NW]
                    dve.wait_ge(combine_done, n * 4 + i + 1)
                    dve.tensor_tensor(xv, ps[:, combine_bank[nh][t], :], xv, ALU.add).then_inc(x_combined, 1)

            choose(0)
            gathered(0)
            lo(HALF_MOE + 2)
            lo(HALF_MOE + 3)
            with dve.Fori(0, NE - 1) as n:
                expert(n, True)
            expert(NE - 1, False)
            dve.wait_ge(route_ready, 1)
            over = dve.value_load(route[0:1, 0:1], min_val=0, max_val=OVERFLOW_PASSES)
            with dve.Fori(0, OVERFLOW_PASSES) as j:
                with dve.If(over > j):
                    lo(HALF_MOE, (j + NE) * GROUPS)
                    lo(HALF_MOE + 1, (j + NE) * GROUPS)
                    choose(j + NE)
                    gathered(j + NE)
                    lo(HALF_MOE + 2, (j + NE) * GROUPS)
                    lo(HALF_MOE + 3, (j + NE) * GROUPS)
                    expert(j + NE, False)
                dve.nop()
            mean(11, D, EPS)
            normed(6, row=fin_w[:, :], out_t=fin_ready)


_INS = ["x", "rel_bias_table", "mlstm_norm", "mlstm_w_in", "mlstm_conv_w", "mlstm_conv_b", "mlstm_b_igate",
        "mlstm_b_fgate", "mlstm_head_norm", "mlstm_w_out", "diff_norm", "diff_w_in", "diff_lambda_q1",
        "diff_lambda_k1", "diff_lambda_q2", "diff_lambda_k2", "diff_subln", "diff_w_out", "ffn_norm",
        "ffn_w_gate", "ffn_w_up", "ffn_w_down", "moe_norm", "moe_w_router", "moe_b_router", "moe_w_gate",
        "moe_w_up", "moe_w_down", "final_norm"]


def kernel(**inputs):
    import numpy as _np
    import concourse.bacc as _bacc
    from concourse import mybir as _mybir
    from concourse.bass_utils import run_bass_kernel_spmd as _run

    nc = _bacc.Bacc("TRN2", target_bir_lowering=False, num_devices=1)
    arrays, aps = {}, {}
    for name in _INS:
        a = _np.ascontiguousarray(inputs[name])
        arrays[f"in_{name}"] = a
        aps[name] = nc.dram_tensor(f"in_{name}", a.shape, _mybir.dt.from_np(a.dtype), kind="ExternalInput").ap()
    hot = _np.array(bucket_hot(), _np.float32)
    arrays["in_bucket_hot"] = hot
    aps["bucket_hot"] = nc.dram_tensor("in_bucket_hot", hot.shape, _mybir.dt.float32, kind="ExternalInput").ap()
    out = nc.dram_tensor("out_0", (1, 256, 1024), _mybir.dt.float32, kind="ExternalOutput").ap()
    bass_hybrid(nc, aps, out)
    r = _run(nc, [arrays], core_ids=[0])
    return r.results[0]["out_0"]
```

```python
import math
from contextlib import ExitStack

import concourse.bass as bass
from concourse import mybir

F32 = mybir.dt.float32
F32R = mybir.dt.float32r
I32 = mybir.dt.int32
U32 = mybir.dt.uint32
ALU = mybir.AluOpType
ACT = mybir.ActivationFunctionType
AX_X = mybir.AxisListType.X

P = 128
T = 256
NT = T // P
D = 1024
KC = D // P
NW = 512
F_FF = 3584
GROUPS = F_FF // NW
NE = 8
HALF = 2048
RAW_SLOTS = 6
SPLIT_SLOTS = 3
OVERFLOW_PASSES = 3
PASSES = NE + OVERFLOW_PASSES

ML_H, ML_DK, ML_DV = 4, 128, 256
ML_DVX = ML_DV + 1
ML_SCALE = ML_DK ** -0.5
CONV_W = 4
ROW = 384

DH, DHD, DDV = 8, 64, 128
DMAPS = 2 * DH
DSCALE = DHD ** -0.5
LAYER = 1
LAM_INIT = 0.8 - 0.6 * math.exp(-0.3 * LAYER)
BUCKETS, MAX_DIST = 32, 128
BIAS_W = 384
NEG = -1.0e30

EPS, SUB_EPS = 1e-6, 1e-5

HALF_Q, HALF_K, HALF_V, HALF_O, HALF_MOUT = 0, 2, 4, 8, 12
HALF_FFN = 16
HALF_DQ = HALF_FFN + 6 * GROUPS
HALF_DK, HALF_DVV, HALF_DOUT = HALF_DQ + 4, HALF_DQ + 8, HALF_DQ + 12
HALF_MOE = HALF_DQ + 16

C_MNORM, C_HNORM, C_FNORM, C_DNORM, C_ENORM, C_CONVB, C_CONVW, C_SUB = 0, 8, 16, 24, 32, 40, 48, 80
PRM = 81

PRM_LOADS = 8

S_RSTD, S_MS, S_ROOT, S_SQ = 0, 2, 4, 6


def bucket_of(n):
    half = BUCKETS // 2
    if n < half:
        return n
    return min(half + int(math.log(n / half) / math.log(MAX_DIST / half) * (BUCKETS - half) + 1e-9), BUCKETS - 1)


def bucket_hot():
    rows = [[0.0] * BIAS_W for _ in range(BUCKETS + 1)]
    for c in range(BIAS_W):
        n = T - 1 - c
        rows[bucket_of(n) if n >= 0 else BUCKETS][c] = 1.0
    return rows


def bass_hybrid(nc, A, out):
    ctx = ExitStack()
    with ctx:
        scope = [ctx]

        def sb(name, shape, dt=F32):
            return scope[-1].enter_context(nc.sbuf_tensor(name, shape, dt))

        def sem(name):
            return ctx.enter_context(nc.semaphore(name))

        x = sb("x", [P, NT, D])
        xs = sb("xs", [P, NT, D])
        xt_hi = sb("xt_hi", [P, KC, T], F32R)
        xt_lo = sb("xt_lo", [P, KC, T], F32R)
        raw = sb("raw", [P, RAW_SLOTS, HALF])
        w_hi = sb("w_hi", [P, SPLIT_SLOTS, HALF], F32R)
        w_lo = sb("w_lo", [P, SPLIT_SLOTS, HALF], F32R)
        gate_act = sb("gate_act", [P, NT, NW])
        hid = sb("hid", [P, NT, NW])
        hid_t_hi = sb("hid_t_hi", [P, 4, T], F32R)
        hid_t_lo = sb("hid_t_lo", [P, 4, T], F32R)
        ident = sb("ident", [P, P])
        ones = sb("ones", [P, P])
        prm = sb("prm", [PRM, P])
        col = sb("col", [P, PRM])
        small = sb("small", [P, 10])
        w8 = sb("w8", [P, 2, KC, 8])
        w8_hi = sb("w8_hi", [P, 2, KC, 8], F32R)
        w8_lo = sb("w8_lo", [P, 2, KC, 8], F32R)
        b_gate = sb("b_gate", [ML_H, 2])
        b_route = sb("b_route", [P, NE])
        lamv = sb("lamv", [P, 4, DHD])
        lamp = sb("lamp", [P, 2, DHD])
        lam = sb("lam", [P, 8])
        sub_w = sb("sub_w", [P, 1])
        diag = sb("diag", [P, NT, P])
        rrow = sb("rrow", [P, T])
        anti = sb("anti", [P, P])

        scope.append(ExitStack())
        qk = sb("qk", [P, 2 * ML_H, T])
        vx = sb("vx", [P, NT, ML_H, ML_DVX])
        sig_o = sb("sig_o", [P, NT, D])
        dec = sb("dec", [P, ML_H, ROW])
        prob = sb("prob", [P, ML_H, ROW])
        grow = sb("grow", [ML_H, 2 * T])
        g_abs = sb("g_abs", [ML_H, T])
        g_exp = sb("g_exp", [ML_H, T])
        g_ln = sb("g_ln", [ML_H, T])
        g_logf = sb("g_logf", [ML_H, T])
        g_cum = sb("g_cum", [ML_H, T])
        g_a = sb("g_a", [ML_H, T])
        g_max = sb("g_max", [ML_H, T])
        g_m = sb("g_m", [ML_H, T])
        g_em = sb("g_em", [ML_H, T])
        zrow = sb("zrow", [ML_H, T])
        headsel = sb("headsel", [ML_H, ML_H, P])
        acol = sb("acol", [P, NT, ML_H])
        em = sb("em", [P, ML_H * NT])
        mn = sb("mn", [P, 8, 8])
        scope.pop().close()

        scope.append(ExitStack())
        qz = sb("qz", [P, DH, 2, T])
        kt = sb("kt", [P, DH, T])
        vv = sb("vv", [P, NT, D])
        bias = sb("bias", [P, DMAPS, T])
        ex = gate_act[:, :, :].rearrange("p i (m k) -> p i m k", m=2)
        aw = sb("aw", [P, 2, T])
        awt = sb("awt", [P, 2, T])
        nmx = sb("nmx", [P, 3, 2])
        sm = sb("sm", [P, 2, 8])
        osq = [gate_act[:, 0, :], gate_act[:, 1, :], hid[:, 0, :], hid[:, 1, :]]
        oms = sb("oms", [P, 4, 2 * DH])
        scope.pop().close()

        scope.append(ExitStack())
        xn_hi = sb("xn_hi", [P, NT, D], F32R)
        xn_lo = sb("xn_lo", [P, NT, D], F32R)
        moe_w = sb("moe_w", [P, D])
        fin_w = sb("fin_w", [P, D])
        y_hi = sb("y_hi", [P, D], F32R)
        y_lo = sb("y_lo", [P, D], F32R)
        pick = sb("pick", [P, NT, P], F32R)
        pick_t = sb("pick_t", [P, T], F32R)
        slots_i = sb("slots_i", [P, P], I32)
        slots = sb("slots", [P, P])
        before = sb("before", [P, P])
        lg = sb("lg", [P, NT, NE])
        lrow = sb("lrow", [NE, T])
        top = sb("top", [P, NT, 8])
        topi = sb("topi", [P, NT, 8], U32)
        topf = sb("topf", [P, NT, 8])
        m12 = sb("m12", [P, NT, 2, NE])
        gsc = sb("gsc", [P, NT, 8])
        rt = sb("rt", [P, 2, NT, NE])
        pos = sb("pos", [P, NT, NE])
        ovf = sb("ovf", [P, 8, NE])
        ovs = sb("ovs", [P, 16])
        plan = sb("plan", [P, PASSES, 6])
        cur = sb("cur", [P, 6])
        gslot = sb("gslot", [P, 1])
        route = sb("route", [1, 4], I32)
        scope.pop().close()

        hot = gate_act[0:BUCKETS + 1, 0, 0:BIAS_W]
        tab = gate_act[0:BUCKETS + 1, 1, 0:DMAPS]
        brow = hid[0:DMAPS, 0, 0:BIAS_W]

        ps = ctx.enter_context(nc.psum_tensor("ps", [P, 8, NW], F32))
        skew = nc.dram_tensor("skew", (DMAPS, BIAS_W), F32, kind="Internal").ap()

        x_landed = [sem(f"x_landed{t}") for t in range(NT)]
        prm_landed = sem("prm_landed")
        w8_landed = sem("w8_landed")
        lam_landed = sem("lam_landed")
        rows_landed = sem("rows_landed")
        tab_landed = sem("tab_landed")
        brow_stored = sem("brow_stored")
        bias_landed = sem("bias_landed")
        out_stored = sem("out_stored")
        raw_landed = [sem(f"raw_landed{s}") for s in range(RAW_SLOTS)]
        hi_ready = sem("hi_ready")
        lo_ready = sem("lo_ready")
        half_used = sem("half_used")
        const_step = sem("const_step")
        act_self = sem("act_self")
        dve_self = sem("dve_self")
        col_t = sem("col_t")
        col_ready = sem("col_ready")
        brow_done = sem("brow_done")
        brow_ready = sem("brow_ready")
        ss_ready = sem("ss_ready")
        ms_ready = sem("ms_ready")
        root_ready = sem("root_ready")
        xs_ready = sem("xs_ready")
        t_done = sem("t_done")
        t_hi = sem("t_hi")
        xt_ready = sem("xt_ready")
        w8h_ready = sem("w8h_ready")
        w8_ready = sem("w8_ready")
        conv_ready = sem("conv_ready")
        qk_ready = sem("qk_ready")
        grow_done = sem("grow_done")
        grow_ready = sem("grow_ready")
        gabs_ready = sem("gabs_ready")
        gln_ready = sem("gln_ready")
        gm_ready = sem("gm_ready")
        gem_ready = sem("gem_ready")
        gbc_done = sem("gbc_done")
        acol_ready = sem("acol_ready")
        v_ready = sem("v_ready")
        o_ready = sem("o_ready")
        z_ready = sem("z_ready")
        e_ready = sem("e_ready")
        mask_ready = sem("mask_ready")
        st_done = sem("st_done")
        prob_ready = sem("prob_ready")
        pv_done = sem("pv_done")
        den_read = sem("den_read")
        x_added = sem("x_added")
        silu_ready = sem("silu_ready")
        hid_ready = sem("hid_ready")
        hid_t_done = sem("hid_t_done")
        hid_t_h = sem("hid_t_h")
        hid_t_ready = sem("hid_t_ready")
        dq_ready = sem("dq_ready")
        dk_ready = sem("dk_ready")
        dv_ready = sem("dv_ready")
        down_half = sem("down_half")
        recip_ready = sem("recip_ready")
        diag_ready = sem("diag_ready")
        rrow_done = sem("rrow_done")
        rrow_ready = sem("rrow_ready")
        qz_zeroed = sem("qz_zeroed")
        logit_done = sem("logit_done")
        max_ready = sem("max_ready")
        exp_ready = sem("exp_ready")
        a_ready = sem("a_ready")
        at_done = sem("at_done")
        at_ready = sem("at_ready")
        opv_done = sem("opv_done")
        osq_ready = sem("osq_ready")
        oms_ready = sem("oms_ready")
        oroot_ready = sem("oroot_ready")
        lam_dot = sem("lam_dot")
        lam_exp = sem("lam_exp")
        xn_h = sem("xn_h")
        xn_ready = sem("xn_ready")
        router_done = sem("router_done")
        lrow_ready = sem("lrow_ready")
        lcol_done = sem("lcol_done")
        gap_ready = sem("gap_ready")
        gexp_ready = sem("gexp_ready")
        chosen_ready = sem("chosen_ready")
        pos_done = sem("pos_done")
        route_ready = sem("route_ready")
        cur_ready = sem("cur_ready")
        pick_ready = sem("pick_ready")
        gather_done = sem("gather_done")
        xe_hi = sem("xe_hi")
        xe_ready = sem("xe_ready")
        pick_t_done = sem("pick_t_done")
        pick_t_ready = sem("pick_t_ready")
        y_h = sem("y_h")
        y_ready = sem("y_ready")
        combine_done = sem("combine_done")
        x_combined = sem("x_combined")
        fin_ready = sem("fin_ready")

        block = ctx.enter_context(nc.Block())

        def at(s, q=0):
            return q * RAW_SLOTS + s

        BANKS_A, BANKS_B = [6, 7, 0, 2], [4, 5, 3, 1]
        T_BANKS = [[0, 1, 2, 3], [5, 6, 7, 0], [1, 2, 1, 2], [4, 5, 4, 5], [4, 5, 6, 7], [4, 5, 6, 7]]
        combine_bank = [[2, 3], [5, 7]]

        def known(v):
            return isinstance(v, int)

        def wait_from(eng, s, v):
            if not (known(v) and v <= 0):
                eng.wait_ge(s, v)

        x_in = A["x"].rearrange("a (t p) d -> (a p) t d", p=P)
        out_v = out.rearrange("a (t p) d -> (a p) t d", p=P)

        @block.sync
        def _(sp):
            def load(s, q, src):
                wait_from(sp, lo_ready, at(s, q) - RAW_SLOTS + 1)
                slot = s % RAW_SLOTS
                n = src.shape[1]
                sp.dma_start(raw[:, slot, :].rearrange("p (k n) -> p k n", k=n), src)\
                  .then_inc(raw_landed[slot], 16)

            def wide(w, k0, n0):
                return w.rearrange("(k p) n -> p k n", p=P)[:, k0:k0 + 4, n0:n0 + NW]

            def slabs(s, w, n_slabs):
                for n in range(n_slabs):
                    for hh in range(2):
                        load(s + 2 * n + hh, 0, wide(w, 4 * hh, n * NW))

            def swiglu(s, q, wg, wu, wd):
                def gate_up(s, q, f):
                    for w in (wg, wu):
                        for hh in range(2):
                            load(s, q, w[:, 4 * hh:4 * hh + 4, bass.ds(f * NW, NW)])
                            s += 1
                    return s

                def down(s, q, f):
                    for hh in range(2):
                        load(s + hh, q, wd[:, bass.ds(f * 4 + 2 * hh, 2), :])

                gate_up(s, q, 0)
                with sp.Fori(1, GROUPS) as f:
                    nxt = gate_up(s + 4, q + (f - 1), f)
                    down(nxt, q + (f - 1), f - 1)
                down(s + 4 + 6 * (GROUPS - 1), q, GROUPS - 1)

            for t in range(NT):
                sp.dma_start(x[:, t, :], x_in[:, t, :]).then_inc(x_landed[t], 16)
            sp.wait_ge(prm_landed, 16 * PRM_LOADS)
            slabs(HALF_Q, A["mlstm_w_in"][0], 6)
            slabs(HALF_MOUT, A["mlstm_w_out"][0], 2)
            swiglu(HALF_FFN, 0, A["ffn_w_gate"][0].rearrange("(k p) f -> p k f", p=P),
                   A["ffn_w_up"][0].rearrange("(k p) f -> p k f", p=P),
                   A["ffn_w_down"][0].rearrange("(c p) d -> p c d", p=P))
            slabs(HALF_DQ, A["diff_w_in"][0], 6)
            slabs(HALF_DOUT, A["diff_w_out"][0], 2)

            mg = A["moe_w_gate"][0].rearrange("e (k p) f -> e p k f", p=P)
            mu = A["moe_w_up"][0].rearrange("e (k p) f -> e p k f", p=P)
            md = A["moe_w_down"][0].rearrange("e (c p) d -> e p c d", p=P)

            def expert(n, e):
                swiglu(HALF_MOE, n * GROUPS, mg[e, :, :, :], mu[e, :, :, :], md[e, :, :, :])

            with sp.Fori(0, NE) as n:
                expert(n, n)
            sp.wait_ge(route_ready, 1)
            over = sp.value_load(route[0:1, 0:1], min_val=0, max_val=OVERFLOW_PASSES)
            with sp.Fori(0, OVERFLOW_PASSES) as j:
                with sp.If(over > j):
                    e = sp.value_load(route[0:1, bass.ds(j + 1, 1)], min_val=0, max_val=NE - 1)
                    expert(j + NE, e)
                sp.nop()
            for t in range(NT):
                sp.wait_ge(fin_ready, t + 1)
                sp.dma_start(out_v[:, t, :], xs[:, t, :]).then_inc(out_stored, 16)
            sp.wait_ge(out_stored, 16 * NT)

        @block.gpsimd
        def _(pool):
            pool.memset(ident[:, :], 0.0).then_inc(const_step, 1)
            pool.memset(anti[:, :], 0.0).then_inc(const_step, 1)
            pool.memset(ones[:, :], 1.0).then_inc(const_step, 1)
            pool.memset(tab, NEG).then_inc(const_step, 1)
            pool.wait_ge(const_step, 1)
            pool.affine_select(out=ident[:, :], in_=ident[:, :], compare_op=ALU.not_equal, fill=1.0, base=0,
                               pattern=[[-1, P]], channel_multiplier=1).then_inc(const_step, 1)
            pool.wait_ge(const_step, 4)
            pool.affine_select(out=anti[:, :], in_=anti[:, :], compare_op=ALU.not_equal, fill=1.0,
                               base=-(P - 1), pattern=[[1, P]], channel_multiplier=1).then_inc(const_step, 1)
            pool.dma_start(hot, A["bucket_hot"]).then_inc(tab_landed, 16)
            pool.dma_start(tab[0:BUCKETS, :], A["rel_bias_table"]).then_inc(tab_landed, 16)
            for i, name in enumerate(("diff_lambda_q1", "diff_lambda_k1", "diff_lambda_q2", "diff_lambda_k2")):
                pool.dma_start(lamv[:, i, :], A[name][0].partition_broadcast(P)).then_inc(lam_landed, 16)
            pool.memset(vx[:, :, :, ML_DV:ML_DVX], 1.0).then_inc(const_step, 1)
            pool.memset(headsel[:, :, :], 0.0).then_inc(const_step, 1)
            pool.memset(zrow[:, :], 0.0).then_inc(const_step, 1)
            pool.wait_ge(const_step, 8)
            pool.affine_select(out=headsel[:, :, :], in_=headsel[:, :, :], compare_op=ALU.not_equal, fill=1.0,
                               base=0, pattern=[[-1, ML_H], [0, P]], channel_multiplier=1)\
                .then_inc(const_step, 1)
            pool.wait_ge(brow_ready, 1)
            pool.dma_start(skew, brow).then_inc(brow_stored, 16)
            pool.wait_ge(e_ready, ML_H)
            for c0 in (0, T):
                d = dec[:, :, c0:c0 + P]
                pool.affine_select(out=d, in_=d, compare_op=ALU.is_ge, fill=0.0, base=0,
                                   pattern=[[0, ML_H], [1, P]], channel_multiplier=-1).then_inc(mask_ready, 1)
            pool.wait_ge(xs_ready, 2 + 2)
            pool.memset(qz[:, :, :, :], 0.0).then_inc(qz_zeroed, 1)
            pool.wait_ge(brow_stored, 16)
            pool.dma_start(bias[:, :, :], bass.AP(skew.tensor, 0, [[1, P], [BIAS_W, DMAPS], [1, T]]))\
                .then_inc(bias_landed, 16)
            pool.wait_ge(xs_ready, 2 * 3)
            pool.dma_start(moe_w[:, :], A["moe_norm"][0].partition_broadcast(P)).then_inc(rows_landed, 16)
            pool.dma_start(fin_w[:, :], A["final_norm"].partition_broadcast(P)).then_inc(rows_landed, 16)
            pool.iota(slots_i[:, :], pattern=[[1, P]], base=0, channel_multiplier=0).then_inc(const_step, 1)
            pool.memset(before[:, :], 1.0).then_inc(const_step, 1)
            pool.wait_ge(const_step, 12)
            pool.affine_select(out=before[:, :], in_=before[:, :], compare_op=ALU.is_gt, fill=0.0, base=0,
                               pattern=[[1, P]], channel_multiplier=-1).then_inc(const_step, 1)
            pool.tensor_copy(slots[:, :], slots_i[:, :]).then_inc(const_step, 1)

        @block.tensor
        def _(pe):
            def three(out_ap, s_hi, s_lo, m_hi, m_lo, start, stop):
                pe.matmul(out_ap, s_hi, m_hi, start=start, stop=False)
                pe.matmul(out_ap, s_hi, m_lo, start=False, stop=False)
                return pe.matmul(out_ap, s_lo, m_hi, start=False, stop=stop)

            def half(s, q, k):
                pe.wait_ge(lo_ready, at(s, q) + 1)
                slot = s % SPLIT_SLOTS
                return [w[:, slot, :].rearrange("p (k n) -> p k n", k=k) for w in (w_hi, w_lo)]

            def tokens_by_columns(s, q, banks, ready=None, between=None):
                for hh in range(2):
                    if hh and between:
                        between()
                    if ready:
                        ready(hh)
                    wh, wl = half(s + hh, q, 4)
                    for k in range(4):
                        kk = 4 * hh + k
                        for t, b in enumerate(banks):
                            mm = three(ps[:, b, :], xt_hi[:, kk, t * P:(t + 1) * P], xt_lo[:, kk, t * P:(t + 1) * P],
                                       wh[:, k, :], wl[:, k, :], kk == 0, kk == KC - 1)
                    mm.then_inc(half_used, 1)

            def columns_by_tokens(s, banks, ready=None, between=None):
                for hh in range(2):
                    if hh and between:
                        between()
                    if ready:
                        ready(hh)
                    wh, wl = half(s + hh, 0, 4)
                    for k in range(4):
                        kk = 4 * hh + k
                        for c, b in enumerate(banks):
                            mm = three(ps[:, b, 0:T], wh[:, k, c * P:(c + 1) * P], wl[:, k, c * P:(c + 1) * P],
                                       xt_hi[:, kk, :], xt_lo[:, kk, :], kk == 0, kk == KC - 1)
                    mm.then_inc(half_used, 1)

            def transposes(n, src, banks, pairs):
                for i in pairs:
                    for c in (2 * i, 2 * i + 1):
                        for t in range(NT):
                            o = (c % 2) * T + t * P
                            mm = pe.transpose(ps[:, banks[i], o:o + P], src[:, t, c * P:(c + 1) * P], ident[:, :])
                    mm.then_inc(t_done, 1)

            def transpose_xs(n, u):
                for nh in range(2):
                    pe.wait_ge(xs_ready, 2 * u + nh + 1)
                    transposes(n, xs, T_BANKS[n], (2 * nh, 2 * nh + 1))

            def transpose_x(n, nh, added):
                pe.wait_ge(x_added, added)
                transposes(n, x, T_BANKS[n], (2 * nh, 2 * nh + 1))

            def xt_wait(n):
                return lambda hh: pe.wait_ge(xt_ready, 4 * n + 2 * hh + 2)

            def narrow(which, c0, n, out_ap, chunks):
                for k in chunks:
                    mm = three(out_ap, w8_hi[:, which, k, c0:c0 + n], w8_lo[:, which, k, c0:c0 + n],
                               xt_hi[:, k, :], xt_lo[:, k, :], k == 0, k == KC - 1)
                return mm

            def dense_last(s):
                halves = [half(s + hh, 0, 2) for hh in range(2)]
                for n in range(2):
                    for hh, (wh, wl) in enumerate(halves):
                        if n and hh:
                            transpose_x(3, 0, 6)
                        for c in range(2):
                            cc = 2 * hh + c
                            for t in range(NT):
                                mm = three(ps[:, 2 * t + n, :], hid_t_hi[:, cc, t * P:(t + 1) * P],
                                           hid_t_lo[:, cc, t * P:(t + 1) * P],
                                           wh[:, c, n * NW:(n + 1) * NW], wl[:, c, n * NW:(n + 1) * NW],
                                           False, cc == 3)
                        if n:
                            mm.then_inc(half_used, 1)
                    if not n:
                        mm.then_inc(down_half, 1)

            def swiglu(s, q, tiles, tb, after_up=None, before_last=None, last_down=None):
                def down(s, q, first, last):
                    for hh in range(2):
                        wh, wl = half(s + hh, q, 2)
                        for c in range(2):
                            cc = 2 * hh + c
                            for t in range(tiles):
                                for n in range(2):
                                    mm = three(ps[:, 2 * t + n, :], hid_t_hi[:, cc, t * P:(t + 1) * P],
                                               hid_t_lo[:, cc, t * P:(t + 1) * P],
                                               wh[:, c, n * NW:(n + 1) * NW], wl[:, c, n * NW:(n + 1) * NW],
                                               first and cc == 0, last and cc == 3)
                        mm.then_inc(half_used, 1)

                def turn(f):
                    for t in range(tiles):
                        pe.wait_ge(hid_ready, tb + f * tiles + t + 1)
                        for c in range(4):
                            mm = pe.transpose(ps[:, 6 + t, c * P:(c + 1) * P], hid[:, t, c * P:(c + 1) * P],
                                              ident[:, :])
                        mm.then_inc(hid_t_done, 1)

                gate_banks, up_banks = list(range(4, 4 + tiles)), list(range(6, 6 + tiles))

                def group(s, q, f, first):
                    tokens_by_columns(s, q, gate_banks)
                    pe.wait_ge(hid_t_ready, tb + f * tiles)
                    tokens_by_columns(s + 2, q, up_banks)
                    down(s + 4, q, first, False)
                    turn(f)

                tokens_by_columns(s + 2, q, up_banks)
                if after_up:
                    after_up()
                turn(0)
                group(s + 4, q, 1, True)
                with pe.Fori(2, GROUPS) as f:
                    group(s + 4, q + (f - 1), f, False)
                if before_last:
                    before_last()
                pe.wait_ge(hid_t_ready, tb + GROUPS * tiles)
                if last_down:
                    last_down(s + 4 + 6 * (GROUPS - 1))
                else:
                    down(s + 4 + 6 * (GROUPS - 1), q, False, True)

            pe.wait_ge(const_step, 6)
            pe.wait_ge(prm_landed, 16 * PRM_LOADS)
            pe.transpose(ps[:, 7, 0:PRM], prm[:, :], ident[0:PRM, 0:PRM]).then_inc(col_t, 1)

            transpose_xs(0, 0)
            pe.wait_ge(col_ready, 1)
            columns_by_tokens(HALF_Q, [4, 5, 6, 7], xt_wait(0))
            columns_by_tokens(HALF_K, [0, 1, 2, 3])
            pe.wait_ge(w8_ready, 1)
            pe.wait_ge(conv_ready, 1)
            for g in range(2):
                mm = narrow(0, g * ML_H, ML_H, ps[0:ML_H, 4, g * T:(g + 1) * T], range(KC))
            mm.then_inc(grow_done, 1)
            pe.wait_ge(conv_ready, 3)
            tokens_by_columns(HALF_V, 0, [5, 6])
            pe.wait_ge(conv_ready, 5)
            tokens_by_columns(HALF_V + 2, 0, [7, 0])
            pe.wait_ge(v_ready, 1)
            tokens_by_columns(HALF_O, 0, [5, 6])
            pe.wait_ge(tab_landed, 32)
            pe.wait_ge(grow_ready, 2)
            pe.matmul(ps[0:DMAPS, 4, 0:BIAS_W], tab, hot, start=True, stop=True).then_inc(brow_done, 1)
            pe.wait_ge(conv_ready, 8)
            pe.wait_ge(const_step, 10)
            pe.wait_ge(gm_ready, 1)
            for h in range(ML_H):
                pe.matmul(ps[:, 1 + h // 2, (h % 2) * T:(h % 2 + 1) * T], headsel[:, h, :], g_max[:, :],
                          start=True, stop=True)
            pe.wait_ge(gem_ready, 1)
            for i, g in enumerate((g_a, g_em)):
                for t in range(NT):
                    o = i * 8 + t * ML_H
                    mm = pe.transpose(ps[:, 3, o:o + ML_H], g[:, t * P:(t + 1) * P], ident[0:ML_H, 0:ML_H])
            mm.then_inc(gbc_done, 1)
            pe.wait_ge(v_ready, 2)
            tokens_by_columns(HALF_O + 2, 0, [7, 0])
            pe.wait_ge(qk_ready, 8)
            pe.wait_ge(z_ready, ML_H)
            pe.wait_ge(brow_ready, 1)
            st_bank = [4, 3, 1, 2]
            for h in range(ML_H):
                b = st_bank[h]
                pe.matmul(ps[:, b, 0:T], qk[:, ML_H + h, 0:P], qk[:, h, :], start=True, stop=True)
                pe.matmul(ps[:, b, T:ROW], qk[:, ML_H + h, P:T], qk[:, h, P:T], start=True, stop=True)\
                  .then_inc(st_done, 1)
            for h in range(ML_H):
                pe.wait_ge(prob_ready, ML_H if h >= 2 else h + 1)
                if h < 2:
                    pe.wait_ge(o_ready, h + 1)
                b0, b1 = (5 + 2 * h) % 8, (6 + 2 * h) % 8
                pe.matmul(ps[:, b0, 0:ML_DVX], prob[:, h, 0:P], vx[:, 0, h, :], start=True, stop=True)
                pe.matmul(ps[:, b1, 0:ML_DVX], prob[:, h, P:T], vx[:, 0, h, :], start=True, stop=False)
                mm = pe.matmul(ps[:, b1, 0:ML_DVX], prob[:, h, T:ROW], vx[:, 1, h, :], start=False, stop=True)
            mm.then_inc(pv_done, 1)
            transpose_xs(1, 1)
            tokens_by_columns(HALF_MOUT, 0, [1, 2], xt_wait(1))
            tokens_by_columns(HALF_MOUT + 2, 0, [0, 3], between=lambda: transpose_x(2, 0, 2))

            tokens_by_columns(HALF_FFN, 0, [4, 5], xt_wait(2), between=lambda: transpose_x(2, 1, 4))
            swiglu(HALF_FFN, 0, NT, 0, last_down=dense_last)

            def row_of_roots():
                transpose_x(3, 1, 8)
                pe.wait_ge(diag_ready, 1)
                pe.matmul(ps[:, 1, 0:T], ones[:, :], diag[:, :, :].rearrange("p t k -> p (t k)"),
                          start=True, stop=True).then_inc(rrow_done, 1)

            columns_by_tokens(HALF_DQ, BANKS_A, xt_wait(3), between=row_of_roots)
            pe.wait_ge(rrow_ready, 1)
            columns_by_tokens(HALF_DQ + 2, BANKS_B)
            pe.wait_ge(dq_ready, 1)
            columns_by_tokens(HALF_DK, BANKS_A)
            pe.wait_ge(dq_ready, 2)
            columns_by_tokens(HALF_DK + 2, BANKS_B)
            pe.wait_ge(dk_ready, 1)
            tokens_by_columns(HALF_DVV, 0, [6, 7])
            tokens_by_columns(HALF_DVV + 2, 0, [0, 2])
            pe.wait_ge(dk_ready, 2)
            pe.wait_ge(bias_landed, 16)
            units = [(h, t) for h in range(DH) for t in range(NT)]

            def logits(i):
                h, t = units[i]
                if i == 2:
                    pe.wait_ge(dv_ready, 1)
                if i >= 3:
                    pe.wait_ge(exp_ready, i - 2)
                for m in range(2):
                    o = ps[:, 4 + i % 3, m * T:m * T + (t + 1) * P]
                    pe.matmul(o, anti[:, :], bias[:, 2 * h + m, (1 - t) * P:T], start=True, stop=False)
                    mm = pe.matmul(o, qz[:, h, m, t * P:(t + 1) * P], kt[:, h, 0:(t + 1) * P],
                                   start=False, stop=True)
                mm.then_inc(logit_done, 1)

            def turn_a(i):
                h, t = units[i]
                pe.wait_ge(a_ready, i + 1)
                if i >= 1:
                    pe.wait_ge(at_ready, i)
                for b in range(t + 1):
                    mm = pe.transpose(ps[:, 7, b * P:(b + 1) * P], aw[:, i % 2, b * P:(b + 1) * P],
                                      ident[:, :])
                mm.then_inc(at_done, 1)

            def values(i):
                h, t = units[i]
                pe.wait_ge(at_ready, i + 1)
                if i == 0:
                    pe.wait_ge(dv_ready, 2)
                c = (h % 4) * P
                for b in range(t + 1):
                    mm = pe.matmul(ps[:, 2 * t + h // 4, c:c + P], awt[:, i % 2, b * P:(b + 1) * P],
                                   vv[:, b, h * DDV:(h + 1) * DDV], start=(b == 0), stop=(b == t))
                mm.then_inc(opv_done, 1)

            logits(0)
            logits(1)
            for i in range(len(units)):
                if i + 2 < len(units):
                    logits(i + 2)
                turn_a(i)
                if i >= 1:
                    values(i - 1)
            values(len(units) - 1)
            transpose_xs(4, 2)
            tokens_by_columns(HALF_DOUT, 0, [0, 2], xt_wait(4))
            tokens_by_columns(HALF_DOUT + 2, 0, [1, 3], between=lambda: transpose_x(5, 0, 10))

            xt_wait(5)(0)
            narrow(1, 0, NE, ps[0:NE, 0, 0:T], range(KC // 2))
            transpose_x(5, 1, 12)
            xt_wait(5)(1)
            narrow(1, 0, NE, ps[0:NE, 0, 0:T], range(KC // 2, KC)).then_inc(router_done, 1)
            pe.wait_ge(lrow_ready, 1)
            for t in range(NT):
                mm = pe.transpose(ps[:, 5, t * NE:(t + 1) * NE], lrow[:, t * P:(t + 1) * P], ident[0:NE, 0:NE])
            mm.then_inc(lcol_done, 1)
            pe.wait_ge(chosen_ready, 1)
            pe.wait_ge(const_step, 14)
            pe.matmul(ps[:, 6, 0:8], before[:, :], rt[:, 0, 0, :], start=True, stop=True)
            pe.matmul(ps[:, 6, 8:16], before[:, :], rt[:, 0, 1, :], start=True, stop=False)
            pe.matmul(ps[:, 6, 8:16], ones[:, :], rt[:, 0, 0, :], start=False, stop=True)
            pe.matmul(ps[:, 6, 16:24], ones[:, :], rt[:, 0, 0, :], start=True, stop=False)
            pe.matmul(ps[:, 6, 16:24], ones[:, :], rt[:, 0, 1, :], start=False, stop=True).then_inc(pos_done, 1)
            pe.wait_ge(xn_ready, NT)

            def gather(n):
                pe.wait_ge(pick_ready, n + 1)
                for b in range(2):
                    for c in range(4):
                        f0 = (4 * b + c) * P
                        for i, (xn, t) in enumerate([(xn, t) for xn in (xn_hi, xn_lo) for t in range(NT)]):
                            mm = pe.matmul(ps[:, 2 + b, c * P:(c + 1) * P], xn[:, t, f0:f0 + P], pick[:, t, :],
                                           start=(i == 0), stop=(i == 3))
                    mm.then_inc(gather_done, 1)

            def first_gate(n, s, q):
                tokens_by_columns(s, q, [4], lambda hh: pe.wait_ge(xe_ready, n * 2 + hh + 1))

            def transpose_pick(n):
                pe.wait_ge(x_combined, n * 4 + 1)
                for t in range(NT):
                    pe.transpose(ps[:, 7, t * P:(t + 1) * P], pick[:, t, :].bitcast(F32), ident[:, :])
                for t in range(NT):
                    mm = pe.matmul(ps[:, 7, T:T + 1], pick[:, t, :].bitcast(F32), cur[:, 4 + t:5 + t],
                                   start=(t == 0), stop=(t == NT - 1))
                mm.then_inc(pick_t_done, 1)

            def combine(n):
                pe.wait_ge(pick_t_ready, n + 1)
                for nh in range(2):
                    pe.wait_ge(y_ready, n * 2 + nh + 1)
                    for t in range(NT):
                        for y in (y_hi, y_lo):
                            mm = pe.matmul(ps[:, combine_bank[nh][t], :], pick_t[:, t * P:(t + 1) * P],
                                           y[:, nh * NW:(nh + 1) * NW], start=(y is y_hi), stop=(y is y_lo))
                        mm.then_inc(combine_done, 1)

            def expert(n, follows):
                swiglu(HALF_MOE, n * GROUPS, 1, NT * GROUPS + n * GROUPS,
                       after_up=lambda: transpose_pick(n),
                       before_last=(lambda: gather(n + 1)) if follows else None)
                if follows:
                    first_gate(n + 1, HALF_MOE + 6 * GROUPS, n * GROUPS)
                combine(n)

            gather(0)
            first_gate(0, HALF_MOE, 0)
            with pe.Fori(0, NE - 1) as n:
                expert(n, True)
            expert(NE - 1, False)
            pe.wait_ge(route_ready, 1)
            over = pe.value_load(route[0:1, 0:1], min_val=0, max_val=OVERFLOW_PASSES)
            with pe.Fori(0, OVERFLOW_PASSES) as j:
                with pe.If(over > j):
                    gather(j + NE)
                    first_gate(j + NE, HALF_MOE, (j + NE) * GROUPS)
                    expert(j + NE, False)
                pe.nop()

        @block.scalar
        def _(act):
            self_n = [0]

            def mine(ins):
                ins.then_inc(act_self, 1)
                self_n[0] += 1
                act.wait_ge(act_self, self_n[0])

            def hi(s, q=0):
                slot = s % RAW_SLOTS
                act.wait_ge(raw_landed[slot], (q + (s // RAW_SLOTS + 1)) * 16)
                wait_from(act, half_used, at(s, q) - SPLIT_SLOTS + 1)
                act.activation(w_hi[:, s % SPLIT_SLOTS, :], raw[:, slot, :], ACT.Copy).then_inc(hi_ready, 1)

            def squares(nh):
                c = slice(nh * NW, (nh + 1) * NW)
                for t in range(NT):
                    act.activation(xs[:, t, c], x[:, t, c], ACT.Square,
                                   accum_out=small[:, S_SQ + 2 * t + nh:S_SQ + 2 * t + nh + 1]).then_inc(ss_ready, 1)

            def root(n):
                act.wait_ge(ms_ready, n + 1)
                act.activation(small[:, S_ROOT:S_ROOT + 2], small[:, S_MS:S_MS + 2], ACT.Sqrt).then_inc(root_ready, 1)

            def evac_xt(n, c0, pairs=range(4), scale=None):
                for i in pairs:
                    act.wait_ge(t_done, 4 * n + i + 1)
                    for j in range(2):
                        c = 2 * i + j
                        w = scale if scale is not None else col[:, c0 + c:c0 + c + 1]
                        ins = act.activation(xt_hi[:, c, :], ps[:, T_BANKS[n][i], j * T:(j + 1) * T], ACT.Copy, scale=w)
                    ins.then_inc(t_hi, 1)

            def swiglu(s, q, tiles, tb, after_gate=None, scale=lambda t: 1.0):
                def evac(f):
                    for t in range(tiles):
                        act.wait_ge(hid_t_done, tb + tiles * f + t + 1)
                        act.activation(hid_t_hi[:, :, t * P:(t + 1) * P],
                                       ps[:, 6 + t, :].rearrange("p (c t) -> p c t", c=4), ACT.Copy)\
                           .then_inc(hid_t_h, 1)

                def gate(s, q):
                    act.wait_ge(half_used, at(s, q) + 2)
                    for t in range(tiles):
                        act.activation(gate_act[:, t, :], ps[:, 4 + t, :], ACT.Silu, scale=scale(t)).then_inc(silu_ready, 1)

                gate(s, q)
                for i in (4, 5):
                    hi(s + i, q)
                if after_gate:
                    after_gate()
                with act.Fori(1, GROUPS) as f:
                    q1, s1 = q + (f - 1), s + 4
                    evac(f - 1)
                    for i in (2, 3):
                        hi(s1 + i, q1)
                    gate(s1, q1)
                    for i in (4, 5, 6, 7):
                        hi(s1 + i, q1)
                evac(GROUPS - 1)

            prm_rows = [("mlstm_norm", C_MNORM), ("mlstm_head_norm", C_HNORM), ("ffn_norm", C_FNORM),
                        ("diff_norm", C_DNORM), ("moe_norm", C_ENORM), ("mlstm_conv_b", C_CONVB)]
            for name, r in prm_rows:
                act.dma_start(prm[r:r + 8, :], A[name][0].rearrange("(c p) -> c p", p=P)).then_inc(prm_landed, 16)
            act.dma_start(prm[C_CONVW:C_CONVW + 32, :], A["mlstm_conv_w"][0].rearrange("w (c p) -> (w c) p", p=P))\
               .then_inc(prm_landed, 16)
            act.dma_start(prm[C_SUB:C_SUB + 1, :], A["diff_subln"]).then_inc(prm_landed, 16)
            act.dma_start(w8[:, 0, :, :], A["mlstm_w_in"][0].rearrange("(k p) n -> p k n", p=P)[:, :, 3 * D:3 * D + 8])\
               .then_inc(w8_landed, 16)
            act.dma_start(w8[:, 1, :, :], A["moe_w_router"][0].rearrange("(k p) n -> p k n", p=P))\
               .then_inc(w8_landed, 16)
            act.dma_start(b_gate[:, 0:1], A["mlstm_b_igate"].rearrange("a h -> h a")).then_inc(w8_landed, 16)
            act.dma_start(b_gate[:, 1:2], A["mlstm_b_fgate"].rearrange("a h -> h a")).then_inc(w8_landed, 16)
            act.dma_start(b_route[:, :], A["moe_b_router"][0].partition_broadcast(P)).then_inc(w8_landed, 16)

            act.preload_act_table(ACT.Sqrt)
            for t in range(NT):
                act.wait_ge(x_landed[t], 16)
                act.activation(xs[:, t, :], x[:, t, :], ACT.Square, accum_out=small[:, S_SQ + 2 * t:S_SQ + 2 * t + 1])\
                   .then_inc(ss_ready, 1)
            root(0)
            act.wait_ge(w8_landed, 16 * 5)
            act.activation(w8_hi[:, :, :, :], w8[:, :, :, :], ACT.Copy).then_inc(w8h_ready, 1)
            act.wait_ge(col_ready, 1)
            hi(0)
            evac_xt(0, C_MNORM, (0, 1))
            hi(1)
            evac_xt(0, C_MNORM, (2, 3))
            hi(2)
            hi(3)

            def silu_qk(c):
                act.wait_ge(conv_ready, c + 1)
                act.activation(qk[:, c, :], qk[:, c, :], ACT.Silu).then_inc(qk_ready, 1)

            for c in (0, 1):
                silu_qk(c)
            hi(4)
            for c in (2, 3):
                silu_qk(c)
            hi(5)
            hi(6)
            for c in (4, 5):
                silu_qk(c)
            hi(7)
            for c in (6, 7):
                silu_qk(c)
            hi(8)

            def evac_v(n, banks):
                act.wait_ge(half_used, HALF_V + 2 * n + 2)
                for t, b in enumerate(banks):
                    ins = act.activation(vx[:, t, 2 * n:2 * n + 2, 0:ML_DV],
                                         ps[:, b, :].rearrange("p (h v) -> p h v", h=2), ACT.Copy)
                ins.then_inc(v_ready, 1)

            def evac_o(n, banks):
                act.wait_ge(half_used, HALF_O + 2 * n + 2)
                for t, b in enumerate(banks):
                    ins = act.activation(sig_o[:, t, n * NW:(n + 1) * NW], ps[:, b, :], ACT.Sigmoid)
                ins.then_inc(o_ready, 1)

            evac_v(0, (5, 6))
            hi(9)
            act.wait_ge(gabs_ready, 1)
            mine(act.activation(g_exp[:, :], g_abs[:, :], ACT.Exp, scale=-1.0))
            act.activation(g_ln[:, :], g_exp[:, :], ACT.Ln, bias=1.0).then_inc(gln_ready, 1)
            hi(10)
            evac_v(1, (7, 0))
            act.wait_ge(gm_ready, 2)
            act.activation(g_em[:, :], g_m[:, :], ACT.Exp, scale=-1.0).then_inc(gem_ready, 1)
            hi(11)
            hi(12)
            evac_o(0, (5, 6))
            for h in range(ML_H):
                act.wait_ge(z_ready, h + 1)
                act.activation(dec[:, h, :], dec[:, h, :], ACT.Exp, scale=-1.0).then_inc(e_ready, 1)
            hi(13)
            evac_o(1, (7, 0))
            act.wait_ge(den_read, 1)
            for r in range(2 * ML_H):
                ins = act.activation(xs[:, r // 4, (r % 4) * ML_DV:(r % 4 + 1) * ML_DV], ps[:, (5 + r) % 8, 0:ML_DV], ACT.Square, accum_out=mn[:, 0, r:r + 1])
            ins.then_inc(ss_ready, 1)
            act.wait_ge(ms_ready, 2)
            act.activation(mn[:, 2, :], mn[:, 1, :], ACT.Sqrt).then_inc(root_ready, 1)
            evac_xt(1, C_HNORM)
            def sum_and_norm(n, s, added, c0):
                for i in range(3):
                    hi(s + i)
                act.wait_ge(x_added, added - 2)
                squares(0)
                hi(s + 3)
                evac_xt(n, c0, (0, 1))
                act.wait_ge(x_added, added)
                squares(1)

            sum_and_norm(2, HALF_MOUT + 2, 4, C_FNORM)

            hi(HALF_FFN + 2)
            root(2)
            evac_xt(2, C_FNORM, (2, 3))
            hi(HALF_FFN + 3)
            act.wait_ge(recip_ready, 1)
            swiglu(HALF_FFN, 0, NT, 0, scale=lambda t: small[:, S_RSTD + t:S_RSTD + t + 1])
            hi(HALF_DQ)

            act.wait_ge(x_added, 6)
            squares(0)
            evac_xt(3, C_DNORM, (0, 1))
            hi(HALF_DQ + 1)
            act.wait_ge(x_added, 8)
            squares(1)
            root(3)
            evac_xt(3, C_DNORM, (2, 3))
            for i in range(HALF_DQ + 2, HALF_DK + 2):
                hi(i)
            act.wait_ge(lam_dot, 1)
            act.activation(lam[:, 2:4], lam[:, 0:2], ACT.Exp).then_inc(lam_exp, 1)
            for i in range(HALF_DK + 2, HALF_DVV + 4):
                hi(i)

            def copy_v(n, banks):
                act.wait_ge(half_used, HALF_DVV + 2 * n + 2)
                for t, b in enumerate(banks):
                    ins = act.activation(vv[:, t, n * NW:(n + 1) * NW], ps[:, b, :], ACT.Copy,
                                         scale=small[:, S_RSTD + t:S_RSTD + t + 1])
                ins.then_inc(dv_ready, 1)

            act.wait_ge(recip_ready, 2)
            copy_v(0, (6, 7))
            hi(HALF_DOUT)
            hi(HALF_DOUT + 1)
            copy_v(1, (0, 2))
            for i in range(2 * DH):
                klen = (i % 2 + 1) * P
                act.wait_ge(max_ready, i + 1)
                if i >= 2:
                    act.wait_ge(a_ready, i - 1)
                for m in range(2):
                    ins = act.activation(ex[:, i % 2, m, 0:klen], ps[:, 4 + i % 3, m * T:m * T + klen], ACT.Exp,
                                         scale=-1.0, bias=nmx[:, i % 3, m:m + 1], accum_out=sm[:, i % 2, m:m + 1])
                ins.then_inc(exp_ready, 1)

                def evac_a(i):
                    klen = (i % 2 + 1) * P
                    act.wait_ge(at_done, i + 1)
                    if i >= 2:
                        act.wait_ge(opv_done, i - 1)
                    act.activation(awt[:, i % 2, 0:klen], ps[:, 7, 0:klen], ACT.Copy).then_inc(at_ready, 1)

                if i >= 1:
                    evac_a(i - 1)
            evac_a(2 * DH - 1)
            act.wait_ge(opv_done, 2 * DH)
            for b in range(4):
                act.activation(osq[b], ps[:, b, :], ACT.Square)\
                   .then_inc(osq_ready, 1)
            act.wait_ge(oms_ready, 1)
            act.activation(oms[:, 2, :], oms[:, 1, :], ACT.Sqrt).then_inc(oroot_ready, 1)
            evac_xt(4, None, scale=sub_w[:, 0:1])
            sum_and_norm(5, HALF_DOUT + 2, 12, C_ENORM)

            evac_xt(5, C_ENORM, (2, 3))
            root(4)
            for t in range(NT):
                act.wait_ge(xs_ready, 2 * 3 + t + 1)
                act.activation(xn_hi[:, t, :], xs[:, t, :], ACT.Copy).then_inc(xn_h, 1)
            act.wait_ge(gap_ready, 1)
            act.activation(gsc[:, :, 1:2], gsc[:, :, 0:1], ACT.Exp).then_inc(gexp_ready, 1)

            def gathered(n):
                for b in range(2):
                    act.wait_ge(gather_done, n * 2 + b + 1)
                    act.activation(xt_hi[:, 4 * b:4 * b + 4, 0:P], ps[:, 2 + b, :].rearrange("p (c t) -> p c t", c=4),
                                   ACT.Copy).then_inc(xe_hi, 1)

            def picked(n):
                act.wait_ge(pick_t_done, n + 1)
                act.activation(pick_t[:, :], ps[:, 7, 0:T], ACT.Copy)
                act.activation(gslot[:, :], ps[:, 7, T:T + 1], ACT.Copy).then_inc(pick_t_ready, 1)

            def expert(n, follows):
                q, nxt = n * GROUPS, HALF_MOE + 6 * GROUPS
                swiglu(HALF_MOE, q, 1, NT * GROUPS + n * GROUPS, lambda: picked(n))
                if follows:
                    gathered(n + 1)
                    hi(nxt, q)
                    hi(nxt + 1, q)
                act.wait_ge(half_used, n * (6 * GROUPS) + (HALF_MOE + 6 * GROUPS))
                act.wait_ge(pick_t_ready, n + 1)
                for nh in range(2):
                    act.activation(y_hi[:, nh * NW:(nh + 1) * NW], ps[:, nh, :], ACT.Copy, scale=gslot[:, 0:1])\
                       .then_inc(y_h, 1)
                if follows:
                    hi(nxt + 2, q)
                    hi(nxt + 3, q)

            gathered(0)
            hi(HALF_MOE + 2)
            hi(HALF_MOE + 3)
            with act.Fori(0, NE - 1) as n:
                expert(n, True)
            expert(NE - 1, False)
            act.wait_ge(route_ready, 1)
            over = act.value_load(route[0:1, 0:1], min_val=0, max_val=OVERFLOW_PASSES)
            with act.Fori(0, OVERFLOW_PASSES) as j:
                with act.If(over > j):
                    hi(HALF_MOE, (j + NE) * GROUPS)
                    hi(HALF_MOE + 1, (j + NE) * GROUPS)
                    gathered(j + NE)
                    hi(HALF_MOE + 2, (j + NE) * GROUPS)
                    hi(HALF_MOE + 3, (j + NE) * GROUPS)
                    expert(j + NE, False)
                act.nop()
            act.wait_ge(x_combined, over * 4 + (4 * NE + 1))
            squares(0)
            squares(1)
            root(5)

        @block.vector
        def _(dve):
            self_n = [0]

            def own(ins):
                ins.then_inc(dve_self, 1)
                self_n[0] += 1
                dve.wait_ge(dve_self, self_n[0])

            def lo(s, q=0):
                slot, ring = s % RAW_SLOTS, s % SPLIT_SLOTS
                dve.wait_ge(hi_ready, at(s, q) + 1)
                dve.tensor_tensor(w_lo[:, ring, :], raw[:, slot, :], w_hi[:, ring, :].bitcast(F32), ALU.subtract)\
                   .then_inc(lo_ready, 1)

            def mean(ss):
                dve.wait_ge(ss_ready, ss)
                sq = small[:, S_SQ:S_SQ + 4].rearrange("p (t n) -> p t n", t=NT)
                own(dve.tensor_tensor(small[:, S_MS:S_MS + 2], sq[:, :, 0], sq[:, :, 1], ALU.add))
                dve.tensor_scalar(small[:, S_MS:S_MS + 2], small[:, S_MS:S_MS + 2], 1.0 / D, EPS, ALU.mult, ALU.add)\
                   .then_inc(ms_ready, 1)

            def inverse(n):
                dve.wait_ge(root_ready, n)
                return dve.reciprocal(small[:, S_RSTD:S_RSTD + 2], small[:, S_ROOT:S_ROOT + 2])

            def normed(row, ready):
                for t in range(NT):
                    dve.scalar_tensor_tensor(out=xs[:, t, :], in0=x[:, t, :], scalar=small[:, S_RSTD + t:S_RSTD + t + 1],
                                             in1=row, op0=ALU.mult, op1=ALU.mult).then_inc(ready, 1)

            def evac_xt(n, c0, pairs=range(4), scale=None):
                for i in pairs:
                    dve.wait_ge(t_hi, 4 * n + i + 1)
                    for j in range(2):
                        c = 2 * i + j
                        w = scale if scale is not None else col[:, c0 + c:c0 + c + 1]
                        ins = dve.scalar_tensor_tensor(out=xt_lo[:, c, :], in0=ps[:, T_BANKS[n][i], j * T:(j + 1) * T],
                                                       scalar=w, in1=xt_hi[:, c, :].bitcast(F32),
                                                       op0=ALU.mult, op1=ALU.subtract)
                    ins.then_inc(xt_ready, 1)

            def add_x(banks, n):
                for t, b in enumerate(banks):
                    xv = x[:, t, n * NW:(n + 1) * NW]
                    dve.tensor_tensor(xv, ps[:, b, :], xv, ALU.add).then_inc(x_added, 1)

            def swiglu(s, q, tiles, tb, after_hidden=None, scale=None):
                def evac(f):
                    for t in range(tiles):
                        dve.wait_ge(hid_t_h, tb + tiles * f + t + 1)
                        dve.tensor_tensor(hid_t_lo[:, :, t * P:(t + 1) * P],
                                          ps[:, 6 + t, :].rearrange("p (c t) -> p c t", c=4),
                                          hid_t_hi[:, :, t * P:(t + 1) * P].bitcast(F32), ALU.subtract)\
                           .then_inc(hid_t_ready, 1)

                def hidden(s, q, f):
                    dve.wait_ge(half_used, at(s, q) + 4)
                    for t in range(tiles):
                        dve.wait_ge(silu_ready, tb + tiles * f + t + 1)
                        if scale:
                            ins = dve.scalar_tensor_tensor(out=hid[:, t, :], in0=ps[:, 6 + t, :], scalar=scale(t),
                                                           in1=gate_act[:, t, :], op0=ALU.mult, op1=ALU.mult)
                        else:
                            ins = dve.tensor_tensor(hid[:, t, :], ps[:, 6 + t, :], gate_act[:, t, :], ALU.mult)
                        ins.then_inc(hid_ready, 1)

                lo(s + 4, q)
                lo(s + 5, q)
                hidden(s, q, 0)
                if after_hidden:
                    after_hidden()
                with dve.Fori(1, GROUPS) as f:
                    q1, s1 = q + (f - 1), s + 4
                    evac(f - 1)
                    for i in (2, 3, 4, 5):
                        lo(s1 + i, q1)
                    hidden(s1, q1, f)
                    for i in (6, 7):
                        lo(s1 + i, q1)
                evac(GROUPS - 1)

            dve.wait_ge(ss_ready, 2)
            dve.tensor_scalar(small[:, S_MS:S_MS + 2], small[:, S_SQ:S_SQ + 4:2], 1.0 / D, EPS, ALU.mult, ALU.add)\
               .then_inc(ms_ready, 1)
            own(inverse(1))
            for nh in range(2):
                for t in range(NT):
                    c = slice(nh * NW, (nh + 1) * NW)
                    ins = dve.tensor_scalar(xs[:, t, c], x[:, t, c], small[:, S_RSTD + t:S_RSTD + t + 1], None, ALU.mult)
                ins.then_inc(xs_ready, 1)
            dve.wait_ge(col_t, 1)
            dve.tensor_copy(col[:, :], ps[:, 7, 0:PRM]).then_inc(col_ready, 1)
            dve.wait_ge(w8h_ready, 1)
            dve.tensor_tensor(w8_lo[:, :, :, :], w8[:, :, :, :], w8_hi[:, :, :, :].bitcast(F32), ALU.subtract)\
               .then_inc(w8_ready, 1)
            lo(0)
            evac_xt(0, C_MNORM, (0, 1))
            lo(1)
            evac_xt(0, C_MNORM, (2, 3))
            lo(2)
            lo(3)

            def conv_pair(c0):
                dve.wait_ge(half_used, 2 if c0 < 4 else 4)
                for d in range(CONV_W):
                    for c in (c0, c0 + 1):
                        b = 4 + c if c < 4 else c - 4
                        w = col[:, C_CONVW + (CONV_W - 1 - d) * 8 + c:C_CONVW + (CONV_W - 1 - d) * 8 + c + 1]
                        if d == 0:
                            ins = dve.tensor_scalar(qk[:, c, :], ps[:, b, 0:T], w, col[:, C_CONVB + c:C_CONVB + c + 1],
                                                    ALU.mult, ALU.add)
                        else:
                            ins = dve.scalar_tensor_tensor(out=qk[:, c, d:T], in0=ps[:, b, 0:T - d], scalar=w,
                                                           in1=qk[:, c, d:T], op0=ALU.mult, op1=ALU.add)
                        if d == CONV_W - 1:
                            ins.then_inc(conv_ready, 1)
                        elif c == c0:
                            ins.then_inc(dve_self, 1)
                            self_n[0] += 1
                        else:
                            own(ins)

            conv_pair(0)
            lo(4)
            conv_pair(2)
            lo(5)
            lo(6)
            conv_pair(4)
            lo(7)
            conv_pair(6)
            lo(8)
            dve.wait_ge(grow_done, 1)
            dve.wait_ge(w8_landed, 16 * 5)
            for g in range(2):
                ins = dve.tensor_scalar(grow[:, g * T:(g + 1) * T], ps[0:ML_H, 4, g * T:(g + 1) * T],
                                        b_gate[:, g:g + 1], None, ALU.add)
                ins.then_inc(grow_ready, 1)
            dve.wait_ge(grow_ready, 2)
            dve.scalar_tensor_tensor(out=g_abs[:, :], in0=grow[:, T:2 * T], scalar=-1.0, in1=grow[:, T:2 * T],
                                     op0=ALU.mult, op1=ALU.max).then_inc(gabs_ready, 1)
            dve.wait_ge(gln_ready, 1)
            own(dve.scalar_tensor_tensor(out=g_logf[:, :], in0=grow[:, T:2 * T], scalar=0.0, in1=g_ln[:, :],
                                         op0=ALU.min, op1=ALU.subtract))
            dve.wait_ge(const_step, 9)
            own(dve.tensor_tensor_scan(g_cum[:, :], g_logf[:, :], zrow[:, :], 0.0, ALU.add, ALU.add))
            own(dve.tensor_tensor(g_a[:, :], grow[:, 0:T], g_cum[:, :], ALU.subtract))
            dve.tensor_tensor_scan(g_max[:, :], g_a[:, :], g_a[:, :], 0.0, ALU.max, ALU.max).then_inc(gm_ready, 1)
            dve.wait_ge(gm_ready, 1)
            dve.tensor_tensor(g_m[:, :], g_cum[:, :], g_max[:, :], ALU.add).then_inc(gm_ready, 1)
            for i in (9, 10, 11):
                lo(i)
            dve.wait_ge(brow_done, 1)
            dve.tensor_scalar(brow, ps[0:DMAPS, 4, 0:BIAS_W], -1.0, None, ALU.mult).then_inc(brow_ready, 1)
            lo(12)
            dve.wait_ge(gbc_done, 1)
            own(dve.tensor_copy(acol[:, :, :], ps[:, 3, 0:8].rearrange("p (t h) -> p t h", t=NT)))
            dve.tensor_copy(em[:, :].rearrange("p (h t) -> p t h", t=NT),
                            ps[:, 3, 8:16].rearrange("p (t h) -> p t h", t=NT)).then_inc(acol_ready, 1)
            for h in range(ML_H):
                mb = ps[:, 1 + h // 2, (h % 2) * T:(h % 2 + 1) * T]
                dve.tensor_scalar(dec[:, h, 0:T], mb, acol[:, 0, h:h + 1], 0.0, ALU.subtract, ALU.max)
                dve.tensor_scalar(dec[:, h, T:ROW], mb[:, P:T], acol[:, 1, h:h + 1], 0.0, ALU.subtract, ALU.max)\
                   .then_inc(z_ready, 1)
            lo(13)
            dve.wait_ge(mask_ready, 2)
            for h, b in enumerate([4, 3, 1, 2]):
                dve.wait_ge(st_done, h + 1)
                dve.scalar_tensor_tensor(out=prob[:, h, :], in0=ps[:, b, 0:ROW], scalar=ML_SCALE, in1=dec[:, h, :],
                                         op0=ALU.mult, op1=ALU.mult).then_inc(prob_ready, 1)
            dve.wait_ge(pv_done, 1)
            dve.tensor_copy(mn[:, 3, 0:3], ps[:, 5:8, ML_DV])
            dve.tensor_copy(mn[:, 3, 3:8], ps[:, 0:5, ML_DV]).then_inc(den_read, 1)
            dve.wait_ge(den_read, 1)
            own(dve.scalar_tensor_tensor(out=mn[:, 4, :], in0=mn[:, 3, :], scalar=-1.0, in1=mn[:, 3, :],
                                         op0=ALU.mult, op1=ALU.max))
            dve.wait_ge(acol_ready, 1)
            own(dve.tensor_tensor(mn[:, 6, :], mn[:, 4, :], em[:, :], ALU.max))
            own(dve.reciprocal(mn[:, 5, :], mn[:, 6, :]))
            own(dve.tensor_tensor(mn[:, 6, :], mn[:, 5, :], mn[:, 5, :], ALU.mult))
            dve.wait_ge(ss_ready, 3)
            own(dve.tensor_tensor(mn[:, 7, :], mn[:, 0, :], mn[:, 6, :], ALU.mult))
            dve.tensor_scalar(mn[:, 1, :], mn[:, 7, :], 1.0 / ML_DV, EPS, ALU.mult, ALU.add).then_inc(ms_ready, 1)
            dve.wait_ge(root_ready, 2)
            own(dve.reciprocal(mn[:, 3, :], mn[:, 2, :]))
            own(dve.tensor_tensor(mn[:, 6, :], mn[:, 3, :], mn[:, 5, :], ALU.mult))
            dve.wait_ge(o_ready, 2)
            for r in range(2 * ML_H):
                h, t = divmod(r, 2)
                c = slice(h * ML_DV, (h + 1) * ML_DV)
                ins = dve.scalar_tensor_tensor(out=xs[:, t, c], in0=ps[:, (5 + r) % 8, 0:ML_DV], scalar=mn[:, 6, r:r + 1],
                                               in1=sig_o[:, t, c], op0=ALU.mult, op1=ALU.mult)
                if r in (3, 7):
                    ins.then_inc(xs_ready, 1)
            evac_xt(1, C_HNORM)

            def sum_and_norm(n, s, c0, first, second):
                lo(s)
                dve.wait_ge(half_used, s)
                add_x(first, 0)
                lo(s + 1)
                lo(s + 2)
                evac_xt(n, c0, (0, 1))
                lo(s + 3)
                dve.wait_ge(half_used, s + 2)
                add_x(second, 1)

            sum_and_norm(2, HALF_MOUT + 2, C_FNORM, (1, 2), (0, 3))

            mean(7)
            lo(HALF_FFN + 2)
            inverse(3).then_inc(recip_ready, 1)
            evac_xt(2, C_FNORM, (2, 3))
            dve.wait_ge(brow_stored, 16)
            lo(HALF_FFN + 3)
            dve.wait_ge(recip_ready, 1)
            swiglu(HALF_FFN, 0, NT, 0, scale=lambda t: small[:, S_RSTD + t:S_RSTD + t + 1])
            dve.wait_ge(down_half, 1)
            add_x((0, 2), 0)
            lo(HALF_DQ)
            evac_xt(3, C_DNORM, (0, 1))
            lo(HALF_DQ + 1)
            dve.wait_ge(half_used, HALF_DQ)
            add_x((1, 3), 1)

            mean(11)
            inverse(4).then_inc(recip_ready, 1)
            dve.wait_ge(recip_ready, 2)
            for t in range(NT):
                ins = dve.tensor_scalar(diag[:, t, :], ident[:, :], small[:, S_RSTD + t:S_RSTD + t + 1], None, ALU.mult)
            ins.then_inc(diag_ready, 1)
            evac_xt(3, C_DNORM, (2, 3))
            dve.wait_ge(rrow_done, 1)
            dve.tensor_copy(rrow[:, :], ps[:, 1, 0:T]).then_inc(rrow_ready, 1)
            dve.wait_ge(lam_landed, 64)
            own(dve.tensor_tensor(lamp[:, :, :], lamv[:, 0:4:2, :], lamv[:, 1:4:2, :], ALU.mult))
            dve.tensor_reduce(lam[:, 0:2], lamp[:, :, :], AX_X, ALU.add).then_inc(lam_dot, 1)
            own(dve.tensor_scalar(sub_w[:, :], col[:, C_SUB:C_SUB + 1], 1.0 - LAM_INIT, None, ALU.mult))
            dve.wait_ge(qz_zeroed, 1)
            dve.wait_ge(rrow_ready, 1)
            for n, banks in enumerate((BANKS_A, BANKS_B)):
                lo(HALF_DQ + 2 * n + 2)
                lo(HALF_DQ + 2 * n + 3)
                dve.wait_ge(half_used, HALF_DQ + 2 * n + 2)
                for c, b in enumerate(banks):
                    for m in range(2):
                        r = slice(m * DHD, (m + 1) * DHD)
                        ins = dve.scalar_tensor_tensor(out=qz[r, 4 * n + c, m, :], in0=ps[r, b, 0:T], scalar=-DSCALE,
                                                       in1=rrow[r, :], op0=ALU.mult, op1=ALU.mult)
                ins.then_inc(dq_ready, 1)

            for n, banks in enumerate((BANKS_A, BANKS_B)):
                lo(HALF_DK + 2 * n + 2)
                lo(HALF_DK + 2 * n + 3)
                dve.wait_ge(half_used, HALF_DK + 2 * n + 2)
                for c, b in enumerate(banks):
                    ins = dve.tensor_tensor(kt[:, 4 * n + c, :], ps[:, b, 0:T], rrow[:, :], ALU.mult)
                ins.then_inc(dk_ready, 1)
            for i in range(HALF_DVV + 2, HALF_DOUT + 2):
                lo(i)
            dve.wait_ge(lam_exp, 1)
            own(dve.tensor_tensor(lam[:, 4:5], lam[:, 3:4], lam[:, 2:3], ALU.subtract))
            own(dve.tensor_scalar(lam[:, 5:6], lam[:, 4:5], -LAM_INIT, None, ALU.add))

            def row_max(i):
                klen = (i % 2 + 1) * P
                dve.wait_ge(logit_done, i + 1)
                if i >= 3:
                    dve.wait_ge(exp_ready, i - 2)
                lg2 = ps[:, 4 + i % 3, :].rearrange("p (m k) -> p m k", m=2)[:, :, 0:klen]
                dve.tensor_reduce(nmx[:, i % 3, :], lg2, AX_X, ALU.min).then_inc(max_ready, 1)

            def mix(i):
                klen = (i % 2 + 1) * P
                j = i % 2
                dve.wait_ge(exp_ready, i + 1)
                own(dve.reciprocal(sm[:, j, 2:4], sm[:, j, 0:2]))
                own(dve.tensor_tensor(sm[:, j, 4:5], sm[:, j, 3:4], lam[:, 5:6], ALU.mult))
                if i >= 2:
                    dve.wait_ge(at_done, i - 1)
                own(dve.tensor_scalar(aw[:, j, 0:klen], ex[:, j, 0, 0:klen], sm[:, j, 2:3], None, ALU.mult))
                dve.scalar_tensor_tensor(out=aw[:, j, 0:klen], in0=ex[:, j, 1, 0:klen], scalar=sm[:, j, 4:5],
                                         in1=aw[:, j, 0:klen], op0=ALU.mult, op1=ALU.add).then_inc(a_ready, 1)

            row_max(0)
            row_max(1)
            for i in range(2 * DH):
                mix(i)
                if i + 2 < 2 * DH:
                    row_max(i + 2)
            for b in range(4):
                dve.wait_ge(osq_ready, b + 1)
                ins = dve.tensor_reduce(oms[:, 0, 4 * b:4 * b + 4],
                                        osq[b].rearrange("p (h v) -> p h v", h=4),
                                        AX_X, ALU.add)
            own(ins)
            dve.tensor_scalar(oms[:, 1, :], oms[:, 0, :], 1.0 / DDV, SUB_EPS, ALU.mult, ALU.add).then_inc(oms_ready, 1)
            dve.wait_ge(oroot_ready, 1)
            own(dve.reciprocal(oms[:, 3, :], oms[:, 2, :]))
            for b in (0, 2, 1, 3):
                r = oms[:, 3, 4 * b:4 * b + 4].unsqueeze(2).to_broadcast([P, 4, DDV])
                ins = dve.tensor_tensor(
                    xs[:, b // 2, (b % 2) * NW:(b % 2 + 1) * NW].rearrange("p (h v) -> p h v", h=4),
                    ps[:, b, :].rearrange("p (h v) -> p h v", h=4), r, ALU.mult)
                if b >= 2:
                    ins.then_inc(xs_ready, 1)
            evac_xt(4, None, scale=sub_w[:, 0:1])
            sum_and_norm(5, HALF_DOUT + 2, C_ENORM, (0, 2), (1, 3))

            mean(15)
            evac_xt(5, C_ENORM, (2, 3))
            own(inverse(5))
            dve.wait_ge(rows_landed, 32)
            normed(moe_w[:, :], xs_ready)
            for t in range(NT):
                dve.wait_ge(xn_h, t + 1)
                dve.tensor_tensor(xn_lo[:, t, :], xs[:, t, :], xn_hi[:, t, :].bitcast(F32), ALU.subtract)\
                   .then_inc(xn_ready, 1)
            dve.wait_ge(router_done, 1)
            dve.tensor_copy(lrow[:, :], ps[0:NE, 0, 0:T]).then_inc(lrow_ready, 1)
            dve.wait_ge(lcol_done, 1)
            for t in range(NT):
                ins = dve.scalar_tensor_tensor(out=lg[:, t, :], in0=ps[:, 5, t * NE:(t + 1) * NE],
                                               scalar=small[:, S_RSTD + t:S_RSTD + t + 1], in1=b_route[:, :],
                                               op0=ALU.mult, op1=ALU.add)
            own(ins)
            for t in range(NT):
                ins = dve.max(top[:, t, :], lg[:, t, :])
            own(ins)
            for t in range(NT):
                ins = dve.max_index(topi[:, t, :], top[:, t, :], lg[:, t, :])
            own(ins)
            dve.tensor_tensor(gsc[:, :, 0:1], top[:, :, 1:2], top[:, :, 0:1], ALU.subtract).then_inc(gap_ready, 1)
            own(dve.tensor_copy(topf[:, :, :], topi[:, :, :]))
            dve.wait_ge(const_step, 14)
            for t in range(NT):
                for i in range(2):
                    ins = dve.tensor_scalar(m12[:, t, i, :], slots[:, 0:NE], topf[:, t, i:i + 1], None, ALU.is_equal)
            own(ins)
            for t in range(NT):
                ins = dve.tensor_tensor(rt[:, 0, t, :], m12[:, t, 0, :], m12[:, t, 1, :], ALU.add)
            ins.then_inc(chosen_ready, 1)
            dve.wait_ge(gexp_ready, 1)
            own(dve.tensor_scalar(gsc[:, :, 2:3], gsc[:, :, 1:2], 1.0, None, ALU.add))
            own(dve.reciprocal(gsc[:, :, 3:4], gsc[:, :, 2:3]))
            own(dve.tensor_tensor(gsc[:, :, 4:5], gsc[:, :, 3:4], gsc[:, :, 1:2], ALU.mult))
            for t in range(NT):
                ins = dve.tensor_scalar(rt[:, 1, t, :], m12[:, t, 0, :], gsc[:, t, 3:4], None, ALU.mult)
            own(ins)
            for t in range(NT):
                ins = dve.scalar_tensor_tensor(out=rt[:, 1, t, :], in0=m12[:, t, 1, :], scalar=gsc[:, t, 4:5],
                                               in1=rt[:, 1, t, :], op0=ALU.mult, op1=ALU.add)
            own(ins)
            dve.wait_ge(pos_done, 1)
            dve.tensor_copy(pos[:, :, :], ps[:, 6, 0:16].rearrange("p (t e) -> p t e", t=NT))
            dve.tensor_scalar(ovf[:, 0, :], ps[:, 6, 16:24], float(P), None, ALU.is_gt).then_inc(x_combined, 1)
            dve.wait_ge(x_combined, 1)
            for t in range(NT):
                dve.tensor_copy(plan[:, 0:NE, t], pos[:, t, :])
                dve.tensor_copy(plan[:, 0:NE, 2 + t], rt[:, 0, t, :])
                ins = dve.tensor_copy(plan[:, 0:NE, 4 + t], rt[:, 1, t, :])
            own(ins)
            def choose(n):
                if not (known(n) and n == 0):
                    dve.wait_ge(pick_t_done, n)
                dve.tensor_copy(cur[:, :], plan[:, bass.ds(n, 1), :].rearrange("p a c -> p (a c)")).then_inc(cur_ready, 1)
                dve.wait_ge(cur_ready, n + 1)
                for t in range(NT):
                    ins = dve.tensor_scalar(pick[:, t, :], slots[:, :], cur[:, t:t + 1], cur[:, 2 + t:3 + t],
                                            ALU.is_equal, ALU.mult)
                ins.then_inc(pick_ready, 1)

            def gathered(n):
                for b in range(2):
                    dve.wait_ge(xe_hi, n * 2 + b + 1)
                    dve.tensor_tensor(xt_lo[:, 4 * b:4 * b + 4, 0:P], ps[:, 2 + b, :].rearrange("p (c t) -> p c t", c=4),
                                      xt_hi[:, 4 * b:4 * b + 4, 0:P].bitcast(F32), ALU.subtract).then_inc(xe_ready, 1)

            def expert(n, follows):
                q, nxt = n * GROUPS, HALF_MOE + 6 * GROUPS
                swiglu(HALF_MOE, q, 1, NT * GROUPS + n * GROUPS, (lambda: choose(n + 1)) if follows else None)
                if follows:
                    gathered(n + 1)
                    lo(nxt, q)
                    lo(nxt + 1, q)
                for nh in range(2):
                    c = slice(nh * NW, (nh + 1) * NW)
                    dve.wait_ge(y_h, n * 2 + nh + 1)
                    dve.scalar_tensor_tensor(out=y_lo[:, c], in0=ps[:, nh, :], scalar=gslot[:, 0:1],
                                             in1=y_hi[:, c].bitcast(F32), op0=ALU.mult, op1=ALU.subtract)\
                       .then_inc(y_ready, 1)
                if follows:
                    lo(nxt + 2, q)
                    lo(nxt + 3, q)
                for i, (nh, t) in enumerate([(nh, t) for nh in range(2) for t in range(NT)]):
                    xv = x[:, t, nh * NW:(nh + 1) * NW]
                    dve.wait_ge(combine_done, n * 4 + i + 1)
                    dve.tensor_tensor(xv, ps[:, combine_bank[nh][t], :], xv, ALU.add).then_inc(x_combined, 1)

            choose(0)
            gathered(0)
            lo(HALF_MOE + 2)
            lo(HALF_MOE + 3)
            own(dve.tensor_copy(ovf[:, 1, :], ovf[:, 0, :]))
            for step in (1, 2, 4):
                src, dst = (1, 2) if step != 2 else (2, 1)
                dve.tensor_copy(ovf[:, dst, 0:step], ovf[:, src, 0:step])
                own(dve.tensor_tensor(ovf[:, dst, step:NE], ovf[:, src, step:NE], ovf[:, src, 0:NE - step], ALU.add))
            for j in range(OVERFLOW_PASSES):
                own(dve.scalar_tensor_tensor(out=ovf[:, 3 + j, :], in0=ovf[:, 2, :], scalar=float(j + 1),
                                             in1=ovf[:, 0, :], op0=ALU.is_equal, op1=ALU.mult))
            for j in range(OVERFLOW_PASSES):
                sel = ovf[:, 3 + j, :]
                for i, (src, shift) in enumerate([(pos[:, 0, :], -float(P)), (pos[:, 1, :], -float(P)),
                                                  (rt[:, 0, 0, :], 0.0), (rt[:, 0, 1, :], 0.0),
                                                  (rt[:, 1, 0, :], 0.0), (rt[:, 1, 1, :], 0.0),
                                                  (slots[:, 0:NE], 0.0)]):
                    dst = plan[:, NE + j, i:i + 1] if i < 6 else ovs[:, 1 + j:2 + j]
                    own(dve.tensor_tensor_reduce(ovf[:, 6, :], sel, src, 1.0, shift, ALU.mult, ALU.add, dst))
            own(dve.tensor_copy(ovs[:, 0:1], ovf[:, 2, NE - 1:NE]))
            dve.tensor_copy(route[0:1, :], ovs[0:1, 0:4]).then_inc(route_ready, 1)

            with dve.Fori(0, NE - 1) as n:
                expert(n, True)
            expert(NE - 1, False)
            dve.wait_ge(route_ready, 1)
            over = dve.value_load(route[0:1, 0:1], min_val=0, max_val=OVERFLOW_PASSES)
            with dve.Fori(0, OVERFLOW_PASSES) as j:
                with dve.If(over > j):
                    lo(HALF_MOE, (j + NE) * GROUPS)
                    lo(HALF_MOE + 1, (j + NE) * GROUPS)
                    choose(j + NE)
                    gathered(j + NE)
                    lo(HALF_MOE + 2, (j + NE) * GROUPS)
                    lo(HALF_MOE + 3, (j + NE) * GROUPS)
                    expert(j + NE, False)
                dve.nop()
            mean(19)
            own(inverse(6))
            normed(fin_w[:, :], fin_ready)


_INS = ["x", "rel_bias_table", "mlstm_norm", "mlstm_w_in", "mlstm_conv_w", "mlstm_conv_b", "mlstm_b_igate",
        "mlstm_b_fgate", "mlstm_head_norm", "mlstm_w_out", "diff_norm", "diff_w_in", "diff_lambda_q1",
        "diff_lambda_k1", "diff_lambda_q2", "diff_lambda_k2", "diff_subln", "diff_w_out", "ffn_norm",
        "ffn_w_gate", "ffn_w_up", "ffn_w_down", "moe_norm", "moe_w_router", "moe_b_router", "moe_w_gate",
        "moe_w_up", "moe_w_down", "final_norm"]


def kernel(**inputs):
    import numpy as _np
    import concourse.bacc as _bacc
    from concourse import mybir as _mybir
    from concourse.bass_utils import run_bass_kernel_spmd as _run

    nc = _bacc.Bacc("TRN2", target_bir_lowering=False, num_devices=1)
    arrays, aps = {}, {}
    for name in _INS:
        a = _np.ascontiguousarray(inputs[name])
        arrays[f"in_{name}"] = a
        aps[name] = nc.dram_tensor(f"in_{name}", a.shape, _mybir.dt.from_np(a.dtype), kind="ExternalInput").ap()
    hot = _np.array(bucket_hot(), _np.float32)
    arrays["in_bucket_hot"] = hot
    aps["bucket_hot"] = nc.dram_tensor("in_bucket_hot", hot.shape, _mybir.dt.float32, kind="ExternalInput").ap()
    out = nc.dram_tensor("out_0", (1, 256, 1024), _mybir.dt.float32, kind="ExternalOutput").ap()
    bass_hybrid(nc, aps, out)
    r = _run(nc, [arrays], core_ids=[0])
    return r.results[0]["out_0"]
```

```python
import math
from contextlib import ExitStack

import concourse.bass as bass
from concourse import mybir

F32 = mybir.dt.float32
F32R = mybir.dt.float32r
I32 = mybir.dt.int32
U32 = mybir.dt.uint32
ALU = mybir.AluOpType
ACT = mybir.ActivationFunctionType
AX_X = mybir.AxisListType.X

P = 128
T = 256
NT = T // P
D = 1024
KC = D // P
NW = 512
F_FF = 3584
GROUPS = F_FF // NW
NE = 8
HALF = 2048
RAW_SLOTS = 6
SPLIT_SLOTS = 3
OVERFLOW_PASSES = 3
PASSES = NE + OVERFLOW_PASSES

ML_H, ML_DK, ML_DV = 4, 128, 256
ML_DVX = ML_DV + 1
ML_SCALE = ML_DK ** -0.5
CONV_W = 4
ROW = 384

DH, DHD, DDV = 8, 64, 128
DMAPS = 2 * DH
DSCALE = DHD ** -0.5
LAYER = 1
LAM_INIT = 0.8 - 0.6 * math.exp(-0.3 * LAYER)
BUCKETS, MAX_DIST = 32, 128
BIAS_W = 384
NEG = -1.0e30

EPS, SUB_EPS = 1e-6, 1e-5

HALF_Q, HALF_K, HALF_V, HALF_O, HALF_MOUT = 0, 2, 4, 8, 12
HALF_FFN = 16
HALF_DQ = HALF_FFN + 6 * GROUPS
HALF_DK, HALF_DVV, HALF_DOUT = HALF_DQ + 4, HALF_DQ + 8, HALF_DQ + 12
HALF_MOE = HALF_DQ + 16
HALF_LAST = HALF_MOE + 6 * GROUPS * (NE - 1)
HALF_OVER = HALF_LAST + 6 * GROUPS
EXTRA_HALVES = (HALF_LAST + 4, HALF_LAST + 5, HALF_LAST + 6 * GROUPS - 6)
EXTRA = len(EXTRA_HALVES)

C_MNORM, C_HNORM, C_FNORM, C_DNORM, C_ENORM, C_CONVB, C_CONVW, C_SUB = 0, 8, 16, 24, 32, 40, 48, 80
PRM = 81

PRM_LOADS = 7

S_RSTD, S_MS, S_ROOT, S_SQ = 0, 2, 4, 6


def bucket_of(n):
    half = BUCKETS // 2
    if n < half:
        return n
    return min(half + int(math.log(n / half) / math.log(MAX_DIST / half) * (BUCKETS - half) + 1e-9), BUCKETS - 1)


def bucket_hot():
    rows = [[0.0] * BIAS_W for _ in range(BUCKETS + 1)]
    for c in range(BIAS_W):
        n = T - 1 - c
        rows[bucket_of(n) if n >= 0 else BUCKETS][c] = 1.0
    return rows


def bass_hybrid(nc, A, out):
    ctx = ExitStack()
    with ctx:
        scope = [ctx]

        def sb(name, shape, dt=F32):
            return scope[-1].enter_context(nc.sbuf_tensor(name, shape, dt))

        def sem(name):
            return ctx.enter_context(nc.semaphore(name))

        x = sb("x", [P, NT, D])
        xs = sb("xs", [P, NT, D])
        xt_hi = sb("xt_hi", [P, KC, T], F32R)
        xt_lo = sb("xt_lo", [P, KC, T], F32R)
        raw = sb("raw", [P, RAW_SLOTS, HALF])
        w_hi = sb("w_hi", [P, SPLIT_SLOTS, HALF], F32R)
        w_lo = sb("w_lo", [P, SPLIT_SLOTS, HALF], F32R)
        gate_act = sb("gate_act", [P, NT, NW])
        hid = sb("hid", [P, NT, NW])
        hid_t_hi = sb("hid_t_hi", [P, 4, T], F32R)
        hid_t_lo = sb("hid_t_lo", [P, 4, T], F32R)
        ident = sb("ident", [P, P])
        ones = sb("ones", [P, P])
        prm = sb("prm", [PRM, P])
        mnorm_rows = sb("mnorm_rows", [KC, P])
        col = sb("col", [P, PRM])
        small = sb("small", [P, 10])
        w8 = sb("w8", [P, 2, KC, 8])
        w8_hi = sb("w8_hi", [P, 2, KC, 8], F32R)
        w8_lo = sb("w8_lo", [P, 2, KC, 8], F32R)
        b_gate = sb("b_gate", [ML_H, 2])
        b_route = sb("b_route", [P, NE])
        lamv = sb("lamv", [P, 4, DHD])
        lamp = sb("lamp", [P, 2, DHD])
        lam = sb("lam", [P, 8])
        sub_w = sb("sub_w", [P, 1])
        diag = sb("diag", [P, NT, P])
        rrow = sb("rrow", [P, T])
        anti = sb("anti", [P, P])

        scope.append(ExitStack())
        qk = sb("qk", [P, 2 * ML_H, T])
        vx = sb("vx", [P, NT, ML_H, ML_DVX])
        sig_o = sb("sig_o", [P, NT, D])
        dec = sb("dec", [P, ML_H, ROW])
        prob = sb("prob", [P, ML_H, ROW])
        grow = sb("grow", [ML_H, 2 * T])
        g_abs = sb("g_abs", [ML_H, T])
        g_exp = sb("g_exp", [ML_H, T])
        g_ln = sb("g_ln", [ML_H, T])
        g_logf = sb("g_logf", [ML_H, T])
        g_cum = sb("g_cum", [ML_H, T])
        g_a = sb("g_a", [ML_H, T])
        g_max = sb("g_max", [ML_H, T])
        g_m = sb("g_m", [ML_H, T])
        g_em2 = sb("g_em2", [ML_H, T])
        zrow = sb("zrow", [ML_H, T])
        headsel = sb("headsel", [ML_H, ML_H, P])
        acol = sb("acol", [P, NT, ML_H])
        em2 = sb("em2", [P, ML_H * NT])
        mn = sb("mn", [P, 8, 8])
        scope.pop().close()

        scope.append(ExitStack())
        qz = sb("qz", [P, DH, 2, T])
        kt = sb("kt", [P, DH, T])
        vv = sb("vv", [P, NT, D])
        bias = sb("bias", [P, DMAPS, T])
        ex = gate_act[:, :, :].rearrange("p i (m k) -> p i m k", m=2)
        aw = sb("aw", [P, 2, T])
        awt = sb("awt", [P, 2, T])
        nmx = sb("nmx", [P, 3, 2])
        sm = sb("sm", [P, 2, 8])
        osq = [xs[:, b // 2, (b % 2) * NW:(b % 2 + 1) * NW] for b in range(4)]
        oms = sb("oms", [P, 4, 2 * DH])
        scope.pop().close()

        scope.append(ExitStack())
        extra = sb("extra", [P, EXTRA, HALF])
        xn_hi = sb("xn_hi", [P, NT, D], F32R)
        xn_lo = sb("xn_lo", [P, NT, D], F32R)
        scope.append(ExitStack())
        moe_w = sb("moe_w", [P, D])
        scope.pop().close()
        y_hi = sb("y_hi", [P, D], F32R)
        y_lo = sb("y_lo", [P, D], F32R)
        pick = sb("pick", [P, NT, P], F32R)
        pick_t = sb("pick_t", [P, T], F32R)
        slots_i = sb("slots_i", [P, P], I32)
        slots = sb("slots", [P, P])
        before = sb("before", [P, P])
        lg = sb("lg", [P, NT, NE])
        lrow = sb("lrow", [NE, T])
        top = sb("top", [P, NT, 8])
        topi = sb("topi", [P, NT, 8], U32)
        topf = sb("topf", [P, NT, 8])
        m12 = sb("m12", [P, NT, 2, NE])
        gsc = sb("gsc", [P, NT, 8])
        rt = sb("rt", [P, 2, NT, NE])
        pos = sb("pos", [P, NT, NE])
        ovf = sb("ovf", [P, 2, NE])
        sel = sb("sel", [P, OVERFLOW_PASSES, NE])
        ovj = sb("ovj", [P, OVERFLOW_PASSES, 6, NE])
        ovi = sb("ovi", [P, OVERFLOW_PASSES, NE])
        zero8 = sb("zero8", [P, NE])
        ovs = sb("ovs", [P, 16])
        plan = sb("plan", [P, PASSES, 6])
        cur = sb("cur", [P, 6])
        gslot = sb("gslot", [P, 1])
        route = sb("route", [1, 4], I32)
        scope.pop().close()

        xg = xs[:, 0, :]
        fin_w = xs[:, 1, :]

        hot = gate_act[0:BUCKETS + 1, 0, 0:BIAS_W]
        tab = gate_act[0:BUCKETS + 1, 1, 0:DMAPS]
        brow = hid[0:DMAPS, 0, 0:BIAS_W]

        ps = ctx.enter_context(nc.psum_tensor("ps", [P, 8, NW], F32))
        skew = nc.dram_tensor("skew", (DMAPS, BIAS_W), F32, kind="Internal").ap()

        x_landed = [sem(f"x_landed{t}") for t in range(NT)]
        prm_landed = sem("prm_landed")
        mnorm_landed = sem("mnorm_landed")
        w8_landed = sem("w8_landed")
        lam_landed = sem("lam_landed")
        rows_landed = sem("rows_landed")
        fin_landed = sem("fin_landed")
        tab_landed = sem("tab_landed")
        brow_stored = sem("brow_stored")
        bias_landed = sem("bias_landed")
        out_stored = sem("out_stored")
        raw_landed = [sem(f"raw_landed{s}") for s in range(RAW_SLOTS)]
        extra_landed = [sem(f"extra_landed{i}") for i in range(EXTRA)]
        hi_ready = sem("hi_ready")
        lo_ready = sem("lo_ready")
        half_used = sem("half_used")
        const_step = sem("const_step")
        act_self = sem("act_self")
        dve_self = sem("dve_self")
        col_t = sem("col_t")
        col_ready = sem("col_ready")
        brow_done = sem("brow_done")
        brow_ready = sem("brow_ready")
        ss_ready = sem("ss_ready")
        ms_ready = sem("ms_ready")
        root_ready = sem("root_ready")
        xs_ready = sem("xs_ready")
        t_done = sem("t_done")
        t_hi = sem("t_hi")
        xt_ready = sem("xt_ready")
        w8h_ready = sem("w8h_ready")
        w8_ready = sem("w8_ready")
        conv_ready = sem("conv_ready")
        qk_ready = sem("qk_ready")
        grow_done = sem("grow_done")
        grow_ready = sem("grow_ready")
        gabs_ready = sem("gabs_ready")
        gln_ready = sem("gln_ready")
        gm_ready = sem("gm_ready")
        gem_ready = sem("gem_ready")
        gbc_done = sem("gbc_done")
        acol_ready = sem("acol_ready")
        v_ready = sem("v_ready")
        o_ready = sem("o_ready")
        z_ready = sem("z_ready")
        e_ready = sem("e_ready")
        mask_ready = sem("mask_ready")
        st_done = sem("st_done")
        prob_ready = sem("prob_ready")
        pv_done = sem("pv_done")
        x_added = sem("x_added")
        silu_ready = sem("silu_ready")
        hid_ready = sem("hid_ready")
        hid_t_done = sem("hid_t_done")
        hid_t_h = sem("hid_t_h")
        hid_t_ready = sem("hid_t_ready")
        dq_ready = sem("dq_ready")
        dk_ready = sem("dk_ready")
        dv_ready = sem("dv_ready")
        down_half = sem("down_half")
        recip_ready = sem("recip_ready")
        diag_ready = sem("diag_ready")
        rrow_done = sem("rrow_done")
        rrow_ready = sem("rrow_ready")
        qz_zeroed = sem("qz_zeroed")
        logit_done = sem("logit_done")
        max_ready = sem("max_ready")
        exp_ready = sem("exp_ready")
        a_ready = sem("a_ready")
        at_done = sem("at_done")
        at_ready = sem("at_ready")
        opv_done = sem("opv_done")
        osq_ready = sem("osq_ready")
        oms_ready = sem("oms_ready")
        oroot_ready = sem("oroot_ready")
        lam_dot = sem("lam_dot")
        lam_exp = sem("lam_exp")
        xn_h = sem("xn_h")
        xn_ready = sem("xn_ready")
        router_done = sem("router_done")
        lrow_ready = sem("lrow_ready")
        lcol_done = sem("lcol_done")
        gap_ready = sem("gap_ready")
        gexp_ready = sem("gexp_ready")
        chosen_ready = sem("chosen_ready")
        pos_done = sem("pos_done")
        route_ready = sem("route_ready")
        cur_ready = sem("cur_ready")
        pick_ready = sem("pick_ready")
        gather_done = sem("gather_done")
        xg_ready = [sem("xg_first"), sem("xg_second")]
        xg_turned = sem("xg_turned")
        y_first = sem("y_first")
        xe_hi = sem("xe_hi")
        xe_ready = sem("xe_ready")
        pick_t_done = sem("pick_t_done")
        pick_t_ready = sem("pick_t_ready")
        y_h = sem("y_h")
        y_ready = sem("y_ready")
        combine_done = sem("combine_done")
        x_combined = sem("x_combined")
        fin_ready = sem("fin_ready")

        block = ctx.enter_context(nc.Block())

        def at(s, q=0):
            return q * RAW_SLOTS + s

        BANKS_A, BANKS_B = [6, 7, 0, 2], [4, 5, 3, 1]
        T_BANKS = [[0, 1, 2, 3], [5, 6, 7, 0], [1, 2, 1, 2], [4, 5, 4, 5], [4, 5, 6, 7], [4, 5, 6, 7]]
        combine_bank = [[2, 3], [5, 7]]

        def raw_at(s):
            return s - sum(e < s for e in EXTRA_HALVES)

        def pass_base(n, j=None):
            if j is not None:
                return HALF_OVER, j * GROUPS
            return (HALF_MOE + 6 * GROUPS * n, 0) if known(n) else (HALF_MOE, n * GROUPS)

        def known(v):
            return isinstance(v, int)

        def wait_from(eng, s, v):
            if not (known(v) and v <= 0):
                eng.wait_ge(s, v)

        x_in = A["x"].rearrange("a (t p) d -> (a p) t d", p=P)
        out_v = out.rearrange("a (t p) d -> (a p) t d", p=P)

        @block.sync
        def _(sp):
            def load(s, q, src):
                wait_from(sp, lo_ready, at(s, q) - RAW_SLOTS + 1)
                slot = raw_at(s) % RAW_SLOTS
                n = src.shape[1]
                sp.dma_start(raw[:, slot, :].rearrange("p (k n) -> p k n", k=n), src)\
                  .then_inc(raw_landed[slot], 16)

            def wide(w, k0, n0):
                return w.rearrange("(k p) n -> p k n", p=P)[:, k0:k0 + 4, n0:n0 + NW]

            def slabs(s, w, n_slabs):
                for n in range(n_slabs):
                    for hh in range(2):
                        load(s + 2 * n + hh, 0, wide(w, 4 * hh, n * NW))

            def gate_up(s, q, wg, wu, f):
                for w in (wg, wu):
                    for hh in range(2):
                        load(s, q, w[:, 4 * hh:4 * hh + 4, bass.ds(f * NW, NW)])
                        s += 1
                return s

            def down(s, q, wd, f):
                for hh in range(2):
                    load(s + hh, q, wd[:, bass.ds(f * 4 + 2 * hh, 2), :])

            def gate_ups_downs(s, q, wg, wu, wd, f0):
                with sp.Fori(f0, GROUPS) as f:
                    nxt = gate_up(s + 4, q + (f - 1), wg, wu, f)
                    down(nxt, q + (f - 1), wd, f - 1)
                down(s + 4 + 6 * (GROUPS - 1), q, wd, GROUPS - 1)

            def swiglu(s, q, wg, wu, wd):
                gate_up(s, q, wg, wu, 0)
                gate_ups_downs(s, q, wg, wu, wd, 1)

            for t in range(NT):
                sp.dma_start(x[:, t, :], x_in[:, t, :]).then_inc(x_landed[t], 16)
            slabs(HALF_Q, A["mlstm_w_in"][0], 6)
            slabs(HALF_MOUT, A["mlstm_w_out"][0], 2)
            swiglu(HALF_FFN, 0, A["ffn_w_gate"][0].rearrange("(k p) f -> p k f", p=P),
                   A["ffn_w_up"][0].rearrange("(k p) f -> p k f", p=P),
                   A["ffn_w_down"][0].rearrange("(c p) d -> p c d", p=P))
            slabs(HALF_DQ, A["diff_w_in"][0], 6)
            slabs(HALF_DOUT, A["diff_w_out"][0], 2)

            mg = A["moe_w_gate"][0].rearrange("e (k p) f -> e p k f", p=P)
            mu = A["moe_w_up"][0].rearrange("e (k p) f -> e p k f", p=P)
            md = A["moe_w_down"][0].rearrange("e (c p) d -> e p c d", p=P)

            def expert_weights(e):
                return mg[e, :, :, :], mu[e, :, :, :], md[e, :, :, :]

            wg, wu, wd = expert_weights(0)
            gate_up(HALF_MOE, 0, wg, wu, 0)
            sp.wait_ge(xs_ready, 2 * 3)
            f_last = (GROUPS - 1) * NW
            for i, src in enumerate((mg[NE - 1, :, 0:4, NW:2 * NW], mg[NE - 1, :, 4:8, NW:2 * NW],
                                     mu[NE - 1, :, 0:4, f_last:f_last + NW])):
                sp.dma_start(extra[:, i, :].rearrange("p (k n) -> p k n", k=4), src).then_inc(extra_landed[i], 16)
            gate_ups_downs(HALF_MOE, 0, wg, wu, wd, 1)
            with sp.Fori(1, NE - 1) as n:
                swiglu(*pass_base(n), *expert_weights(n))
            wg, wu, wd = expert_weights(NE - 1)
            s = HALF_LAST
            gate_up(s, 0, wg, wu, 0)
            for hh in range(2):
                load(s + 6 + hh, 0, wu[:, 4 * hh:4 * hh + 4, NW:2 * NW])
            down(s + 8, 0, wd, 0)
            with sp.Fori(2, GROUPS - 1) as f:
                down(gate_up(s + 10, f - 2, wg, wu, f), f - 2, wd, f - 1)
            s += 4 + 6 * (GROUPS - 2)
            for hh in range(2):
                load(s + hh, 0, wg[:, 4 * hh:4 * hh + 4, f_last:f_last + NW])
            load(s + 3, 0, wu[:, 4:8, f_last:f_last + NW])
            for f in (GROUPS - 2, GROUPS - 1):
                s += 4 if f == GROUPS - 2 else 2
                down(s, 0, wd, f)

            sp.wait_ge(route_ready, 1)
            over = sp.value_load(route[0:1, 0:1], min_val=0, max_val=OVERFLOW_PASSES)
            with sp.Fori(0, OVERFLOW_PASSES) as j:
                with sp.If(over > j):
                    e = sp.value_load(route[0:1, bass.ds(j + 1, 1)], min_val=0, max_val=NE - 1)
                    swiglu(*pass_base(None, j), *expert_weights(e))
                sp.nop()
            for t in range(NT):
                sp.wait_ge(fin_ready, t + 1)
                sp.dma_start(out_v[:, t, :], xs[:, t, :]).then_inc(out_stored, 16)
            sp.wait_ge(out_stored, 16 * NT)

        @block.gpsimd
        def _(pool):
            pool.memset(ident[:, :], 0.0).then_inc(const_step, 1)
            pool.memset(anti[:, :], 0.0).then_inc(const_step, 1)
            pool.memset(ones[:, :], 1.0).then_inc(const_step, 1)
            pool.memset(tab, NEG).then_inc(const_step, 1)
            pool.wait_ge(const_step, 1)
            pool.affine_select(out=ident[:, :], in_=ident[:, :], compare_op=ALU.not_equal, fill=1.0, base=0,
                               pattern=[[-1, P]], channel_multiplier=1).then_inc(const_step, 1)
            pool.wait_ge(const_step, 4)
            pool.affine_select(out=anti[:, :], in_=anti[:, :], compare_op=ALU.not_equal, fill=1.0,
                               base=-(P - 1), pattern=[[1, P]], channel_multiplier=1).then_inc(const_step, 1)
            pool.memset(prm[0:KC, :], 0.0).then_inc(const_step, 1)
            prm_rows = [("mlstm_conv_b", C_CONVB), ("mlstm_head_norm", C_HNORM), ("ffn_norm", C_FNORM),
                        ("diff_norm", C_DNORM), ("moe_norm", C_ENORM)]
            for name, r in prm_rows:
                pool.dma_start(prm[r:r + 8, :], A[name][0].rearrange("(c p) -> c p", p=P)).then_inc(prm_landed, 16)
            pool.dma_start(prm[C_CONVW:C_CONVW + 32, :], A["mlstm_conv_w"][0].rearrange("w (c p) -> (w c) p", p=P))\
               .then_inc(prm_landed, 16)
            pool.dma_start(prm[C_SUB:C_SUB + 1, :], A["diff_subln"]).then_inc(prm_landed, 16)
            pool.dma_start(w8[:, 0, :, :], A["mlstm_w_in"][0].rearrange("(k p) n -> p k n", p=P)[:, :, 3 * D:3 * D + 8])\
               .then_inc(w8_landed, 16)
            pool.dma_start(w8[:, 1, :, :], A["moe_w_router"][0].rearrange("(k p) n -> p k n", p=P))\
               .then_inc(w8_landed, 16)
            pool.dma_start(b_gate[:, 0:1], A["mlstm_b_igate"].rearrange("a h -> h a")).then_inc(w8_landed, 16)
            pool.dma_start(b_gate[:, 1:2], A["mlstm_b_fgate"].rearrange("a h -> h a")).then_inc(w8_landed, 16)
            pool.dma_start(b_route[:, :], A["moe_b_router"][0].partition_broadcast(P)).then_inc(w8_landed, 16)
            pool.dma_start(hot, A["bucket_hot"]).then_inc(tab_landed, 16)
            pool.dma_start(tab[0:BUCKETS, :], A["rel_bias_table"]).then_inc(tab_landed, 16)
            for i, name in enumerate(("diff_lambda_q1", "diff_lambda_k1", "diff_lambda_q2", "diff_lambda_k2")):
                pool.dma_start(lamv[:, i, :], A[name][0].partition_broadcast(P)).then_inc(lam_landed, 16)
            pool.memset(vx[:, :, :, ML_DV:ML_DVX], 1.0).then_inc(const_step, 1)
            pool.memset(headsel[:, :, :], 0.0).then_inc(const_step, 1)
            pool.memset(zrow[:, :], 0.0).then_inc(const_step, 1)
            pool.wait_ge(const_step, 9)
            pool.affine_select(out=headsel[:, :, :], in_=headsel[:, :, :], compare_op=ALU.not_equal, fill=1.0,
                               base=0, pattern=[[-1, ML_H], [0, P]], channel_multiplier=1)\
                .then_inc(const_step, 1)
            pool.wait_ge(brow_ready, 1)
            pool.dma_start(skew, brow).then_inc(brow_stored, 16)
            pool.wait_ge(e_ready, ML_H)
            for c0 in (0, T):
                d = dec[:, :, c0:c0 + P]
                pool.affine_select(out=d, in_=d, compare_op=ALU.is_ge, fill=0.0, base=0,
                                   pattern=[[0, ML_H], [1, P]], channel_multiplier=-1).then_inc(mask_ready, 1)
            pool.wait_ge(xs_ready, 2 + 2)
            pool.memset(qz[:, :, :, :], 0.0).then_inc(qz_zeroed, 1)
            pool.wait_ge(brow_stored, 16)
            pool.dma_start(bias[:, :, :], bass.AP(skew.tensor, 0, [[1, P], [BIAS_W, DMAPS], [1, T]]))\
                .then_inc(bias_landed, 16)
            pool.wait_ge(xs_ready, 2 * 3)
            pool.dma_start(moe_w[:, :], A["moe_norm"][0].partition_broadcast(P)).then_inc(rows_landed, 16)
            pool.iota(slots_i[:, :], pattern=[[1, P]], base=0, channel_multiplier=0).then_inc(const_step, 1)
            pool.memset(before[:, :], 1.0).then_inc(const_step, 1)
            pool.memset(zero8[:, :], 0.0).then_inc(const_step, 1)
            pool.wait_ge(const_step, 14)
            pool.affine_select(out=before[:, :], in_=before[:, :], compare_op=ALU.is_gt, fill=0.0, base=0,
                               pattern=[[1, P]], channel_multiplier=-1).then_inc(const_step, 1)
            pool.tensor_copy(slots[:, :], slots_i[:, :]).then_inc(const_step, 1)
            pool.wait_ge(rows_landed, 16)
            for nh in range(2):
                pool.wait_ge(x_added, 10 + 2 * nh)
                for t in range(NT):
                    c = slice(nh * NW, (nh + 1) * NW)
                    pool.tensor_tensor(xs[:, t, c], x[:, t, c], moe_w[:, c], ALU.mult).then_inc(xs_ready, 1)
            pool.wait_ge(xn_ready, NT)
            pool.dma_start(fin_w, A["final_norm"].partition_broadcast(P)).then_inc(fin_landed, 16)

        @block.tensor
        def _(pe):
            def three(out_ap, s_hi, s_lo, m_hi, m_lo, start, stop):
                pe.matmul(out_ap, s_hi, m_hi, start=start, stop=False)
                pe.matmul(out_ap, s_hi, m_lo, start=False, stop=False)
                return pe.matmul(out_ap, s_lo, m_hi, start=False, stop=stop)

            def half(s, q, k):
                pe.wait_ge(lo_ready, at(s, q) + 1)
                slot = s % SPLIT_SLOTS
                return [w[:, slot, :].rearrange("p (k n) -> p k n", k=k) for w in (w_hi, w_lo)]

            def tokens_by_columns(s, q, banks, ready=None, inserts={}):
                for hh in range(2):
                    if ready:
                        ready(hh)
                    wh, wl = half(s + hh, q, 4)
                    for k in range(4):
                        kk = 4 * hh + k
                        if kk in inserts:
                            inserts[kk]()
                        for t, b in enumerate(banks):
                            mm = three(ps[:, b, :], xt_hi[:, kk, t * P:(t + 1) * P], xt_lo[:, kk, t * P:(t + 1) * P],
                                       wh[:, k, :], wl[:, k, :], kk == 0, kk == KC - 1)
                    mm.then_inc(half_used, 1)

            def columns_by_tokens(s, banks, ready=None, inserts={}):
                for hh in range(2):
                    if ready:
                        ready(hh)
                    wh, wl = half(s + hh, 0, 4)
                    for k in range(4):
                        kk = 4 * hh + k
                        if kk in inserts:
                            inserts[kk]()
                        for c, b in enumerate(banks):
                            mm = three(ps[:, b, 0:T], wh[:, k, c * P:(c + 1) * P], wl[:, k, c * P:(c + 1) * P],
                                       xt_hi[:, kk, :], xt_lo[:, kk, :], kk == 0, kk == KC - 1)
                    mm.then_inc(half_used, 1)

            def transposes(n, src, banks, pairs):
                for i in pairs:
                    for c in (2 * i, 2 * i + 1):
                        for t in range(NT):
                            o = (c % 2) * T + t * P
                            mm = pe.transpose(ps[:, banks[i], o:o + P], src[:, t, c * P:(c + 1) * P], ident[:, :])
                    mm.then_inc(t_done, 1)

            def transpose_xs(n, u):
                for nh in range(2):
                    pe.wait_ge(xs_ready, 2 * u + nh + 1)
                    transposes(n, xs, T_BANKS[n], (2 * nh, 2 * nh + 1))

            def transpose_x(n, nh, added):
                pe.wait_ge(x_added, added)
                transposes(n, x, T_BANKS[n], (2 * nh, 2 * nh + 1))

            def xt_wait(n):
                return lambda hh: pe.wait_ge(xt_ready, 4 * n + 2 * hh + 2)

            def narrow(which, c0, n, out_ap, chunks):
                for k in chunks:
                    mm = three(out_ap, w8_hi[:, which, k, c0:c0 + n], w8_lo[:, which, k, c0:c0 + n],
                               xt_hi[:, k, :], xt_lo[:, k, :], k == 0, k == KC - 1)
                return mm

            def dense_last(s):
                for n in range(2):
                    for hh in range(2):
                        wh, wl = half(s + hh, 0, 2)
                        if n and hh:
                            transpose_x(3, 0, 6)
                        for c in range(2):
                            cc = 2 * hh + c
                            for t in range(NT):
                                mm = three(ps[:, 2 * t + n, :], hid_t_hi[:, cc, t * P:(t + 1) * P],
                                           hid_t_lo[:, cc, t * P:(t + 1) * P],
                                           wh[:, c, n * NW:(n + 1) * NW], wl[:, c, n * NW:(n + 1) * NW],
                                           False, cc == 3)
                        if n:
                            mm.then_inc(half_used, 1)
                    if not n:
                        mm.then_inc(down_half, 1)

            def expert_last(s, q, between):
                for hh in range(2):
                    if hh and between:
                        between()
                    wh, wl = half(s + hh, q, 2)
                    for n in range(2):
                        for c in range(2):
                            cc = 2 * hh + c
                            mm = three(ps[:, n, :], hid_t_hi[:, cc, 0:P], hid_t_lo[:, cc, 0:P],
                                       wh[:, c, n * NW:(n + 1) * NW], wl[:, c, n * NW:(n + 1) * NW], False, cc == 3)
                        if hh and not n:
                            mm.then_inc(y_first, 1)
                    mm.then_inc(half_used, 1)

            def swiglu(s, q, tiles, tb, after_up=None, before_last=None, last_down=None):
                def down(s, q, first):
                    for hh in range(2):
                        wh, wl = half(s + hh, q, 2)
                        for c in range(2):
                            cc = 2 * hh + c
                            for t in range(tiles):
                                for n in range(2):
                                    mm = three(ps[:, 2 * t + n, :], hid_t_hi[:, cc, t * P:(t + 1) * P],
                                               hid_t_lo[:, cc, t * P:(t + 1) * P],
                                               wh[:, c, n * NW:(n + 1) * NW], wl[:, c, n * NW:(n + 1) * NW],
                                               first and cc == 0, False)
                        mm.then_inc(half_used, 1)

                def turn(f):
                    for t in range(tiles):
                        pe.wait_ge(hid_ready, tb + f * tiles + t + 1)
                        for c in range(4):
                            mm = pe.transpose(ps[:, 6 + t, c * P:(c + 1) * P], hid[:, t, c * P:(c + 1) * P],
                                              ident[:, :])
                        mm.then_inc(hid_t_done, 1)

                gate_banks, up_banks = list(range(4, 4 + tiles)), list(range(6, 6 + tiles))

                def group(s, q, f, first):
                    tokens_by_columns(s, q, gate_banks)
                    pe.wait_ge(hid_t_ready, tb + f * tiles)
                    tokens_by_columns(s + 2, q, up_banks)
                    down(s + 4, q, first)
                    turn(f)

                tokens_by_columns(s + 2, q, up_banks)
                if after_up:
                    after_up()
                turn(0)
                group(s + 4, q, 1, True)
                with pe.Fori(2, GROUPS) as f:
                    group(s + 4, q + (f - 1), f, False)
                if before_last:
                    before_last()
                pe.wait_ge(hid_t_ready, tb + GROUPS * tiles)
                last_down(s + 4 + 6 * (GROUPS - 1), q)

            pe.wait_ge(const_step, 6)
            pe.wait_ge(mnorm_landed, 16)
            pe.transpose(ps[:, 7, 0:KC], mnorm_rows[:, :], ident[0:KC, 0:KC]).then_inc(col_t, 1)

            transpose_xs(0, 0)
            pe.wait_ge(col_ready, 1)
            columns_by_tokens(HALF_Q, [4, 5, 6, 7], xt_wait(0))
            pe.wait_ge(prm_landed, 16 * PRM_LOADS)
            pe.wait_ge(const_step, 7)
            pe.transpose(ps[:, 3, 0:PRM], prm[:, :], ident[0:PRM, 0:PRM]).then_inc(col_t, 1)
            pe.wait_ge(col_ready, 2)
            columns_by_tokens(HALF_K, [0, 1, 2, 3])
            pe.wait_ge(w8_ready, 1)
            pe.wait_ge(conv_ready, 1)
            for g in range(2):
                mm = narrow(0, g * ML_H, ML_H, ps[0:ML_H, 4, g * T:(g + 1) * T], range(KC))
            mm.then_inc(grow_done, 1)
            pe.wait_ge(conv_ready, 3)
            tokens_by_columns(HALF_V, 0, [5, 6])
            pe.wait_ge(conv_ready, 5)
            tokens_by_columns(HALF_V + 2, 0, [7, 0])
            pe.wait_ge(v_ready, 1)
            tokens_by_columns(HALF_O, 0, [5, 6])
            pe.wait_ge(tab_landed, 32)
            pe.wait_ge(grow_ready, 2)
            pe.matmul(ps[0:DMAPS, 4, 0:BIAS_W], tab, hot, start=True, stop=True).then_inc(brow_done, 1)
            pe.wait_ge(conv_ready, 8)
            pe.wait_ge(const_step, 11)
            pe.wait_ge(gm_ready, 1)
            for h in range(ML_H):
                pe.matmul(ps[:, 1 + h // 2, (h % 2) * T:(h % 2 + 1) * T], headsel[:, h, :], g_max[:, :],
                          start=True, stop=True)
            pe.wait_ge(gem_ready, 1)
            for i, g in enumerate((g_a, g_em2)):
                for t in range(NT):
                    o = i * 8 + t * ML_H
                    mm = pe.transpose(ps[:, 3, o:o + ML_H], g[:, t * P:(t + 1) * P], ident[0:ML_H, 0:ML_H])
            mm.then_inc(gbc_done, 1)
            pe.wait_ge(v_ready, 2)
            tokens_by_columns(HALF_O + 2, 0, [7, 0])
            pe.wait_ge(qk_ready, 8)
            pe.wait_ge(z_ready, ML_H)
            pe.wait_ge(brow_ready, 1)
            st_bank = [4, 3, 1, 2]
            for h in range(ML_H):
                b = st_bank[h]
                pe.matmul(ps[:, b, 0:T], qk[:, ML_H + h, 0:P], qk[:, h, :], start=True, stop=True)
                pe.matmul(ps[:, b, T:ROW], qk[:, ML_H + h, P:T], qk[:, h, P:T], start=True, stop=True)\
                  .then_inc(st_done, 1)
            for h in range(ML_H):
                pe.wait_ge(prob_ready, ML_H if h >= 2 else h + 1)
                if h < 2:
                    pe.wait_ge(o_ready, h + 1)
                b0, b1 = (5 + 2 * h) % 8, (6 + 2 * h) % 8
                pe.matmul(ps[:, b0, 0:ML_DVX], prob[:, h, 0:P], vx[:, 0, h, :], start=True, stop=True)\
                  .then_inc(pv_done, 1)
                pe.matmul(ps[:, b1, 0:ML_DVX], prob[:, h, P:T], vx[:, 0, h, :], start=True, stop=False)
                pe.matmul(ps[:, b1, 0:ML_DVX], prob[:, h, T:ROW], vx[:, 1, h, :], start=False, stop=True)\
                  .then_inc(pv_done, 1)
            transpose_xs(1, 1)
            tokens_by_columns(HALF_MOUT, 0, [1, 2], xt_wait(1))
            tokens_by_columns(HALF_MOUT + 2, 0, [0, 3], inserts={4: lambda: transpose_x(2, 0, 2)})

            tokens_by_columns(HALF_FFN, 0, [4, 5], xt_wait(2), inserts={2: lambda: transpose_x(2, 1, 4)})
            swiglu(HALF_FFN, 0, NT, 0, 
                   last_down=lambda s, q: dense_last(s))

            def row_of_roots():
                pe.wait_ge(x_added, 8)
                pe.wait_ge(diag_ready, 1)
                pe.matmul(ps[:, 1, 0:T], ones[:, :], diag[:, :, :].rearrange("p t k -> p (t k)"),
                          start=True, stop=True).then_inc(rrow_done, 1)

            columns_by_tokens(HALF_DQ, BANKS_A, xt_wait(3), 
                              inserts={3: lambda: transpose_x(3, 1, 8), 6: row_of_roots})
            pe.wait_ge(rrow_ready, 1)
            columns_by_tokens(HALF_DQ + 2, BANKS_B)
            pe.wait_ge(dq_ready, 1)
            columns_by_tokens(HALF_DK, BANKS_A)
            pe.wait_ge(dq_ready, 2)
            columns_by_tokens(HALF_DK + 2, BANKS_B)
            pe.wait_ge(dk_ready, 1)
            tokens_by_columns(HALF_DVV, 0, [6, 7])
            tokens_by_columns(HALF_DVV + 2, 0, [0, 2])
            pe.wait_ge(dk_ready, 2)
            pe.wait_ge(bias_landed, 16)
            units = [(h, t) for h in range(DH) for t in range(NT)]

            def logits(i):
                h, t = units[i]
                if i == 2:
                    pe.wait_ge(dv_ready, 1)
                if i >= 3:
                    pe.wait_ge(exp_ready, i - 2)
                for m in range(2):
                    o = ps[:, 4 + i % 3, m * T:m * T + (t + 1) * P]
                    pe.matmul(o, anti[:, :], bias[:, 2 * h + m, (1 - t) * P:T], start=True, stop=False)
                    mm = pe.matmul(o, qz[:, h, m, t * P:(t + 1) * P], kt[:, h, 0:(t + 1) * P],
                                   start=False, stop=True)
                mm.then_inc(logit_done, 1)

            def turn_a(i):
                h, t = units[i]
                pe.wait_ge(a_ready, i + 1)
                if i >= 1:
                    pe.wait_ge(at_ready, i)
                for b in range(t + 1):
                    mm = pe.transpose(ps[:, 7, b * P:(b + 1) * P], aw[:, i % 2, b * P:(b + 1) * P],
                                      ident[:, :])
                mm.then_inc(at_done, 1)

            def values(i):
                h, t = units[i]
                pe.wait_ge(at_ready, i + 1)
                if i == 0:
                    pe.wait_ge(dv_ready, 2)
                c = (h % 4) * P
                for b in range(t + 1):
                    mm = pe.matmul(ps[:, 2 * t + h // 4, c:c + P], awt[:, i % 2, b * P:(b + 1) * P],
                                   vv[:, b, h * DDV:(h + 1) * DDV], start=(b == 0), stop=(b == t))
                mm.then_inc(opv_done, 1)

            logits(0)
            logits(1)
            for i in range(len(units)):
                if i + 2 < len(units):
                    logits(i + 2)
                if i >= 1:
                    values(i - 1)
                turn_a(i)
            values(len(units) - 1)
            transpose_xs(4, 2)
            tokens_by_columns(HALF_DOUT, 0, [0, 2], xt_wait(4))
            tokens_by_columns(HALF_DOUT + 2, 0, [1, 3], inserts={4: lambda: transpose_x(5, 0, 10)})

            xt_wait(5)(0)
            narrow(1, 0, NE, ps[0:NE, 0, 0:T], range(KC // 2))
            transpose_x(5, 1, 12)
            for i in (2, 3):
                pe.wait_ge(xt_ready, 4 * 5 + i + 1)
                mm = narrow(1, 0, NE, ps[0:NE, 0, 0:T], (2 * i, 2 * i + 1))
            mm.then_inc(router_done, 1)
            pe.wait_ge(lrow_ready, 1)
            for t in range(NT):
                mm = pe.transpose(ps[:, 5, t * NE:(t + 1) * NE], lrow[:, t * P:(t + 1) * P], ident[0:NE, 0:NE])
            mm.then_inc(lcol_done, 1)
            pe.wait_ge(chosen_ready, 1)
            pe.wait_ge(const_step, 16)
            pe.matmul(ps[:, 6, 8:16], before[:, :], rt[:, 0, 1, :], start=True, stop=False)
            pe.matmul(ps[:, 6, 8:16], ones[:, :], rt[:, 0, 0, :], start=False, stop=True)
            pe.matmul(ps[:, 6, 0:8], before[:, :], rt[:, 0, 0, :], start=True, stop=True).then_inc(pos_done, 1)
            pe.matmul(ps[:, 5, 16:24], ones[:, :], rt[:, 0, 0, :], start=True, stop=False)
            pe.matmul(ps[:, 5, 16:24], ones[:, :], rt[:, 0, 1, :], start=False, stop=True).then_inc(pos_done, 1)
            pe.wait_ge(xn_ready, NT)

            def gather(n):
                pe.wait_ge(pick_ready, n + 1)
                for nh in range(2):
                    for i, (xn, t) in enumerate([(xn, t) for xn in (xn_hi, xn_lo) for t in range(NT)]):
                        mm = pe.matmul(ps[:, 2 + nh, :], pick[:, t, :], xn[:, t, nh * NW:(nh + 1) * NW],
                                       start=(i == 0), stop=(i == 3))
                    mm.then_inc(gather_done, 1)

            def turn_gathered(n):
                for b in range(2):
                    pe.wait_ge(xg_ready[b], n + 1)
                    for c in range(4):
                        f0 = (4 * b + c) * P
                        mm = pe.transpose(ps[:, 2 + b, c * P:(c + 1) * P], xg[:, f0:f0 + P], ident[:, :])
                    mm.then_inc(xg_turned, 1)

            def first_gate(n, s, q):
                tokens_by_columns(s, q, [4], lambda hh: pe.wait_ge(xe_ready, n * 2 + hh + 1))

            def transpose_pick(n):
                pe.wait_ge(x_combined, n * 4 + 1)
                for t in range(NT):
                    pe.transpose(ps[:, 7, t * P:(t + 1) * P], pick[:, t, :].bitcast(F32), ident[:, :])
                for t in range(NT):
                    mm = pe.matmul(ps[:, 7, T:T + 1], pick[:, t, :].bitcast(F32), cur[:, 4 + t:5 + t],
                                   start=(t == 0), stop=(t == NT - 1))
                mm.then_inc(pick_t_done, 1)

            def combine(n):
                pe.wait_ge(pick_t_ready, n + 1)
                for nh in range(2):
                    pe.wait_ge(y_ready, n * 2 + nh + 1)
                    for t in range(NT):
                        for y in (y_hi, y_lo):
                            mm = pe.matmul(ps[:, combine_bank[nh][t], :], pick_t[:, t * P:(t + 1) * P],
                                           y[:, nh * NW:(nh + 1) * NW], start=(y is y_hi), stop=(y is y_lo))
                        mm.then_inc(combine_done, 1)

            def expert(n, follows, j=None):
                s, q = pass_base(n, j)
                swiglu(s, q, 1, NT * GROUPS + n * GROUPS,
                       after_up=lambda: transpose_pick(n),
                       before_last=(lambda: gather(n + 1)) if follows else None,
                       last_down=lambda s, q: expert_last(s, q, (lambda: turn_gathered(n + 1)) if follows else None))
                if follows:
                    first_gate(n + 1, s + 6 * GROUPS, q)
                combine(n)

            gather(0)
            turn_gathered(0)
            first_gate(0, HALF_MOE, 0)
            with pe.Fori(0, NE - 1) as n:
                expert(n, True)
            expert(NE - 1, False)
            pe.wait_ge(route_ready, 1)
            over = pe.value_load(route[0:1, 0:1], min_val=0, max_val=OVERFLOW_PASSES)
            with pe.Fori(0, OVERFLOW_PASSES) as j:
                with pe.If(over > j):
                    gather(j + NE)
                    turn_gathered(j + NE)
                    first_gate(j + NE, *pass_base(None, j))
                    expert(j + NE, False, j)
                pe.nop()

        @block.scalar
        def _(act):
            self_n = [0]

            def mine(ins):
                ins.then_inc(act_self, 1)
                self_n[0] += 1
                act.wait_ge(act_self, self_n[0])

            def hi(s, q=0):
                if s in EXTRA_HALVES:
                    i = EXTRA_HALVES.index(s)
                    act.wait_ge(extra_landed[i], 16)
                    src = extra[:, i, :]
                else:
                    r = raw_at(s)
                    act.wait_ge(raw_landed[r % RAW_SLOTS], (q + (r // RAW_SLOTS + 1)) * 16)
                    src = raw[:, r % RAW_SLOTS, :]
                wait_from(act, half_used, at(s, q) - SPLIT_SLOTS + 1)
                act.activation(w_hi[:, s % SPLIT_SLOTS, :], src, ACT.Copy).then_inc(hi_ready, 1)

            def squares(nh):
                c = slice(nh * NW, (nh + 1) * NW)
                for t in range(NT):
                    act.activation((gate_act, hid)[nh][:, t, :], x[:, t, c], ACT.Square,
                                   accum_out=small[:, S_SQ + 2 * t + nh:S_SQ + 2 * t + nh + 1]).then_inc(ss_ready, 1)

            def root(n):
                act.wait_ge(ms_ready, n + 1)
                act.activation(small[:, S_ROOT:S_ROOT + 2], small[:, S_MS:S_MS + 2], ACT.Sqrt).then_inc(root_ready, 1)

            def evac_xt(n, c0, pairs=range(4), scale=None):
                for i in pairs:
                    act.wait_ge(t_done, 4 * n + i + 1)
                    for j in range(2):
                        c = 2 * i + j
                        w = scale if scale is not None else col[:, c0 + c:c0 + c + 1]
                        ins = act.activation(xt_hi[:, c, :], ps[:, T_BANKS[n][i], j * T:(j + 1) * T], ACT.Copy, scale=w)
                    ins.then_inc(t_hi, 1)

            def swiglu(s, q, tiles, tb, after_gate=None, scale=lambda t: 1.0):
                def evac(f):
                    for t in range(tiles):
                        act.wait_ge(hid_t_done, tb + tiles * f + t + 1)
                        act.activation(hid_t_hi[:, :, t * P:(t + 1) * P],
                                       ps[:, 6 + t, :].rearrange("p (c t) -> p c t", c=4), ACT.Copy)\
                           .then_inc(hid_t_h, 1)

                def gate(s, q):
                    act.wait_ge(half_used, at(s, q) + 2)
                    for t in range(tiles):
                        act.activation(gate_act[:, t, :], ps[:, 4 + t, :], ACT.Silu, scale=scale(t)).then_inc(silu_ready, 1)

                gate(s, q)
                for i in (4, 5):
                    hi(s + i, q)
                if after_gate:
                    after_gate()
                def group(f, s1, q1):
                    evac(f - 1)
                    for i in (2, 3):
                        hi(s1 + i, q1)
                    gate(s1, q1)
                    for i in (4, 5, 6, 7):
                        hi(s1 + i, q1)

                with act.Fori(1, GROUPS - 1) as f:
                    group(f, s + 4, q + (f - 1))
                group(GROUPS - 1, s + 4 + 6 * (GROUPS - 2), q)
                evac(GROUPS - 1)

            act.dma_start(mnorm_rows[:, :], A["mlstm_norm"][0].rearrange("(c p) -> c p", p=P)).then_inc(mnorm_landed, 16)

            act.preload_act_table(ACT.Sqrt)
            for t in range(NT):
                act.wait_ge(x_landed[t], 16)
                act.activation(xs[:, t, :], x[:, t, :], ACT.Square, accum_out=small[:, S_SQ + 2 * t:S_SQ + 2 * t + 1])\
                   .then_inc(ss_ready, 1)
            root(0)
            act.wait_ge(col_ready, 1)
            hi(0)
            evac_xt(0, C_MNORM, (0, 1))
            hi(1)
            evac_xt(0, C_MNORM, (2, 3))
            hi(2)
            hi(3)

            def silu_qk(c):
                act.wait_ge(conv_ready, c + 1)
                act.activation(qk[:, c, :], qk[:, c, :], ACT.Silu).then_inc(qk_ready, 1)

            act.wait_ge(w8_landed, 16 * 5)
            act.activation(w8_hi[:, :, :, :], w8[:, :, :, :], ACT.Copy).then_inc(w8h_ready, 1)
            for c in (0, 1):
                silu_qk(c)
            hi(4)
            for c in (2, 3):
                silu_qk(c)
            hi(5)
            hi(6)
            for c in (4, 5):
                silu_qk(c)
            hi(7)
            for c in (6, 7):
                silu_qk(c)
            hi(8)

            def evac_v(n, banks):
                act.wait_ge(half_used, HALF_V + 2 * n + 2)
                for t, b in enumerate(banks):
                    ins = act.activation(vx[:, t, 2 * n:2 * n + 2, 0:ML_DV],
                                         ps[:, b, :].rearrange("p (h v) -> p h v", h=2), ACT.Copy)
                ins.then_inc(v_ready, 1)

            def evac_o(n, banks):
                act.wait_ge(half_used, HALF_O + 2 * n + 2)
                for t, b in enumerate(banks):
                    ins = act.activation(sig_o[:, t, n * NW:(n + 1) * NW], ps[:, b, :], ACT.Sigmoid)
                ins.then_inc(o_ready, 1)

            evac_v(0, (5, 6))
            hi(9)
            act.wait_ge(gabs_ready, 1)
            mine(act.activation(g_exp[:, :], g_abs[:, :], ACT.Exp, scale=-1.0))
            act.activation(g_ln[:, :], g_exp[:, :], ACT.Ln, bias=1.0).then_inc(gln_ready, 1)
            hi(10)
            evac_v(1, (7, 0))
            act.wait_ge(gm_ready, 2)
            act.activation(g_em2[:, :], g_m[:, :], ACT.Exp, scale=-2.0).then_inc(gem_ready, 1)
            hi(11)
            hi(12)
            evac_o(0, (5, 6))
            for h in range(ML_H):
                act.wait_ge(z_ready, h + 1)
                act.activation(dec[:, h, :], dec[:, h, :], ACT.Exp, scale=-1.0).then_inc(e_ready, 1)
            hi(13)
            evac_o(1, (7, 0))
            act.preload_act_table(ACT.Sqrt)
            for r in range(2 * ML_H):
                act.wait_ge(pv_done, r + 1)
                act.activation(xs[:, r // 4, (r % 4) * ML_DV:(r % 4 + 1) * ML_DV], ps[:, (5 + r) % 8, 0:ML_DV],
                               ACT.Square, accum_out=mn[:, 0, r:r + 1])
                ins = act.activation(mn[:, 3, r:r + 1], ps[:, (5 + r) % 8, ML_DV:ML_DVX], ACT.Square)
            ins.then_inc(ss_ready, 1)
            act.wait_ge(ms_ready, 2)
            act.activation(mn[:, 2, :], mn[:, 1, :], ACT.Sqrt).then_inc(root_ready, 1)
            evac_xt(1, C_HNORM)
            def sum_and_norm(n, s, added, c0):
                for i in range(3):
                    hi(s + i)
                act.wait_ge(x_added, added - 2)
                squares(0)
                hi(s + 3)
                evac_xt(n, c0, (0, 1))

            act.wait_ge(brow_stored, 16)
            sum_and_norm(2, HALF_MOUT + 2, 4, C_FNORM)

            hi(HALF_FFN + 2)
            act.wait_ge(x_added, 4)
            squares(1)
            evac_xt(2, C_FNORM, (2, 3))
            root(2)
            hi(HALF_FFN + 3)
            act.wait_ge(recip_ready, 1)
            swiglu(HALF_FFN, 0, NT, 0, scale=lambda t: small[:, S_RSTD + t:S_RSTD + t + 1])
            hi(HALF_DQ)
            act.preload_act_table(ACT.Sqrt)

            act.wait_ge(x_added, 6)
            squares(0)
            evac_xt(3, C_DNORM, (0, 1))
            hi(HALF_DQ + 1)
            evac_xt(3, C_DNORM, (2, 3))
            act.wait_ge(x_added, 8)
            squares(1)
            root(3)
            for i in range(HALF_DQ + 2, HALF_DK + 2):
                hi(i)
            act.wait_ge(lam_dot, 1)
            act.activation(lam[:, 2:4], lam[:, 0:2], ACT.Exp).then_inc(lam_exp, 1)
            for i in range(HALF_DK + 2, HALF_DVV + 4):
                hi(i)

            def copy_v(n, banks):
                act.wait_ge(half_used, HALF_DVV + 2 * n + 2)
                for t, b in enumerate(banks):
                    ins = act.activation(vv[:, t, n * NW:(n + 1) * NW], ps[:, b, :], ACT.Copy,
                                         scale=small[:, S_RSTD + t:S_RSTD + t + 1])
                ins.then_inc(dv_ready, 1)

            act.wait_ge(recip_ready, 2)
            copy_v(0, (6, 7))
            hi(HALF_DOUT)
            hi(HALF_DOUT + 1)
            copy_v(1, (0, 2))

            def square_outputs(banks, done):
                act.wait_ge(opv_done, done)
                for b in banks:
                    act.activation(osq[b], ps[:, b, :], ACT.Square).then_inc(osq_ready, 1)

            for i in range(2 * DH):
                klen = (i % 2 + 1) * P
                act.wait_ge(max_ready, i + 1)
                if i >= 2:
                    act.wait_ge(a_ready, i - 1)
                for m in range(2):
                    ins = act.activation(ex[:, i % 2, m, 0:klen], ps[:, 4 + i % 3, m * T:m * T + klen], ACT.Exp,
                                         scale=-1.0, bias=nmx[:, i % 3, m:m + 1], accum_out=sm[:, i % 2, m:m + 1])
                ins.then_inc(exp_ready, 1)

                def evac_a(i):
                    klen = (i % 2 + 1) * P
                    act.wait_ge(at_done, i + 1)
                    if i >= 2:
                        act.wait_ge(opv_done, i - 1)
                    act.activation(awt[:, i % 2, 0:klen], ps[:, 7, 0:klen], ACT.Copy).then_inc(at_ready, 1)

                if i == 2 * DH - 1:
                    act.preload_act_table(ACT.Sqrt)
                if i >= 1:
                    evac_a(i - 1)
                if i == DH + 2:
                    square_outputs((0, 2), DH)
            evac_a(2 * DH - 1)
            square_outputs((1,), 2 * DH - 1)
            square_outputs((3,), 2 * DH)
            act.wait_ge(oms_ready, 1)
            act.activation(oms[:, 2, :], oms[:, 1, :], ACT.Sqrt).then_inc(oroot_ready, 1)
            evac_xt(4, None, scale=sub_w[:, 0:1])
            sum_and_norm(5, HALF_DOUT + 2, 12, C_ENORM)

            hi(HALF_MOE + 2)
            evac_xt(5, C_ENORM, (2, 3))
            squares(1)
            root(4)
            act.preload_act_table(ACT.Exp)
            act.wait_ge(recip_ready, 3)
            act.wait_ge(xs_ready, 2 * 3 + 4)
            for t in range(NT):
                act.activation(xn_hi[:, t, :], xs[:, t, :], ACT.Copy, scale=small[:, S_RSTD + t:S_RSTD + t + 1])\
                   .then_inc(xn_h, 1)
            act.wait_ge(gap_ready, 1)
            act.activation(gsc[:, :, 1:2], gsc[:, :, 0:1], ACT.Exp).then_inc(gexp_ready, 1)

            def gathered_rows(n):
                act.wait_ge(gather_done, n * 2 + 1)
                act.activation(xg[:, 0:NW], ps[:, 2, :], ACT.Copy).then_inc(xg_ready[0], 1)

            def gathered(n):
                for b in range(2):
                    act.wait_ge(xg_turned, n * 2 + b + 1)
                    act.activation(xt_hi[:, 4 * b:4 * b + 4, 0:P], ps[:, 2 + b, :].rearrange("p (c t) -> p c t", c=4),
                                   ACT.Copy).then_inc(xe_hi, 1)

            def picked(n):
                act.wait_ge(pick_t_done, n + 1)
                act.activation(pick_t[:, :], ps[:, 7, 0:T], ACT.Copy)
                act.activation(gslot[:, :], ps[:, 7, T:T + 1], ACT.Copy).then_inc(pick_t_ready, 1)

            def expert(n, follows, j=None):
                s, q = pass_base(n, j)
                nxt = s + 6 * GROUPS
                swiglu(s, q, 1, NT * GROUPS + n * GROUPS, lambda: picked(n))
                if follows:
                    gathered_rows(n + 1)
                    hi(nxt, q)
                    gathered(n + 1)
                    hi(nxt + 1, q)
                act.wait_ge(pick_t_ready, n + 1)
                for nh in range(2):
                    if nh == 0:
                        act.wait_ge(y_first, n + 1)
                    else:
                        act.wait_ge(half_used, n * (6 * GROUPS) + (HALF_MOE + 6 * GROUPS))
                    act.activation(y_hi[:, nh * NW:(nh + 1) * NW], ps[:, nh, :], ACT.Copy, scale=gslot[:, 0:1])\
                       .then_inc(y_h, 1)
                if follows:
                    hi(nxt + 2, q)
                    hi(nxt + 3, q)

            gathered_rows(0)
            gathered(0)
            hi(HALF_MOE + 3)
            with act.Fori(0, NE - 1) as n:
                expert(n, True)
            expert(NE - 1, False)
            act.wait_ge(route_ready, 1)
            over = act.value_load(route[0:1, 0:1], min_val=0, max_val=OVERFLOW_PASSES)
            with act.Fori(0, OVERFLOW_PASSES) as j:
                with act.If(over > j):
                    hi(HALF_OVER, j * GROUPS)
                    hi(HALF_OVER + 1, j * GROUPS)
                    gathered_rows(j + NE)
                    gathered(j + NE)
                    hi(HALF_OVER + 2, j * GROUPS)
                    hi(HALF_OVER + 3, j * GROUPS)
                    expert(j + NE, False, j)
                act.nop()
            act.preload_act_table(ACT.Sqrt)
            for nh in range(2):
                act.wait_ge(x_combined, over * 4 + (4 * NE - 1 + 2 * nh))
                squares(nh)
            root(5)

        @block.vector
        def _(dve):
            self_n = [0]

            def own(ins):
                ins.then_inc(dve_self, 1)
                self_n[0] += 1
                dve.wait_ge(dve_self, self_n[0])

            def lo(s, q=0):
                ring = s % SPLIT_SLOTS
                src = extra[:, EXTRA_HALVES.index(s), :] if s in EXTRA_HALVES else raw[:, raw_at(s) % RAW_SLOTS, :]
                dve.wait_ge(hi_ready, at(s, q) + 1)
                dve.tensor_tensor(w_lo[:, ring, :], src, w_hi[:, ring, :].bitcast(F32), ALU.subtract)\
                   .then_inc(lo_ready, 1)

            def mean(ss):
                dve.wait_ge(ss_ready, ss)
                sq = small[:, S_SQ:S_SQ + 4].rearrange("p (t n) -> p t n", t=NT)
                own(dve.tensor_tensor(small[:, S_MS:S_MS + 2], sq[:, :, 0], sq[:, :, 1], ALU.add))
                dve.tensor_scalar(small[:, S_MS:S_MS + 2], small[:, S_MS:S_MS + 2], 1.0 / D, EPS, ALU.mult, ALU.add)\
                   .then_inc(ms_ready, 1)

            def inverse(n):
                dve.wait_ge(root_ready, n)
                return dve.reciprocal(small[:, S_RSTD:S_RSTD + 2], small[:, S_ROOT:S_ROOT + 2])

            def evac_xt(n, c0, pairs=range(4), scale=None):
                for i in pairs:
                    dve.wait_ge(t_hi, 4 * n + i + 1)
                    for j in range(2):
                        c = 2 * i + j
                        w = scale if scale is not None else col[:, c0 + c:c0 + c + 1]
                        ins = dve.scalar_tensor_tensor(out=xt_lo[:, c, :], in0=ps[:, T_BANKS[n][i], j * T:(j + 1) * T],
                                                       scalar=w, in1=xt_hi[:, c, :].bitcast(F32),
                                                       op0=ALU.mult, op1=ALU.subtract)
                    ins.then_inc(xt_ready, 1)

            def add_x(banks, n):
                for t, b in enumerate(banks):
                    xv = x[:, t, n * NW:(n + 1) * NW]
                    dve.tensor_tensor(xv, ps[:, b, :], xv, ALU.add).then_inc(x_added, 1)

            def swiglu(s, q, tiles, tb, after_hidden=None, scale=None):
                def evac(f):
                    for t in range(tiles):
                        dve.wait_ge(hid_t_h, tb + tiles * f + t + 1)
                        dve.tensor_tensor(hid_t_lo[:, :, t * P:(t + 1) * P],
                                          ps[:, 6 + t, :].rearrange("p (c t) -> p c t", c=4),
                                          hid_t_hi[:, :, t * P:(t + 1) * P].bitcast(F32), ALU.subtract)\
                           .then_inc(hid_t_ready, 1)

                def hidden(s, q, f):
                    dve.wait_ge(half_used, at(s, q) + 4)
                    for t in range(tiles):
                        dve.wait_ge(silu_ready, tb + tiles * f + t + 1)
                        if scale:
                            ins = dve.scalar_tensor_tensor(out=hid[:, t, :], in0=ps[:, 6 + t, :], scalar=scale(t),
                                                           in1=gate_act[:, t, :], op0=ALU.mult, op1=ALU.mult)
                        else:
                            ins = dve.tensor_tensor(hid[:, t, :], ps[:, 6 + t, :], gate_act[:, t, :], ALU.mult)
                        ins.then_inc(hid_ready, 1)

                lo(s + 4, q)
                hidden(s, q, 0)
                lo(s + 5, q)
                if after_hidden:
                    after_hidden()
                def group(f, s1, q1):
                    evac(f - 1)
                    for i in (2, 3, 4, 5):
                        lo(s1 + i, q1)
                    hidden(s1, q1, f)
                    lo(s1 + 6, q1)
                    return s1 + 7, q1

                with dve.Fori(1, GROUPS - 1) as f:
                    lo(*group(f, s + 4, q + (f - 1)))
                last = group(GROUPS - 1, s + 4 + 6 * (GROUPS - 2), q)
                evac(GROUPS - 1)
                lo(*last)

            dve.wait_ge(ss_ready, 2)
            dve.tensor_scalar(small[:, S_MS:S_MS + 2], small[:, S_SQ:S_SQ + 4:2], 1.0 / D, EPS, ALU.mult, ALU.add)\
               .then_inc(ms_ready, 1)
            own(inverse(1))
            for nh in range(2):
                for t in range(NT):
                    c = slice(nh * NW, (nh + 1) * NW)
                    ins = dve.tensor_scalar(xs[:, t, c], x[:, t, c], small[:, S_RSTD + t:S_RSTD + t + 1], None, ALU.mult)
                ins.then_inc(xs_ready, 1)
            dve.wait_ge(col_t, 1)
            dve.tensor_copy(col[:, 0:KC], ps[:, 7, 0:KC]).then_inc(col_ready, 1)
            lo(0)
            evac_xt(0, C_MNORM, (0, 1))
            lo(1)
            evac_xt(0, C_MNORM, (2, 3))
            lo(2)
            lo(3)

            def conv_pair(c0):
                dve.wait_ge(half_used, 2 if c0 < 4 else 4)
                for d in range(CONV_W):
                    for c in (c0, c0 + 1):
                        b = 4 + c if c < 4 else c - 4
                        w = col[:, C_CONVW + (CONV_W - 1 - d) * 8 + c:C_CONVW + (CONV_W - 1 - d) * 8 + c + 1]
                        if d == 0:
                            ins = dve.tensor_scalar(qk[:, c, :], ps[:, b, 0:T], w, col[:, C_CONVB + c:C_CONVB + c + 1],
                                                    ALU.mult, ALU.add)
                        else:
                            ins = dve.scalar_tensor_tensor(out=qk[:, c, d:T], in0=ps[:, b, 0:T - d], scalar=w,
                                                           in1=qk[:, c, d:T], op0=ALU.mult, op1=ALU.add)
                        if d == CONV_W - 1:
                            ins.then_inc(conv_ready, 1)
                        elif c == c0:
                            ins.then_inc(dve_self, 1)
                            self_n[0] += 1
                        else:
                            own(ins)

            dve.wait_ge(col_t, 2)
            dve.tensor_copy(col[:, KC:PRM], ps[:, 3, KC:PRM]).then_inc(col_ready, 1)
            dve.wait_ge(col_ready, 2)
            conv_pair(0)
            dve.wait_ge(w8h_ready, 1)
            dve.tensor_tensor(w8_lo[:, :, :, :], w8[:, :, :, :], w8_hi[:, :, :, :].bitcast(F32), ALU.subtract)\
               .then_inc(w8_ready, 1)
            lo(4)
            conv_pair(2)
            lo(5)
            lo(6)
            conv_pair(4)
            lo(7)
            conv_pair(6)
            lo(8)
            dve.wait_ge(grow_done, 1)
            dve.wait_ge(w8_landed, 16 * 5)
            for g in range(2):
                ins = dve.tensor_scalar(grow[:, g * T:(g + 1) * T], ps[0:ML_H, 4, g * T:(g + 1) * T],
                                        b_gate[:, g:g + 1], None, ALU.add)
                ins.then_inc(grow_ready, 1)
            dve.wait_ge(grow_ready, 2)
            dve.scalar_tensor_tensor(out=g_abs[:, :], in0=grow[:, T:2 * T], scalar=-1.0, in1=grow[:, T:2 * T],
                                     op0=ALU.mult, op1=ALU.max).then_inc(gabs_ready, 1)
            dve.wait_ge(gln_ready, 1)
            own(dve.scalar_tensor_tensor(out=g_logf[:, :], in0=grow[:, T:2 * T], scalar=0.0, in1=g_ln[:, :],
                                         op0=ALU.min, op1=ALU.subtract))
            dve.wait_ge(const_step, 10)
            own(dve.tensor_tensor_scan(g_cum[:, :], g_logf[:, :], zrow[:, :], 0.0, ALU.add, ALU.add))
            own(dve.tensor_tensor(g_a[:, :], grow[:, 0:T], g_cum[:, :], ALU.subtract))
            dve.tensor_tensor_scan(g_max[:, :], g_a[:, :], g_a[:, :], 0.0, ALU.max, ALU.max).then_inc(gm_ready, 1)
            dve.wait_ge(gm_ready, 1)
            own(dve.tensor_tensor(g_m[:, :], g_cum[:, :], g_max[:, :], ALU.add))
            dve.tensor_scalar(g_m[:, :], g_m[:, :], -40.0, None, ALU.max).then_inc(gm_ready, 1)
            for i in (9, 10, 11):
                lo(i)
            dve.wait_ge(brow_done, 1)
            dve.tensor_scalar(brow, ps[0:DMAPS, 4, 0:BIAS_W], -1.0, None, ALU.mult).then_inc(brow_ready, 1)
            lo(12)
            dve.wait_ge(gbc_done, 1)
            own(dve.tensor_copy(acol[:, :, :], ps[:, 3, 0:8].rearrange("p (t h) -> p t h", t=NT)))
            dve.tensor_copy(em2[:, :].rearrange("p (h t) -> p t h", t=NT),
                            ps[:, 3, 8:16].rearrange("p (t h) -> p t h", t=NT)).then_inc(acol_ready, 1)
            for h in range(ML_H):
                mb = ps[:, 1 + h // 2, (h % 2) * T:(h % 2 + 1) * T]
                dve.tensor_scalar(dec[:, h, 0:T], mb, acol[:, 0, h:h + 1], 0.0, ALU.subtract, ALU.max)
                dve.tensor_scalar(dec[:, h, T:ROW], mb[:, P:T], acol[:, 1, h:h + 1], 0.0, ALU.subtract, ALU.max)\
                   .then_inc(z_ready, 1)
            lo(13)
            dve.wait_ge(mask_ready, 2)
            for h, b in enumerate([4, 3, 1, 2]):
                dve.wait_ge(st_done, h + 1)
                dve.scalar_tensor_tensor(out=prob[:, h, :], in0=ps[:, b, 0:ROW], scalar=ML_SCALE, in1=dec[:, h, :],
                                         op0=ALU.mult, op1=ALU.mult).then_inc(prob_ready, 1)
            dve.wait_ge(acol_ready, 1)
            dve.wait_ge(ss_ready, 3)
            dve.tensor_scalar(mn[:, 5, :], mn[:, 0, :], 1.0 / ML_DV, None, ALU.mult)
            own(dve.tensor_tensor(mn[:, 4, :], mn[:, 3, :], em2[:, :], ALU.max))
            dve.scalar_tensor_tensor(out=mn[:, 1, :], in0=mn[:, 4, :], scalar=EPS, in1=mn[:, 5, :],
                                     op0=ALU.mult, op1=ALU.add).then_inc(ms_ready, 1)
            dve.wait_ge(root_ready, 2)
            own(dve.reciprocal(mn[:, 6, :], mn[:, 2, :]))
            dve.wait_ge(o_ready, 2)
            for r in range(2 * ML_H):
                h, t = divmod(r, 2)
                c = slice(h * ML_DV, (h + 1) * ML_DV)
                ins = dve.scalar_tensor_tensor(out=xs[:, t, c], in0=ps[:, (5 + r) % 8, 0:ML_DV], scalar=mn[:, 6, r:r + 1],
                                               in1=sig_o[:, t, c], op0=ALU.mult, op1=ALU.mult)
                if r in (3, 7):
                    ins.then_inc(xs_ready, 1)
            evac_xt(1, C_HNORM)

            def sum_and_norm(n, s, c0, first, second):
                lo(s)
                dve.wait_ge(half_used, s)
                add_x(first, 0)
                lo(s + 1)
                lo(s + 2)
                evac_xt(n, c0, (0, 1))
                lo(s + 3)
                dve.wait_ge(half_used, s + 2)
                add_x(second, 1)

            sum_and_norm(2, HALF_MOUT + 2, C_FNORM, (1, 2), (0, 3))

            lo(HALF_FFN + 2)
            mean(7)
            evac_xt(2, C_FNORM, (2, 3))
            inverse(3).then_inc(recip_ready, 1)
            dve.wait_ge(brow_stored, 16)
            lo(HALF_FFN + 3)
            dve.wait_ge(recip_ready, 1)
            swiglu(HALF_FFN, 0, NT, 0, scale=lambda t: small[:, S_RSTD + t:S_RSTD + t + 1])
            dve.wait_ge(down_half, 1)
            add_x((0, 2), 0)
            lo(HALF_DQ)
            evac_xt(3, C_DNORM, (0, 1))
            lo(HALF_DQ + 1)
            dve.wait_ge(half_used, HALF_DQ)
            add_x((1, 3), 1)

            evac_xt(3, C_DNORM, (2, 3))
            mean(11)
            inverse(4).then_inc(recip_ready, 1)
            dve.wait_ge(recip_ready, 2)
            for t in range(NT):
                ins = dve.tensor_scalar(diag[:, t, :], ident[:, :], small[:, S_RSTD + t:S_RSTD + t + 1], None, ALU.mult)
            ins.then_inc(diag_ready, 1)
            dve.wait_ge(lam_landed, 64)
            own(dve.tensor_tensor(lamp[:, :, :], lamv[:, 0:4:2, :], lamv[:, 1:4:2, :], ALU.mult))
            dve.tensor_reduce(lam[:, 0:2], lamp[:, :, :], AX_X, ALU.add).then_inc(lam_dot, 1)
            own(dve.tensor_scalar(sub_w[:, :], col[:, C_SUB:C_SUB + 1], 1.0 - LAM_INIT, None, ALU.mult))
            dve.wait_ge(qz_zeroed, 1)
            for n, banks in enumerate((BANKS_A, BANKS_B)):
                lo(HALF_DQ + 2 * n + 2)
                if n == 0:
                    dve.wait_ge(rrow_done, 1)
                    dve.tensor_copy(rrow[:, :], ps[:, 1, 0:T]).then_inc(rrow_ready, 1)
                    dve.wait_ge(rrow_ready, 1)
                lo(HALF_DQ + 2 * n + 3)
                dve.wait_ge(half_used, HALF_DQ + 2 * n + 2)
                for c, b in enumerate(banks):
                    for m in range(2):
                        r = slice(m * DHD, (m + 1) * DHD)
                        ins = dve.scalar_tensor_tensor(out=qz[r, 4 * n + c, m, :], in0=ps[r, b, 0:T], scalar=-DSCALE,
                                                       in1=rrow[r, :], op0=ALU.mult, op1=ALU.mult)
                ins.then_inc(dq_ready, 1)

            for n, banks in enumerate((BANKS_A, BANKS_B)):
                lo(HALF_DK + 2 * n + 2)
                lo(HALF_DK + 2 * n + 3)
                dve.wait_ge(half_used, HALF_DK + 2 * n + 2)
                for c, b in enumerate(banks):
                    ins = dve.tensor_tensor(kt[:, 4 * n + c, :], ps[:, b, 0:T], rrow[:, :], ALU.mult)
                ins.then_inc(dk_ready, 1)
            for i in range(HALF_DVV + 2, HALF_DOUT + 2):
                lo(i)
            dve.wait_ge(lam_exp, 1)
            own(dve.tensor_tensor(lam[:, 4:5], lam[:, 3:4], lam[:, 2:3], ALU.subtract))
            own(dve.tensor_scalar(lam[:, 5:6], lam[:, 4:5], -LAM_INIT, None, ALU.add))

            def row_max(i):
                klen = (i % 2 + 1) * P
                dve.wait_ge(logit_done, i + 1)
                if i >= 3:
                    dve.wait_ge(exp_ready, i - 2)
                lg2 = ps[:, 4 + i % 3, :].rearrange("p (m k) -> p m k", m=2)[:, :, 0:klen]
                dve.tensor_reduce(nmx[:, i % 3, :], lg2, AX_X, ALU.min).then_inc(max_ready, 1)

            def mix(i):
                klen = (i % 2 + 1) * P
                j = i % 2
                dve.wait_ge(exp_ready, i + 1)
                own(dve.reciprocal(sm[:, j, 2:4], sm[:, j, 0:2]))
                own(dve.tensor_tensor(sm[:, j, 4:5], sm[:, j, 3:4], lam[:, 5:6], ALU.mult))
                if i >= 2:
                    dve.wait_ge(at_done, i - 1)
                own(dve.tensor_scalar(aw[:, j, 0:klen], ex[:, j, 0, 0:klen], sm[:, j, 2:3], None, ALU.mult))
                dve.scalar_tensor_tensor(out=aw[:, j, 0:klen], in0=ex[:, j, 1, 0:klen], scalar=sm[:, j, 4:5],
                                         in1=aw[:, j, 0:klen], op0=ALU.mult, op1=ALU.add).then_inc(a_ready, 1)

            row_max(0)
            row_max(1)
            def sum_outputs(banks, done):
                for i, b in enumerate(banks):
                    dve.wait_ge(osq_ready, done + i + 1)
                    ins = dve.tensor_reduce(oms[:, 0, 4 * b:4 * b + 4], osq[b].rearrange("p (h v) -> p h v", h=4),
                                            AX_X, ALU.add)
                return ins

            for i in range(2 * DH):
                mix(i)
                if i + 2 < 2 * DH:
                    row_max(i + 2)
                if i == DH + 4:
                    sum_outputs((0, 2), 0)
            ins = sum_outputs((1, 3), 2)
            own(ins)
            dve.tensor_scalar(oms[:, 1, :], oms[:, 0, :], 1.0 / DDV, SUB_EPS, ALU.mult, ALU.add).then_inc(oms_ready, 1)
            dve.wait_ge(oroot_ready, 1)
            own(dve.reciprocal(oms[:, 3, :], oms[:, 2, :]))
            for b in (0, 2, 1, 3):
                r = oms[:, 3, 4 * b:4 * b + 4].unsqueeze(2).to_broadcast([P, 4, DDV])
                ins = dve.tensor_tensor(
                    xs[:, b // 2, (b % 2) * NW:(b % 2 + 1) * NW].rearrange("p (h v) -> p h v", h=4),
                    ps[:, b, :].rearrange("p (h v) -> p h v", h=4), r, ALU.mult)
                if b >= 2:
                    ins.then_inc(xs_ready, 1)
            evac_xt(4, None, scale=sub_w[:, 0:1])
            sum_and_norm(5, HALF_DOUT + 2, C_ENORM, (0, 2), (1, 3))

            evac_xt(5, C_ENORM, (2, 3))
            mean(15)
            inverse(5).then_inc(recip_ready, 1)
            dve.wait_ge(recip_ready, 3)
            def split_rows(t):
                dve.wait_ge(xn_h, t + 1)
                dve.scalar_tensor_tensor(out=xn_lo[:, t, :], in0=xs[:, t, :], scalar=small[:, S_RSTD + t:S_RSTD + t + 1],
                                         in1=xn_hi[:, t, :].bitcast(F32), op0=ALU.mult, op1=ALU.subtract)\
                   .then_inc(xn_ready, 1)

            dve.wait_ge(router_done, 1)
            dve.tensor_copy(lrow[:, :], ps[0:NE, 0, 0:T]).then_inc(lrow_ready, 1)
            dve.wait_ge(lcol_done, 1)
            for t in range(NT):
                ins = dve.scalar_tensor_tensor(out=lg[:, t, :], in0=ps[:, 5, t * NE:(t + 1) * NE],
                                               scalar=small[:, S_RSTD + t:S_RSTD + t + 1], in1=b_route[:, :],
                                               op0=ALU.mult, op1=ALU.add)
            own(ins)
            for t in range(NT):
                ins = dve.max(top[:, t, :], lg[:, t, :])
            own(ins)
            for t in range(NT):
                ins = dve.max_index(topi[:, t, :], top[:, t, :], lg[:, t, :])
            own(ins)
            dve.tensor_tensor(gsc[:, :, 0:1], top[:, :, 1:2], top[:, :, 0:1], ALU.subtract).then_inc(gap_ready, 1)
            own(dve.tensor_copy(topf[:, :, :], topi[:, :, :]))
            dve.wait_ge(const_step, 16)
            for t in range(NT):
                for i in range(2):
                    ins = dve.tensor_scalar(m12[:, t, i, :], slots[:, 0:NE], topf[:, t, i:i + 1], None, ALU.is_equal)
            own(ins)
            for t in range(NT):
                ins = dve.tensor_tensor(rt[:, 0, t, :], m12[:, t, 0, :], m12[:, t, 1, :], ALU.add)
            ins.then_inc(chosen_ready, 1)
            def make_pick(c):
                for t in range(NT):
                    ins = dve.tensor_scalar(pick[:, t, :], slots[:, :], c[:, t:t + 1], c[:, 2 + t:3 + t],
                                            ALU.is_equal, ALU.mult)
                ins.then_inc(pick_ready, 1)

            def choose(n):
                dve.wait_ge(pick_t_done, n)
                dve.tensor_copy(cur[:, :], plan[:, bass.ds(n, 1), :].rearrange("p a c -> p (a c)")).then_inc(cur_ready, 1)
                dve.wait_ge(cur_ready, n + 1)
                make_pick(cur)

            split_rows(0)
            split_rows(1)
            dve.wait_ge(pos_done, 1)
            dve.tensor_copy(pos[:, :, :], ps[:, 6, 0:16].rearrange("p (t e) -> p t e", t=NT)).then_inc(dve_self, 1)
            self_n[0] += 1
            for t in range(NT):
                dve.tensor_copy(plan[:, 0:NE, t], ps[:, 6, t * NE:(t + 1) * NE])
                ins = dve.tensor_copy(plan[:, 0:NE, 2 + t], rt[:, 0, t, :])
            own(ins)
            make_pick(plan[:, 0, :])
            lo(HALF_MOE + 2)
            dve.wait_ge(gexp_ready, 1)
            own(dve.tensor_scalar(gsc[:, :, 2:3], gsc[:, :, 1:2], 1.0, None, ALU.add))
            own(dve.reciprocal(gsc[:, :, 3:4], gsc[:, :, 2:3]))
            own(dve.tensor_tensor(gsc[:, :, 4:5], gsc[:, :, 3:4], gsc[:, :, 1:2], ALU.mult))
            for t in range(NT):
                ins = dve.tensor_scalar(rt[:, 1, t, :], m12[:, t, 0, :], gsc[:, t, 3:4], None, ALU.mult)
            own(ins)
            for t in range(NT):
                ins = dve.scalar_tensor_tensor(out=rt[:, 1, t, :], in0=m12[:, t, 1, :], scalar=gsc[:, t, 4:5],
                                               in1=rt[:, 1, t, :], op0=ALU.mult, op1=ALU.add)
            own(ins)
            for t in range(NT):
                ins = dve.tensor_copy(plan[:, 0:NE, 4 + t], rt[:, 1, t, :])
            own(ins)
            dve.tensor_copy(cur[:, :], plan[:, 0, :]).then_inc(cur_ready, 1)
            dve.wait_ge(cur_ready, 1)
            dve.nop().then_inc(x_combined, 1)

            def gathered_rows(n):
                dve.wait_ge(gather_done, n * 2 + 2)
                dve.tensor_copy(xg[:, NW:2 * NW], ps[:, 3, :]).then_inc(xg_ready[1], 1)

            def gathered(n):
                for b in range(2):
                    dve.wait_ge(xe_hi, n * 2 + b + 1)
                    dve.tensor_tensor(xt_lo[:, 4 * b:4 * b + 4, 0:P], ps[:, 2 + b, :].rearrange("p (c t) -> p c t", c=4),
                                      xt_hi[:, 4 * b:4 * b + 4, 0:P].bitcast(F32), ALU.subtract).then_inc(xe_ready, 1)

            def expert(n, follows, j=None):
                s, q = pass_base(n, j)
                nxt = s + 6 * GROUPS
                swiglu(s, q, 1, NT * GROUPS + n * GROUPS, (lambda: choose(n + 1)) if follows else None)
                if follows:
                    gathered_rows(n + 1)
                    lo(nxt, q)
                    gathered(n + 1)
                    lo(nxt + 1, q)
                for nh in range(2):
                    c = slice(nh * NW, (nh + 1) * NW)
                    dve.wait_ge(y_h, n * 2 + nh + 1)
                    dve.scalar_tensor_tensor(out=y_lo[:, c], in0=ps[:, nh, :], scalar=gslot[:, 0:1],
                                             in1=y_hi[:, c].bitcast(F32), op0=ALU.mult, op1=ALU.subtract)\
                       .then_inc(y_ready, 1)
                if follows:
                    lo(nxt + 2, q)
                    lo(nxt + 3, q)
                for i, (nh, t) in enumerate([(nh, t) for nh in range(2) for t in range(NT)]):
                    xv = x[:, t, nh * NW:(nh + 1) * NW]
                    dve.wait_ge(combine_done, n * 4 + i + 1)
                    dve.tensor_tensor(xv, ps[:, combine_bank[nh][t], :], xv, ALU.add).then_inc(x_combined, 1)

            gathered_rows(0)
            gathered(0)
            lo(HALF_MOE + 3)
            dve.wait_ge(pos_done, 2)
            own(dve.tensor_scalar(ovf[:, 0, :], ps[:, 5, 16:24], float(P), None, ALU.is_gt))
            with dve.Fori(0, NE - 1) as n:
                expert(n, True)
            own(dve.tensor_tensor_scan(ovf[:, 1, :], ovf[:, 0, :], zero8[:, :], 0.0, ALU.add, ALU.add))
            for j in range(OVERFLOW_PASSES):
                ins = dve.scalar_tensor_tensor(out=sel[:, j, :], in0=ovf[:, 1, :], scalar=float(j + 1),
                                               in1=ovf[:, 0, :], op0=ALU.is_equal, op1=ALU.mult)
            own(ins)
            for j in range(OVERFLOW_PASSES):
                dve.tensor_tensor(ovj[:, j, :, :], plan[:, 0:NE, :].rearrange("p e c -> p c e"),
                                  sel[:, j, :].unsqueeze(1).to_broadcast([P, 6, NE]), ALU.mult)
            own(dve.tensor_tensor(ovi[:, :, :], sel[:, :, :],
                                  slots[:, 0:NE].unsqueeze(1).to_broadcast([P, OVERFLOW_PASSES, NE]), ALU.mult))
            for j in range(OVERFLOW_PASSES):
                dve.tensor_reduce(plan[:, NE + j, :], ovj[:, j, :, :], AX_X, ALU.add)
            dve.tensor_reduce(ovs[:, 1:1 + OVERFLOW_PASSES], ovi[:, :, :], AX_X, ALU.add)
            own(dve.tensor_copy(ovs[:, 0:1], ovf[:, 1, NE - 1:NE]))
            dve.tensor_scalar(plan[:, NE:PASSES, 0:2], plan[:, NE:PASSES, 0:2], -float(P), None, ALU.add)
            dve.tensor_copy(route[0:1, :], ovs[0:1, 0:4]).then_inc(route_ready, 1)
            expert(NE - 1, False)
            dve.wait_ge(route_ready, 1)
            over = dve.value_load(route[0:1, 0:1], min_val=0, max_val=OVERFLOW_PASSES)
            with dve.Fori(0, OVERFLOW_PASSES) as j:
                with dve.If(over > j):
                    lo(HALF_OVER, j * GROUPS)
                    lo(HALF_OVER + 1, j * GROUPS)
                    choose(j + NE)
                    gathered_rows(j + NE)
                    gathered(j + NE)
                    lo(HALF_OVER + 2, j * GROUPS)
                    lo(HALF_OVER + 3, j * GROUPS)
                    expert(j + NE, False, j)
                dve.nop()
            mean(19)
            inverse(6).then_inc(recip_ready, 1)
            dve.wait_ge(recip_ready, 4)
            dve.wait_ge(fin_landed, 16)
            for t in range(NT):
                dve.scalar_tensor_tensor(out=xs[:, t, :], in0=x[:, t, :], scalar=small[:, S_RSTD + t:S_RSTD + t + 1],
                                         in1=fin_w, op0=ALU.mult, op1=ALU.mult).then_inc(fin_ready, 1)


_INS = ["x", "rel_bias_table", "mlstm_norm", "mlstm_w_in", "mlstm_conv_w", "mlstm_conv_b", "mlstm_b_igate",
        "mlstm_b_fgate", "mlstm_head_norm", "mlstm_w_out", "diff_norm", "diff_w_in", "diff_lambda_q1",
        "diff_lambda_k1", "diff_lambda_q2", "diff_lambda_k2", "diff_subln", "diff_w_out", "ffn_norm",
        "ffn_w_gate", "ffn_w_up", "ffn_w_down", "moe_norm", "moe_w_router", "moe_b_router", "moe_w_gate",
        "moe_w_up", "moe_w_down", "final_norm"]


def kernel(**inputs):
    import numpy as _np
    import concourse.bacc as _bacc
    from concourse import mybir as _mybir
    from concourse.bass_utils import run_bass_kernel_spmd as _run

    nc = _bacc.Bacc("TRN2", target_bir_lowering=False, num_devices=1)
    arrays, aps = {}, {}
    for name in _INS:
        a = _np.ascontiguousarray(inputs[name])
        arrays[f"in_{name}"] = a
        aps[name] = nc.dram_tensor(f"in_{name}", a.shape, _mybir.dt.from_np(a.dtype), kind="ExternalInput").ap()
    hot = _np.array(bucket_hot(), _np.float32)
    arrays["in_bucket_hot"] = hot
    aps["bucket_hot"] = nc.dram_tensor("in_bucket_hot", hot.shape, _mybir.dt.float32, kind="ExternalInput").ap()
    out = nc.dram_tensor("out_0", (1, 256, 1024), _mybir.dt.float32, kind="ExternalOutput").ap()
    bass_hybrid(nc, aps, out)
    r = _run(nc, [arrays], core_ids=[0])
    return r.results[0]["out_0"]
```
